# Optimizing a Trainium2 kernel written in Bass

```python
import math
import jax, jax.numpy as jnp
from jax import lax
import numpy as np

D_MODEL = 1024
BATCH = 1
SEQ = 256
DEPTH = 1

DA_HEADS = 4
DA_HD = 64
DA_WIDTH = DA_HEADS * 2 * DA_HD
ML_HEADS = 4
ML_HD = 128
ML_WIDTH = ML_HEADS * ML_HD
CONV_W = 4
CHUNK = 64
Q_BLOCK = 128
N_GROUPS = 4
EXPERTS_PER_GROUP = 8
TOP_K = 2
D_EXPERT = 256
EPS = 1e-6
IN_SIZES = (DA_WIDTH, DA_WIDTH, DA_WIDTH,
            2 * ML_WIDTH, ML_WIDTH, ML_WIDTH,
            2 * ML_HEADS,
            D_MODEL, D_MODEL)
N_IN = sum(IN_SIZES)

kernel_name = 'hybrid_diffattn_mlstm_hmoe_adaln'

def rmsnorm(x, g):
    x32 = x.astype(jnp.float32)
    y = x32 * lax.rsqrt(jnp.mean(x32 * x32, axis=-1, keepdims=True) + EPS)
    return y.astype(x.dtype) * g

def alibi_slopes(n):
    return jnp.asarray(2.0 ** (-8.0 * np.arange(1, n + 1) / n), dtype=jnp.float32)

def causal_conv(x, w, b):
    K = w.shape[0]
    S = x.shape[1]
    xp = jnp.pad(x, ((0, 0), (K - 1, 0), (0, 0)))
    return sum(xp[:, j:j + S] * w[j] for j in range(K)) + b

def diff_attention(q, k, v, lam, lambda_init, head_gain):
    B, S = q.shape[:2]
    nb = S // Q_BLOCK
    slopes = alibi_slopes(DA_HEADS)
    scale = DA_HD ** -0.5
    qb = q.reshape(B, nb, Q_BLOCK, DA_HEADS, 2, DA_HD).swapaxes(0, 1)
    kpos = jnp.arange(S)

    def block(args):
        qi, bi = args
        s = jnp.einsum('bqhcd,bkhcd->bhcqk', qi, k).astype(jnp.float32) * scale
        qpos = bi * Q_BLOCK + jnp.arange(Q_BLOCK)
        dist = (qpos[:, None] - kpos[None, :]).astype(jnp.float32)
        s = s - (slopes[:, None, None] * dist)[None, :, None]
        s = jnp.where(dist >= 0, s, -jnp.inf)
        p = jax.nn.softmax(s, axis=-1)
        a = p[:, :, 0] - lam * p[:, :, 1]
        return jnp.einsum('bhqk,bkhe->bqhe', a.astype(v.dtype), v)

    o = lax.map(block, (qb, jnp.arange(nb)))
    o = o.swapaxes(0, 1).reshape(B, S, DA_HEADS, 2 * DA_HD)
    o = rmsnorm(o, head_gain) * (1.0 - lambda_init)
    return o.reshape(B, S, DA_WIDTH)

def mlstm(q, k, v, i_pre, f_pre):
    B, S, H, dh = q.shape
    nc = S // CHUNK
    f32 = jnp.float32
    k = k * dh ** -0.5
    logi = i_pre.astype(f32)
    logf = jax.nn.log_sigmoid(f_pre.astype(f32))

    def to_chunks(t):
        return t.reshape(B, nc, CHUNK, *t.shape[2:]).swapaxes(0, 1)

    xs = (to_chunks(q), to_chunks(k), to_chunks(v), to_chunks(logi), to_chunks(logf))
    causal = jnp.tril(jnp.ones((CHUNK, CHUNK), dtype=bool))

    def step(carry, inp):
        C, n, m = carry
        qc, kc, vc, li, lf = inp
        qc = qc.astype(f32); kc = kc.astype(f32); vc = vc.astype(f32)
        bh = jnp.cumsum(lf, axis=1).swapaxes(1, 2)
        ih = li.swapaxes(1, 2)
        g = bh[..., -1]
        Dm = bh[..., :, None] - bh[..., None, :] + ih[..., None, :]
        Dm = jnp.where(causal, Dm, -jnp.inf)
        inter = bh + m[..., None]
        mj = jnp.maximum(inter, Dm.max(-1))
        w_intra = jnp.exp(Dm - mj[..., None])
        w_inter = jnp.exp(inter - mj)
        qk = jnp.einsum('bjhd,bshd->bhjs', qc, kc) * w_intra
        num = (jnp.einsum('bhjs,bshe->bjhe', qk, vc)
               + jnp.einsum('bhed,bjhd->bjhe', C, qc) * w_inter.swapaxes(1, 2)[..., None])
        den = qk.sum(-1) + w_inter * jnp.einsum('bhd,bjhd->bhj', n, qc)
        denom = jnp.maximum(jnp.abs(den), jnp.exp(-mj)).swapaxes(1, 2)
        h = num / denom[..., None]
        a = g[..., None] - bh + ih
        m_new = jnp.maximum(g + m, a.max(-1))
        wa = jnp.exp(a - m_new[..., None])
        decay = jnp.exp(g + m - m_new)
        C_new = decay[..., None, None] * C + jnp.einsum('bhs,bshe,bshd->bhed', wa, vc, kc)
        n_new = decay[..., None] * n + jnp.einsum('bhs,bshd->bhd', wa, kc)
        return (C_new, n_new, m_new), h

    init = (jnp.zeros((B, H, dh, dh), f32), jnp.zeros((B, H, dh), f32), jnp.zeros((B, H), f32))
    _, hs = lax.scan(step, init, xs)
    return hs.swapaxes(0, 1).reshape(B, S, H, dh).astype(q.dtype)

def hier_moe(h, w_rg, b_rg, w_re, b_re, w_e1, w_e3, w_e2):
    B, S, D = h.shape
    f32 = jnp.float32
    t = h.reshape(-1, D)
    T = t.shape[0]
    g_logits = (t @ w_rg + b_rg).astype(f32)
    g_prob = jax.nn.softmax(g_logits, axis=-1)
    g_sel = jnp.argmax(g_logits, axis=-1)
    p_grp = jnp.take_along_axis(g_prob, g_sel[:, None], axis=1)[:, 0]
    e_logits = (t @ w_re + b_re).astype(f32).reshape(T, N_GROUPS, EXPERTS_PER_GROUP)
    e_sel = jnp.take_along_axis(e_logits, g_sel[:, None, None], axis=1)[:, 0]
    e_prob = jax.nn.softmax(e_sel, axis=-1)
    topv, topi = lax.top_k(e_prob, TOP_K)
    topv = topv / topv.sum(-1, keepdims=True)
    w_e = jnp.einsum('tke,tk->te', jax.nn.one_hot(topi, EXPERTS_PER_GROUP, dtype=f32), topv)
    gate = (jax.nn.one_hot(g_sel, N_GROUPS, dtype=f32)[:, :, None]
            * w_e[:, None, :] * p_grp[:, None, None]).astype(t.dtype)
    y = jnp.zeros_like(t)
    for gi in range(N_GROUPS):
        a = jnp.einsum('td,edf->tef', t, w_e1[gi])
        b = jnp.einsum('td,edf->tef', t, w_e3[gi])
        hid = jax.nn.silu(a) * b * gate[:, gi, :, None]
        y = y + jnp.einsum('tef,efd->td', hid, w_e2[gi])
    return y.reshape(B, S, D)

def setup_inputs(seed: int = 0) -> dict:
    key = jax.random.key(seed)
    ks = jax.random.split(key, 32)
    L, D, G, E, F = DEPTH, D_MODEL, N_GROUPS, EXPERTS_PER_GROUP, D_EXPERT
    nrm = lambda k, shape, s: jax.random.normal(k, shape, jnp.float32) * s
    f_bias = jnp.broadcast_to(jnp.linspace(3.0, 6.0, ML_HEADS, dtype=jnp.float32), (L, ML_HEADS))
    b_if = jnp.concatenate([nrm(ks[5], (L, ML_HEADS), 0.1),
                            f_bias + nrm(ks[6], (L, ML_HEADS), 0.1)], axis=-1)
    return {
        'x': nrm(ks[0], (BATCH, SEQ, D), 1.0),
        'c': nrm(ks[1], (BATCH, D), 1.0),
        'w_ada': nrm(ks[2], (L, D, 6 * D), 0.5 * D ** -0.5),
        'b_ada': nrm(ks[3], (L, 6 * D), 0.01),
        'norm1': 1.0 + nrm(ks[4], (L, D), 0.02),
        'w_in': nrm(ks[7], (L, D, N_IN), D ** -0.5),
        'b_if': b_if,
        'conv_w': nrm(ks[8], (L, CONV_W, 2 * ML_WIDTH), CONV_W ** -0.5),
        'conv_b': nrm(ks[9], (L, 2 * ML_WIDTH), 0.01),
        'lam_q1': nrm(ks[10], (L, DA_HD), 0.1),
        'lam_k1': nrm(ks[11], (L, DA_HD), 0.1),
        'lam_q2': nrm(ks[12], (L, DA_HD), 0.1),
        'lam_k2': nrm(ks[13], (L, DA_HD), 0.1),
        'diff_norm': 1.0 + nrm(ks[14], (L, 2 * DA_HD), 0.02),
        'mlstm_norm': 1.0 + nrm(ks[15], (L, ML_HD), 0.02),
        'w_br_a': nrm(ks[16], (L, DA_WIDTH, D), DA_WIDTH ** -0.5),
        'w_br_m': nrm(ks[17], (L, ML_WIDTH, D), ML_WIDTH ** -0.5),
        'w_out': nrm(ks[18], (L, D, D), D ** -0.5),
        'norm2': 1.0 + nrm(ks[19], (L, D), 0.02),
        'w_rg': nrm(ks[20], (L, D, G), D ** -0.5),
        'b_rg': nrm(ks[21], (L, G), 0.01),
        'w_re': nrm(ks[22], (L, D, G * E), D ** -0.5),
        'b_re': nrm(ks[23], (L, G * E), 0.01),
        'w_e1': nrm(ks[24], (L, G, E, D, F), D ** -0.5),
        'w_e3': nrm(ks[25], (L, G, E, D, F), D ** -0.5),
        'w_e2': nrm(ks[26], (L, G, E, F, D), F ** -0.5),
        'norm_f': 1.0 + nrm(ks[27], (D,), 0.02),
    }

def reference(x, c, w_ada, b_ada, norm1, w_in, b_if, conv_w, conv_b, lam_q1, lam_k1, lam_q2, lam_k2,
              diff_norm, mlstm_norm, w_br_a, w_br_m, w_out, norm2, w_rg, b_rg, w_re, b_re,
              w_e1, w_e3, w_e2, norm_f):
    B, S, D = x.shape
    cs = jax.nn.silu(c)
    split_idx = list(np.cumsum(IN_SIZES)[:-1])
    for l in range(DEPTH):
        mod = (cs @ w_ada[l] + b_ada[l])[:, None, :]
        sh1, sc1, gt1, sh2, sc2, gt2 = jnp.split(mod, 6, axis=-1)
        h = rmsnorm(x, norm1[l]) * (1.0 + sc1) + sh1
        proj = h @ w_in[l]
        da_q, da_k, da_v, ml_qk, ml_v, ml_o, ml_if, g_a, g_m = jnp.split(proj, split_idx, axis=-1)
        lambda_init = 0.8 - 0.6 * math.exp(-0.3 * l)
        lam = (jnp.exp(jnp.sum(lam_q1[l] * lam_k1[l])) - jnp.exp(jnp.sum(lam_q2[l] * lam_k2[l]))
               + lambda_init)
        y_a = diff_attention(da_q.reshape(B, S, DA_HEADS, 2, DA_HD),
                             da_k.reshape(B, S, DA_HEADS, 2, DA_HD),
                             da_v.reshape(B, S, DA_HEADS, 2 * DA_HD),
                             lam, lambda_init, diff_norm[l])
        qk = jax.nn.silu(causal_conv(ml_qk, conv_w[l], conv_b[l]))
        m_q, m_k = jnp.split(qk, 2, axis=-1)
        gates = ml_if + b_if[l]
        h_t = mlstm(m_q.reshape(B, S, ML_HEADS, ML_HD), m_k.reshape(B, S, ML_HEADS, ML_HD),
                    ml_v.reshape(B, S, ML_HEADS, ML_HD), gates[..., :ML_HEADS], gates[..., ML_HEADS:])
        o_gate = jax.nn.sigmoid(ml_o).reshape(B, S, ML_HEADS, ML_HD)
        y_m = rmsnorm(o_gate * h_t, mlstm_norm[l]).reshape(B, S, ML_WIDTH)
        merged = jax.nn.sigmoid(g_a) * (y_a @ w_br_a[l]) + jax.nn.sigmoid(g_m) * (y_m @ w_br_m[l])
        x = x + gt1 * (merged @ w_out[l])
        h2 = rmsnorm(x, norm2[l]) * (1.0 + sc2) + sh2
        x = x + gt2 * hier_moe(h2, w_rg[l], b_rg[l], w_re[l], b_re[l], w_e1[l], w_e3[l], w_e2[l])
    return rmsnorm(x, norm_f)


_drawn_inputs = setup_inputs


def setup_inputs(seed=0):
    import zlib

    import numpy as np

    out = dict(_drawn_inputs(seed))
    spreads = {}
    factors = {'b_ada': 4.398,
     'norm1': 6.064,
     'conv_b': 64.0,
     'lam_q1': 8.0,
     'lam_q2': 4.417,
     'diff_norm': 8.0,
     'mlstm_norm': 8.0,
     'norm2': 4.487,
     'b_rg': 8.0,
     'b_re': 8.0,
     'norm_f': 9.676}
    for name, (base, spread) in spreads.items():
        noise = np.random.default_rng([zlib.crc32(name.encode()), seed]).standard_normal(out[name].shape)
        drawn = base * np.exp(spread * noise) if base else spread * noise
        out[name] = __import__('jax').numpy.asarray(drawn.astype(out[name].dtype))
    for name, factor in factors.items():
        out[name] = (out[name] * factor).astype(out[name].dtype)
    return out
```

```python
from contextlib import ExitStack

import numpy as np
import concourse.bass as bass
from concourse import mybir

F32 = mybir.dt.float32
I32 = mybir.dt.int32
U32 = mybir.dt.uint32
ALU = mybir.AluOpType
ACT = mybir.ActivationFunctionType
AX = mybir.AxisListType

P = 128
D, T = 1024, 256
KD, TT = D // P, T // P
HEADS, DA_HD = 4, 64
EPS = 1e-6
G, E, F = 4, 8, 256
NE = G * E
QUAD = 4
NQ = NE // QUAD
CAP = P // QUAD
PASSES = T // CAP
LAMBDA_INIT = 0.8 - 0.6 * float(np.exp(-0.3 * 0))
NEG = -1.0e30
RING = 12
UNIT = 2048

ROWS, NROWS = {}, 0
for _name, _n in (("c", 8), ("norm1", 8), ("norm2", 8), ("b_ada", 48), ("conv_w", 32),
                  ("conv_b", 8), ("diff_norm", 1), ("mlstm_norm", 1)):
    ROWS[_name] = (NROWS, NROWS + _n)
    NROWS += _n

C_Q, C_K, C_V, C_MQK, C_MV, C_MO, C_IF, C_GA, C_GM = 0, 512, 1024, 1536, 2560, 3072, 3584, 3592, 4616


def unit_list():
    units = [("ada", 256 * i) for i in range(8)]
    for c0, n in ((C_Q, 2), (C_K, 2), (C_V, 2), (C_MQK, 4), (C_MV, 2), (C_MO, 2), (C_GA, 4), (C_GM, 4)):
        units += [("in", c0 + 256 * i) for i in range(n)]
    units += [("ada", 2048 + 256 * i) for i in range(8)]
    units += [("br_a", 0), ("br_a", 512), ("br_m", 0), ("br_m", 512)]
    units += [("ada", 4096 + 256 * i) for i in range(4)]
    units += [("out", 256 * i) for i in range(4)]
    units += [("ada", 5120 + 256 * i) for i in range(4)]
    return units


def unit_jobs():
    jobs = ["ada0"] * 4 + ["ada1"] * 4
    jobs += [f"qk{i}" for i in range(4)] + ["v0", "v1"] + [f"ml{i}" for i in range(4)]
    jobs += ["mv0", "mv1", "mo0", "mo1"] + [f"ga{i}" for i in range(4)] + [f"gm{i}" for i in range(4)]
    jobs += ["ada2"] * 4 + ["ada3"] * 4 + ["bra1", "bra3", "brm1", "brm3"]
    return jobs + ["ada4"] * 4 + [f"wo{i}" for i in range(4)] + ["ada5"] * 4


UNITS = unit_list()
NPRE = len(UNITS)
QUAD_UNITS = [(w, e) for w in ("w1", "w3", "w2") for e in range(QUAD)]
UP_UNITS = 8
QU = len(QUAD_UNITS)
QUAD_POS = {u: i for i, u in enumerate(QUAD_UNITS)}

JOBS = (["cT", "ada0", "ada1", "vT"] + [f"xT{i}" for i in range(4)] + ["adaT0", "adaT1", "if"]
        + ["qk0", "ifT", "qk1", "qk2", "qk3"]
        + ["v0", "v1"] + [f"s{i}" for i in range(8)] + [f"ml{i}" for i in range(4)]
        + ["cols", "Mb0", "Mb1", "mv0", "mv1", "o0", "o1", "aT0", "aT1", "mo0", "aT2", "aT3", "mo1"]
        + ["ga0", "ga1", "ms0", "ms1", "ga2", "num0", "ms2", "num1", "ms3", "ga3", "num2", "num3"]
        + ["yaT0", "yaT1"] + [f"gm{i}" for i in range(4)]
        + ["ymT0", "ymT1", "ada2", "ada3", "gt1b0", "gt1b1", "adaT3"]
        + [f"bra{i}" for i in range(4)] + [f"brm{i}" for i in range(4)]
        + ["ada4", "wo0", "adaT4", "wo1", "rb", "wo2", "x2T0", "wo3", "x2T1", "ada5", "x2T2", "x2T3", "lg",
           "gt2b0", "gt2b1", "rank"])
UNIT_JOB = unit_jobs()
JOB = {n: i for i, n in enumerate(JOBS)}

CONSTS, NCONST = {}, 0
for _name, _shape in (("ident", (P,)), ("ones", (P,)), ("tri", (P,)), ("alibi", (HEADS, 384)), ("mask", (384,)),
                      ("slot", (TT, QUAD, CAP)), ("iota8", (TT, 8))):
    CONSTS[_name] = (NCONST, _shape)
    NCONST += int(np.prod(_shape))


def constants():
    out = np.zeros((P, NCONST), np.float32)

    def put(name, value):
        c0, shape = CONSTS[name]
        out[:, c0:c0 + int(np.prod(shape))] = np.broadcast_to(value, (P,) + shape).reshape(P, -1)

    i = np.arange(P)
    put("ident", np.eye(P))
    put("ones", np.ones((P, P)))
    put("tri", (i[:, None] < i[None, :]) * 1.0)
    slopes = 2.0 ** (-8.0 * np.arange(1, HEADS + 1) / HEADS)
    dist = (P + i)[:, None] - np.arange(2 * P)[None, :]
    ali = np.where(dist >= 0, -slopes[:, None, None] * dist, NEG).transpose(1, 0, 2)
    put("alibi", np.concatenate([ali[:, :, P:], ali], axis=2))
    tri = np.where(i[None, :] >= i[:, None], 0.0, NEG)
    put("mask", np.concatenate([tri, np.zeros((P, P)), tri], axis=1))
    put("slot", np.arange(CAP)[None, None, None, :])
    put("iota8", np.arange(8)[None, None, :])
    return out


def build(nc, t, out):
    with ExitStack() as ctx:
        def sb(name, shape, dt=F32):
            return ctx.enter_context(nc.sbuf_tensor(name, [P] + list(shape), dt))

        def sem(name):
            return ctx.enter_context(nc.semaphore(name))

        ring = sb("ring", [RING, UNIT])
        const = sb("const", [NCONST])
        x = sb("x", [TT, D])
        xn = sb("xn", [TT, D])
        hT = sb("hT", [KD, T])
        qkT = sb("qkT", [8, T])
        v = sb("v", [TT, 512])
        raw = sb("raw", [8, T + 3])
        gm = sb("gm", [KD, T])
        mqk = sb("mqk", [8, T])
        vaug = sb("vaug", [TT, HEADS, P + 1])
        osig = sb("osig", [TT, 512])
        att = sb("att", [3072])
        WT = sb("WT", [2, 384])
        o = sb("o", [TT, 512])
        tmp = sb("tmp", [2, 512])
        vrows = sb("vrows", [P])
        cols = sb("cols", [NROWS])
        w_if = sb("w_if", [KD, 8])
        b_if = sb("b_if", [8])
        b_r = sb("b_r", [G + NE])
        w_r = sb("w_r", [KD, G + NE])
        sm = sb("sm", [320])
        router = sb("router", [800])
        flag = sb("flag", [1], I32)
        idx = sb("idx", [2, TT, 8], U32)

        ga = gm
        gm2 = mqk
        sc = att[:, 0:1536].rearrange("p (b c n) -> p b c n", b=2, c=2)
        a_sb = xn[:].rearrange("p a n -> p (a n)")[:, 0:1536].rearrange("p (h n) -> p h n", h=HEADS)
        wts = [WT[:, 0], WT[:, 1], att[:, 1536:1920], att[:, 1920:2304]]
        aT = att[:, 2304:3072].rearrange("p (b n) -> p b n", b=2)
        gt1b = att[:, 0:1024]
        gt2b = att[:, 1024:2048]
        nfb = att[:, 2048:3072]
        yT = qkT
        sig, act_a, hid = tmp[:, 0, 0:F], tmp[:, 0, F:2 * F], tmp[:, 1, 0:F]
        hidT = WT[:].rearrange("p b n -> p (b n)")[:, 0:2 * P].rearrange("p (f n) -> p f n", f=2)
        arow = sb("arow", [2, 256])
        rbias = sb("rbias", [G + NE])
        lamv = tmp[:, 0, 0:4 * DA_HD].rearrange("p (a n) -> p a n", a=4)
        spare = const[:, CONSTS["alibi"][0]:CONSTS["alibi"][0] + 1024]
        pone = spare[:, 0:256].rearrange("p (t e n) -> p t e n", t=TT, e=QUAD)
        pgate = spare[:, 256:512].rearrange("p (t e n) -> p t e n", t=TT, e=QUAD)
        ptg = spare[:, 512:1024].rearrange("p (b t n) -> p b t n", b=2, t=TT)
        grow = o[:].rearrange("p a (b n) -> p (a b) n", b=2)
        xg = raw[:, :, 0:256].rearrange("p k (b n) -> p b k n", b=2)
        outs = v
        outs2 = outs[:].rearrange("p a n -> p (a n)")
        junk = hT[:].rearrange("p a n -> p (a n)")

        def K(name):
            c0, shape = CONSTS[name]
            ap = const[:, c0:c0 + int(np.prod(shape))]
            if len(shape) == 2:
                return ap.rearrange("p (a b) -> p a b", a=shape[0])
            if len(shape) == 3:
                return ap.rearrange("p (a b c) -> p a b c", a=shape[0], b=shape[1])
            return ap

        ident, ones = K("ident"), K("ones")

        def col(name, i=0, n=1):
            r0 = ROWS[name][0]
            return cols[:, r0 + i:r0 + i + n]

        small_at, small = [0], {}

        def S(name, n=1):
            if name not in small:
                small[name] = (small_at[0], n)
                small_at[0] += n
            a, n = small[name]
            return sm[:, a:a + n]

        r_at, r_names = [0], {}

        def R(name, *shape):
            if name not in r_names:
                r_names[name] = (r_at[0], shape)
                r_at[0] += int(np.prod(shape))
            a, shape = r_names[name]
            ap = router[:, a:a + int(np.prod(shape))]
            if len(shape) == 2:
                return ap.rearrange("p (a b) -> p a b", a=shape[0])
            if len(shape) == 3:
                return ap.rearrange("p (a b c) -> p a b c", a=shape[0], b=shape[1])
            return ap

        bank = [ctx.enter_context(nc.psum_tensor(f"bank{i}", [P, 512], F32)) for i in range(8)]
        bank_full = [sem(f"bank_full{i}") for i in range(8)]
        bank_free = [sem(f"bank_free{i}") for i in range(8)]

        def pb(job):
            return bank[JOB[job] % 8]

        def full(job):
            return bank_full[JOB[job] % 8], JOB[job] // 8 + 1

        def free(job):
            return bank_free[JOB[job] % 8], JOB[job] // 8 + 1

        def filled(ins, job):
            ins.then_inc(bank_full[JOB[job] % 8], 1)

        def release(ins, job):
            ins.then_inc(bank_free[JOB[job] % 8], 1)

        x_in, const_in, const2_in, c_in, vec_in, bc_in, nf_in, gt1_in, gt2_in, wr_in, out_done = (
            sem(n) for n in ("x_in", "const_in", "const2_in", "c_in", "vec_in", "bc_in", "nf_in", "gt1_in", "gt2_in", "wr_in", "out_done"))
        landed = [sem(f"landed{i}") for i in range(RING)]
        used = sem("used")
        dve_chain, act_chain = sem("dve_chain"), sem("act_chain")
        names = ["sq", "var", "std", "xn_r", "cols_r", "mod1", "gates", "gexp", "gln", "grows", "conv_out", "mqk_r",
                 "smax", "pexp", "a_r", "emn", "warg", "wexp", "pv", "h_sq", "var2", "std2", "hn_r", "var3", "std3",
                 "arow_r", "mod2", "wr_r", "merged", "lexp", "lam_e", "x2", "sq2", "var4", "std4", "x2n", "xT_r", "lg_r",
                 "rexp", "mask_r", "flag_r", "pads", "x3", "sq5", "var5", "std5", "y_out",
                 "g_full", "g_evac", "pg_ready", "pt_full", "pt_evac", "sig_r", "hid_done", "hT_evac",
                 "o_act", "o_dve", "scat", "act_end", "dve_end", "moe_chain", "y_full", "r_chain"]
        s = {n: sem(n) for n in names}

        w_ada = t["w_ada"][0].rearrange("(k p) n -> p k n", p=P)
        w_in = t["w_in"][0].rearrange("(k p) n -> p k n", p=P)
        w_bra = t["w_br_a"][0].rearrange("(k p) n -> p k n", p=P)
        w_brm = t["w_br_m"][0].rearrange("(k p) n -> p k n", p=P)
        w_out = t["w_out"][0].rearrange("(k p) n -> p k n", p=P)
        w_e = {"w1": t["w_e1"].rearrange("l g e (k p) f -> (l g e) p k f", p=P),
               "w3": t["w_e3"].rearrange("l g e (k p) f -> (l g e) p k f", p=P),
               "w2": t["w_e2"].rearrange("l g e (k p) n -> (l g e) p k n", p=P)}

        def unit(n, k):
            return ring[:, n % RING, :].rearrange("p (k n) -> p k n", k=k)

        block = ctx.enter_context(nc.Block())

        @block.sync
        def _(sp):
            sp.dma_start(vrows[ROWS["c"][0]:ROWS["c"][1], :], t["c"].rearrange("l (r n) -> (l r) n", n=P)
                         ).then_inc(c_in, 16)
            sp.dma_start(const[:, 0:2 * P], t["const"][:, 0:2 * P]).then_inc(const_in, 16)
            for tt in range(TT):
                sp.dma_start(x[:, tt, :], t["x"][0, tt * P:(tt + 1) * P, :]).then_inc(x_in, 16)
            src = {"ada": w_ada, "in": w_in, "br_a": w_bra, "br_m": w_brm, "out": w_out}
            for n, (kind, c0) in enumerate(UNITS):
                if n >= RING:
                    sp.wait_ge(*full(UNIT_JOB[n - RING]))
                k = 4 if kind in ("br_a", "br_m") else 8
                w = UNIT // k
                sp.dma_start(unit(n, k), src[kind][:, :, c0:c0 + w]).then_inc(landed[n % RING], 16)

            def load(q, u):
                w, e = QUAD_UNITS[u]
                n = NPRE + u
                k = 2 if w == "w2" else 8
                expert = w_e[w][q * QUAD + e] if isinstance(q, int) else \
                    w_e[w][bass.ds(q * QUAD + e, 1)].rearrange("a p k n -> p (a k) n")
                sp.dma_start(unit(n, k), expert).then_inc(landed[n % RING], 16)

            def load_quad(q, it):
                for u in range(QU):
                    sp.wait_ge(used, it * QU + (u - QU + 1))
                    load(q, u)

            for u in range(QU):
                sp.wait_ge(*full(UNIT_JOB[NPRE + u - RING]))
                load(0, u)
            with sp.Fori(1, NQ) as q:
                load_quad(q, q)
            sp.wait_ge(s["flag_r"], 1)
            over = sp.value_load(flag[0:1, 0:1], min_val=0, max_val=1)
            with sp.If(over > 0):
                with sp.Fori(1, PASSES) as p:
                    with sp.Fori(0, NQ) as q:
                        load_quad(q, p * NQ + q)
            for tt in range(TT):
                sp.wait_ge(s["y_out"], tt + 1)
                sp.dma_start(out[0, tt * P:(tt + 1) * P, :], x[:, tt, :]).then_inc(out_done, 16)
            sp.wait_ge(out_done, 16 * TT)

        @block.gpsimd
        def _(pool):
            pool.memset(raw[:, :, 0:3], 0.0).then_inc(s["pads"], 1)
            pool.memset(vaug[:, :, :, P:P + 1], 1.0).then_inc(s["pads"], 1)

        @block.scalar
        def _(act):
            chain = [0]

            def link(ins):
                chain[0] += 1
                ins.then_inc(act_chain, 1)
                act.wait_ge(act_chain, chain[0])

            for name, src in (("norm1", t["norm1"]), ("norm2", t["norm2"]), ("b_ada", t["b_ada"]),
                              ("conv_w", t["conv_w"].rearrange("l j n -> l (j n)")), ("conv_b", t["conv_b"]),
                              ("diff_norm", t["diff_norm"]), ("mlstm_norm", t["mlstm_norm"])):
                r0, r1 = ROWS[name]
                act.dma_start(vrows[r0:r1, :], src.rearrange("l (r n) -> (l r) n", n=P)).then_inc(vec_in, 16)
            act.dma_start(w_if[:], w_in[:, :, C_IF:C_IF + 8]).then_inc(bc_in, 16)
            act.dma_start(b_if[:], t["b_if"][0].partition_broadcast(P)).then_inc(bc_in, 16)
            for i, n in enumerate(("lam_q1", "lam_k1", "lam_q2", "lam_k2")):
                act.dma_start(lamv[:, i, :], t[n][0].partition_broadcast(P)).then_inc(bc_in, 16)
            act.dma_start(const[:, 2 * P:NCONST], t["const"][:, 2 * P:NCONST]).then_inc(const2_in, 16)
            act.dma_start(b_r[:, 0:G], t["b_rg"][0].partition_broadcast(P)).then_inc(wr_in, 16)
            act.dma_start(b_r[:, G:G + NE], t["b_re"][0].partition_broadcast(P)).then_inc(wr_in, 16)
            act.dma_start(w_r[:, :, 0:G], t["w_rg"][0].rearrange("(k p) n -> p k n", p=P)).then_inc(wr_in, 16)
            act.dma_start(w_r[:, :, G:G + NE], t["w_re"][0].rearrange("(k p) n -> p k n", p=P)).then_inc(wr_in, 16)

            act.wait_ge(*full("cT"))
            release(act.activation(S("cs", 8), pb("cT")[:, 0:8], ACT.Silu), "cT")
            act.wait_ge(x_in, 16 * TT)
            for tt in range(TT):
                act.activation(junk[:, tt * D:(tt + 1) * D], x[:, tt, :], ACT.Square,
                               accum_out=S("ms1", TT)[:, tt:tt + 1]).then_inc(s["sq"], 1)
            act.wait_ge(s["var"], 1)
            act.activation(S("std1", TT), S("var1", TT), ACT.Sqrt).then_inc(s["std"], 1)
            act.wait_ge(s["mod1"], 2)
            for i in range(2):
                act.wait_ge(*full(f"xT{i}"))
                for j in range(2):
                    k = 2 * i + j
                    ins = act.activation(hT[:, k, :], pb(f"xT{i}")[:, j * T:(j + 1) * T], ACT.Identity,
                                         bias=S("B1", KD)[:, k:k + 1], scale=S("A1", KD)[:, k:k + 1])
                release(ins, f"xT{i}")
            act.wait_ge(s["lam_e"], 1)
            act.activation(S("lexp", 2), S("ldot", 2), ACT.Exp).then_inc(s["lexp"], 1)
            for i in range(4):
                act.wait_ge(*full(f"qk{i}"))
                release(act.activation(qkT[:, 2 * i:2 * i + 2, :], pb(f"qk{i}")[:].rearrange("p (a n) -> p a n", a=2),
                                       ACT.Copy), f"qk{i}")
                if i == 1:
                    act.wait_ge(s["gates"], 2)
                    act.activation(grow[0:4, 2, :], grow[0:4, 2, :], ACT.Exp).then_inc(s["gexp"], 1)
                    act.wait_ge(s["gexp"], 1)
                    act.activation(grow[0:4, 2, :], grow[0:4, 2, :], ACT.Ln, bias=1.0).then_inc(s["gln"], 1)
            for h in range(HEADS):
                for c in range(2):
                    act.wait_ge(s["smax"], 2 * h + c + 1)
                    act.activation(sc[:, h % 2, c, 0:P], sc[:, h % 2, c, 0:P], ACT.Exp,
                                   bias=S(f"nmx{h % 2}", 4)[:, 2 * c:2 * c + 1],
                                   accum_out=S(f"Z{h % 2}", 4)[:, 2 * c:2 * c + 1])
                    act.activation(sc[:, h % 2, c, P:384], sc[:, h % 2, c, P:384], ACT.Exp,
                                   bias=S(f"nmx{h % 2}", 4)[:, 2 * c + 1:2 * c + 2],
                                   accum_out=S(f"Z{h % 2}", 4)[:, 2 * c + 1:2 * c + 2]).then_inc(s["pexp"], 1)
                act.wait_ge(s["pads"], 1)
                act.wait_ge(*full(f"ml{h}"))
                release(act.activation(raw[:, 2 * h:2 * h + 2, 3:T + 3],
                                       pb(f"ml{h}")[:].rearrange("p (a n) -> p a n", a=2), ACT.Copy), f"ml{h}")
            act.wait_ge(*free("cols"))
            act.activation(S("emn", 8), S("ccol", 16)[:, 8:16], ACT.Exp).then_inc(s["emn"], 1)
            for h in range(HEADS):
                if h % 2:
                    act.wait_ge(*free(f"Mb{h // 2}"))
                else:
                    act.wait_ge(s["warg"], h // 2 + 1)
                act.activation(wts[h][:, 0:T], wts[h][:, 0:T], ACT.Exp, bias=S("ccol", 16)[:, h:h + 1])
                act.activation(wts[h][:, T:384], wts[h][:, T:384], ACT.Exp,
                               bias=S("ccol", 16)[:, 4 + h:5 + h]).then_inc(s["wexp"], 1)
            act.wait_ge(s["pads"], 2)
            for i in range(2):
                act.wait_ge(*full(f"mv{i}"))
                release(act.activation(vaug[:, :, 2 * i:2 * i + 2, 0:P],
                                       pb(f"mv{i}")[:].rearrange("p (t h n) -> p t h n", t=2, h=2), ACT.Copy), f"mv{i}")
            for h in range(HEADS):
                act.wait_ge(*full(f"aT{h}"))
                if h >= 2:
                    act.wait_ge(s["pv"], h - 1)
                release(act.activation(aT[:, h % 2, :], pb(f"aT{h}")[:, 0:384], ACT.Copy), f"aT{h}")
            for i in range(4):
                act.wait_ge(s["conv_out"], i + 1)
                pair = mqk[:, 2 * i:2 * i + 2, :].rearrange("p a n -> p (a n)")
                act.activation(pair, pair, ACT.Silu).then_inc(s["mqk_r"], 1)
            for i in range(2):
                act.wait_ge(*full(f"mo{i}"))
                release(act.activation(osig[:, :, 256 * i:256 * i + 256],
                                       pb(f"mo{i}")[:].rearrange("p (t n) -> p t n", t=2), ACT.Sigmoid), f"mo{i}")
            act.wait_ge(s["a_r"], 8)
            act.dma_start(gt1b, t["b_ada"][0, 2 * D:3 * D].partition_broadcast(P)).then_inc(gt1_in, 16)
            for tt in range(TT):
                act.wait_ge(*full(f"o{tt}"))
                for h in range(HEADS):
                    ins = act.activation(o[:, tt, h * P:(h + 1) * P], pb(f"o{tt}")[:, h * P:(h + 1) * P], ACT.Square,
                                         accum_out=S("ms2", 8)[:, tt * 4 + h:tt * 4 + h + 1])
            ins.then_inc(s["h_sq"], 1)
            act.wait_ge(s["var2"], 1)
            act.activation(S("std2", 8), S("var2", 8), ACT.Sqrt).then_inc(s["std2"], 1)
            for i in range(4):
                act.wait_ge(*full(f"ga{i}"))
                release(act.activation(ga[:, 2 * i:2 * i + 2, :], pb(f"ga{i}")[:].rearrange("p (a n) -> p a n", a=2),
                                       ACT.Sigmoid), f"ga{i}")
            for h in range(HEADS):
                act.wait_ge(*free(f"num{h}"))
                for tt in range(TT):
                    ins = act.activation(tmp[:, 0, (2 * h + tt) % 4 * P:((2 * h + tt) % 4 + 1) * P],
                                         osig[:, tt, h * P:(h + 1) * P], ACT.Square,
                                         accum_out=S("ms3", 8)[:, tt * 4 + h:tt * 4 + h + 1])
                    if h == 3 and tt == 1:
                        ins.then_inc(s["h_sq"], 1)
                    else:
                        link(ins)
            act.wait_ge(s["var3"], 1)
            act.activation(S("std3", 8), S("var3", 8), ACT.Sqrt).then_inc(s["std3"], 1)
            for i in range(2):
                act.wait_ge(*full(f"yaT{i}"))
                release(act.activation(yT[:, 2 * i:2 * i + 2, :], pb(f"yaT{i}")[:].rearrange("p (a n) -> p a n", a=2),
                                       ACT.Identity, scale=S("dgain", 1), bias=0.0), f"yaT{i}")
            act.wait_ge(*full("num2"))
            act.wait_ge(*full("num3"))
            act.dma_start(gt2b, t["b_ada"][0, 5 * D:6 * D].partition_broadcast(P)).then_inc(gt2_in, 16)
            act.dma_start(nfb, t["norm_f"].partition_broadcast(P)).then_inc(nf_in, 16)
            for i in range(4):
                act.wait_ge(*full(f"gm{i}"))
                release(act.activation(gm2[:, 2 * i:2 * i + 2, :], pb(f"gm{i}")[:].rearrange("p (a n) -> p a n", a=2),
                                       ACT.Sigmoid), f"gm{i}")
            for i in range(2):
                act.wait_ge(*full(f"ymT{i}"))
                release(act.activation(yT[:, 4 + 2 * i:6 + 2 * i, :], pb(f"ymT{i}")[:].rearrange("p (a n) -> p a n", a=2),
                                       ACT.Identity, scale=col("mlstm_norm"), bias=0.0), f"ymT{i}")
            for i in range(4):
                act.wait_ge(s["x2"], i + 1)
                for tt in range(TT):
                    ins = act.activation(tmp[:, 1, 0:256], x[:, tt, 256 * i:256 * i + 256], ACT.Square,
                                         accum_out=S("ms4", 8)[:, 2 * i + tt:2 * i + tt + 1])
                    if i < 3 or tt == 0:
                        link(ins)
                if i == 3:
                    ins.then_inc(s["sq2"], 1)
                act.wait_ge(*full(f"x2T{i}"))
                release(act.activation(hT[:, 2 * i:2 * i + 2, :], pb(f"x2T{i}")[:].rearrange("p (a n) -> p a n", a=2),
                                       ACT.Copy), f"x2T{i}")
            act.wait_ge(s["var4"], 1)
            act.activation(S("std4", TT), S("var4", TT), ACT.Sqrt).then_inc(s["std4"], 1)
            act.wait_ge(s["lg_r"], 1)
            for tt in range(TT):
                act.activation(R("gexp", TT, G)[:, tt, :], R("lg", TT, 36)[:, tt, 0:G], ACT.Exp,
                               bias=R("ngmax", TT)[:, tt:tt + 1],
                               accum_out=R("gsum", TT)[:, tt:tt + 1]).then_inc(s["rexp"], 1)
            act.wait_ge(s["lg_r"], 2)
            act.activation(R("e2", TT), R("dv", TT), ACT.Exp).then_inc(s["rexp"], 1)

            act.memzero(outs2[:, 0:512]).then_inc(s["o_act"], 1)

            def gather_half(b, half, count):
                act.wait_ge(s["g_full"], count)
                for j in range(4):
                    k = 4 * half + j
                    ins = act.activation(xg[:, b, k, :], bank[4][:, j * P:(j + 1) * P], ACT.Identity,
                                         bias=S("B2", KD)[:, k:k + 1], scale=S("A2", KD)[:, k:k + 1])
                ins.then_inc(s["g_evac"], 1)

            def quad(it, b):
                act.wait_ge(used, it * QU + UP_UNITS)
                act.activation(sig, bank[5][:, 0:F], ACT.Sigmoid).then_inc(s["sig_r"], 1)
                gather_half(1 - b, 0, it * 2 + 3)
                gather_half(1 - b, 1, it * 2 + 4)
                act.wait_ge(used, it * QU + QU)
                act.wait_ge(s["scat"], it + 1)
                act.activation(outs2[:, 0:512], bank[6][:], ACT.Copy).then_inc(s["o_act"], 1)

            gather_half(0, 0, 1)
            gather_half(0, 1, 2)
            with act.Fori(0, NQ // 2) as i:
                for b in range(2):
                    quad(i * 2 + b, b)
            act.wait_ge(s["flag_r"], 1)
            over = act.value_load(flag[0:1, 0:1], min_val=0, max_val=1)
            with act.If(over > 0):
                with act.Fori(1, PASSES) as p:
                    with act.Fori(0, NQ // 2) as i:
                        for b in range(2):
                            quad(p * NQ + i * 2 + b, b)
            act.activation(S("one_k", 1), ones[:, 0:1], ACT.Copy).then_inc(s["act_end"], 1)

            for tt in range(TT):
                act.wait_ge(s["x3"], 2 * tt + 2)
                act.activation(junk[:, tt * D:(tt + 1) * D], x[:, tt, :], ACT.Square,
                               accum_out=S("ms5", TT)[:, tt:tt + 1]).then_inc(s["sq5"], 1)
            act.wait_ge(s["var5"], 1)
            act.activation(S("std5", TT), S("var5", TT), ACT.Sqrt).then_inc(s["std5"], 1)

        @block.vector
        def _(dve):
            chain = [0]

            def link(ins):
                chain[0] += 1
                ins.then_inc(dve_chain, 1)
                dve.wait_ge(dve_chain, chain[0])

            def own(ins, name, n):
                ins.then_inc(s[name], 1)
                dve.wait_ge(s[name], n)

            def rows(i):
                dve.wait_ge(*full(f"ada{i}"))
                if i >= 2:
                    last = {2: "adaT0", 3: "adaT1", 4: "gt1b1", 5: "adaT3"}[i]
                    dve.wait_ge(*full(last))
                release(dve.tensor_copy(arow[:, i % 2, :], pb(f"ada{i}")[:, 0:256]), f"ada{i}")

            def columns(dst, i):
                dve.wait_ge(*full(f"adaT{i}"))
                turned = pb(f"adaT{i}")[:, 0:256].rearrange("p (j u r) -> p u j r", j=2, u=4)[:, :, :, 0]
                release(dve.tensor_tensor(dst.rearrange("p (u j) -> p u j", u=4), turned,
                                          col("b_ada", 8 * i, 8).rearrange("p (u j) -> p u j", u=4), ALU.add),
                        f"adaT{i}")
                dve.wait_ge(*free(f"adaT{i}"))

            def spread(dst, g):
                for i in range(2):
                    job, sl = f"gt{g}b{i}", slice(512 * i, 512 * i + 512)
                    dve.wait_ge(*full(job))
                    release(dve.tensor_tensor(dst[:, sl], pb(job)[:], dst[:, sl], ALU.add), job)

            dve.wait_ge(s["sq"], 2)
            dve.tensor_scalar(S("var1", TT), S("ms1", TT), 1.0 / D, EPS, ALU.mult, ALU.add).then_inc(s["var"], 1)
            dve.wait_ge(s["std"], 1)
            link(dve.reciprocal(S("r1", TT), S("std1", TT)))
            for tt in range(TT):
                dve.tensor_scalar(xn[:, tt, :], x[:, tt, :], S("r1", TT)[:, tt:tt + 1], None,
                                  ALU.mult).then_inc(s["xn_r"], 1)
            dve.wait_ge(*full("vT"))
            release(dve.tensor_copy(cols[:], pb("vT")[:, 0:NROWS]), "vT")
            dve.wait_ge(*free("vT"))
            dve.tensor_scalar(S("dgain", 1), col("diff_norm"), 1.0 - LAMBDA_INIT, None, ALU.mult).then_inc(s["cols_r"], 1)
            rows(0)
            rows(1)
            dve.wait_ge(bc_in, 96)
            for i in range(2):
                ins = dve.tensor_tensor_reduce(lamv[:, 2 * i, :], lamv[:, 2 * i, :], lamv[:, 2 * i + 1, :], 1.0, 0.0,
                                               ALU.mult, ALU.add, S("ldot", 2)[:, i:i + 1])
            ins.then_inc(s["lam_e"], 1)
            m1 = S("m1", 16)
            columns(m1[:, 0:8], 0)
            columns(m1[:, 8:16], 1)
            dve.tensor_copy(S("B1", KD), m1[:, 0:8]).then_inc(s["mod1"], 1)
            dve.scalar_tensor_tensor(out=S("A1", KD), in0=m1[:, 8:16], scalar=1.0, in1=col("norm1", 0, 8),
                                     op0=ALU.add, op1=ALU.mult).then_inc(s["mod1"], 1)
            dve.wait_ge(s["mod1"], 2)
            for i in range(2, 4):
                dve.wait_ge(*full(f"xT{i}"))
                for j in range(2):
                    k = 2 * i + j
                    ins = dve.tensor_scalar(hT[:, k, :], pb(f"xT{i}")[:, j * T:(j + 1) * T], S("A1", KD)[:, k:k + 1],
                                            S("B1", KD)[:, k:k + 1], ALU.mult, ALU.add)
                release(ins, f"xT{i}")
            dve.wait_ge(s["lexp"], 1)
            link(dve.tensor_tensor(S("nlam", 1), S("lexp", 2)[:, 1:2], S("lexp", 2)[:, 0:1], ALU.subtract))
            link(dve.tensor_scalar(S("nlam2", 1), S("nlam", 1), -LAMBDA_INIT, None, ALU.add))
            dve.wait_ge(*full("if"))
            release(dve.tensor_tensor(S("gpre", 16).rearrange("p (t n) -> p t n", t=2),
                                      pb("if")[:, 0:16].rearrange("p (t n) -> p t n", t=2),
                                      b_if[:].unsqueeze(1).to_broadcast([P, TT, 8]), ALU.add), "if")
            dve.wait_ge(*full("ifT"))
            release(dve.tensor_copy(grow[0:4, 0:2, :], pb("ifT")[0:4, :].rearrange("p (a n) -> p a n", a=2)), "ifT")
            dve.wait_ge(*free("ifT"))
            link(dve.tensor_scalar(grow[0:4, 3, :], grow[0:4, 1, :], -1.0, None, ALU.mult))
            own(dve.tensor_tensor(grow[0:4, 2, :], grow[0:4, 3, :], grow[0:4, 1, :], ALU.min), "gates", 1)
            own(dve.tensor_scalar(grow[0:4, 3, :], grow[0:4, 1, :], 0.0, None, ALU.min), "gates", 2)
            for i in range(2):
                dve.wait_ge(*full(f"v{i}"))
                release(dve.tensor_copy(v[:, :, 256 * i:256 * i + 256],
                                        pb(f"v{i}")[:].rearrange("p (t n) -> p t n", t=2)), f"v{i}")
            dve.wait_ge(*free("v1"))
            dve.wait_ge(const2_in, 16)
            dve.wait_ge(s["gln"], 1)
            link(dve.tensor_tensor(grow[0:4, 3, :], grow[0:4, 3, :], grow[0:4, 2, :], ALU.subtract))
            link(dve.tensor_tensor_scan(grow[0:4, 1, :], ones[0:4, 0:1].to_broadcast([4, T]), grow[0:4, 3, :], 0.0, ALU.mult, ALU.add))
            link(dve.tensor_tensor(grow[0:4, 2, :], grow[0:4, 0, :], grow[0:4, 1, :], ALU.subtract))
            link(dve.tensor_tensor_scan(grow[0:4, 3, :], K("mask")[0:4, P:P + 1].to_broadcast([4, T]), grow[0:4, 2, :], 0.0, ALU.add, ALU.max))
            dve.scalar_tensor_tensor(out=grow[0:4, 0, :], in0=grow[0:4, 1, :], scalar=-1.0, in1=grow[0:4, 3, :],
                                     op0=ALU.mult, op1=ALU.subtract).then_inc(s["grows"], 1)

            def scores(h):
                if h >= 2:
                    dve.wait_ge(s["a_r"], 2 * h - 2)
                for c in range(2):
                    job = f"s{2 * h + c}"
                    dve.wait_ge(*full(job))
                    release(dve.scalar_tensor_tensor(out=sc[:, h % 2, c, :], in0=pb(job)[:, 0:384], scalar=DA_HD ** -0.5,
                                                     in1=K("alibi")[:, h, :], op0=ALU.mult, op1=ALU.add), job)
                    dve.wait_ge(*free(job))
                    dve.tensor_reduce(S(f"nmx{h % 2}", 4)[:, 2 * c:2 * c + 1], sc[:, h % 2, c, 0:P], AX.X, ALU.max, negate=True)
                    dve.tensor_reduce(S(f"nmx{h % 2}", 4)[:, 2 * c + 1:2 * c + 2], sc[:, h % 2, c, P:384], AX.X, ALU.max,
                                      negate=True).then_inc(s["smax"], 1)

            def combine(h):
                dve.wait_ge(s["pexp"], 2 * h + 2)
                link(dve.reciprocal(S(f"rZ{h % 2}", 4), S(f"Z{h % 2}", 4)))
                link(dve.tensor_scalar(S("rZl", 2), S(f"rZ{h % 2}", 4)[:, 2:4], S("nlam2", 1), None, ALU.mult))
                for i, (a, b) in enumerate(((0, P), (P, 384))):
                    link(dve.tensor_scalar(a_sb[:, h, a:b], sc[:, h % 2, 1, a:b], S("rZl", 2)[:, i:i + 1], None,
                                           ALU.mult))
                    dve.scalar_tensor_tensor(out=a_sb[:, h, a:b], in0=sc[:, h % 2, 0, a:b],
                                             scalar=S(f"rZ{h % 2}", 4)[:, i:i + 1], in1=a_sb[:, h, a:b],
                                             op0=ALU.mult, op1=ALU.add).then_inc(s["a_r"], 1)

            def conv(i):
                dve.wait_ge(*free(f"ml{i}"))
                for k in (2 * i, 2 * i + 1):
                    link(dve.tensor_scalar(mqk[:, k, :], raw[:, k, 3:T + 3], col("conv_w", 24 + k), col("conv_b", k),
                                           ALU.mult, ALU.add))
                    for j in range(3):
                        ins = dve.scalar_tensor_tensor(out=mqk[:, k, :], in0=raw[:, k, j:j + T],
                                                       scalar=col("conv_w", 8 * j + k), in1=mqk[:, k, :],
                                                       op0=ALU.mult, op1=ALU.add)
                        if j < 2:
                            link(ins)
                    if k % 2 == 0:
                        link(ins)
                ins.then_inc(s["conv_out"], 1)

            scores(0)
            scores(1)
            combine(0)
            scores(2)
            combine(1)
            scores(3)
            conv(0)
            combine(2)
            conv(1)
            combine(3)
            conv(2)
            dve.wait_ge(*full("cols"))
            release(dve.tensor_copy(S("ccol", 16), pb("cols")[:, 0:16]), "cols")

            def decay_arg(h):
                job = f"Mb{h // 2}"
                dve.wait_ge(*full(job))
                m = pb(job)[:, (h % 2) * T:(h % 2) * T + T]
                dve.tensor_tensor(wts[h][:, 0:T], K("mask")[:, 0:T], m, ALU.subtract)
                ins = dve.tensor_tensor(wts[h][:, T:384], K("mask")[:, T:384], m[:, P:T], ALU.subtract)
                if h % 2:
                    release(ins, job)
                else:
                    ins.then_inc(s["warg"], 1)

            for h in range(HEADS):
                decay_arg(h)
            conv(3)
            dve.wait_ge(s["h_sq"], 1)
            dve.tensor_scalar(S("var2", 8), S("ms2", 8), 1.0 / P, EPS, ALU.mult, ALU.add).then_inc(s["var2"], 1)
            dve.wait_ge(s["std2"], 1)
            link(dve.reciprocal(S("r2", 8), S("std2", 8)))
            for tt in range(TT):
                release(dve.tensor_tensor(o[:, tt, :].rearrange("p (h n) -> p h n", h=4),
                                          pb(f"o{tt}")[:].rearrange("p (h n) -> p h n", h=4),
                                          S("r2", 8)[:, 4 * tt:4 * tt + 4].unsqueeze(2).to_broadcast([P, 4, P]),
                                          ALU.mult), f"o{tt}")

            def decay(h):
                dve.wait_ge(s["wexp"], h + 1)
                job = f"ms{h}"
                dve.wait_ge(*full(job))
                release(dve.scalar_tensor_tensor(out=wts[h], in0=pb(job)[:, 0:384], scalar=P ** -0.5,
                                                 in1=wts[h], op0=ALU.mult, op1=ALU.mult), job)

            def hidden(h):
                job = f"num{h}"
                dve.wait_ge(*full(job))
                dve.wait_ge(s["emn"], 1)
                nd = pb(job)[:, 0:2 * (P + 1)].rearrange("p (t n) -> p t n", t=2)
                den, em = nd[:, :, P:P + 1], S("emn", 8).rearrange("p (t n) -> p t n", t=2)[:, :, h:h + 1]
                d1, d2 = (S(n, 2).rearrange("p (t n) -> p t n", t=2) for n in ("d1", "d2"))
                link(dve.scalar_tensor_tensor(out=d1, in0=den, scalar=-1.0, in1=em, op0=ALU.mult, op1=ALU.max))
                link(dve.tensor_tensor(d2, den, d1, ALU.max))
                link(dve.reciprocal(S("rd", 2), S("d2", 2)))
                for tt in range(TT):
                    ins = dve.scalar_tensor_tensor(out=osig[:, tt, h * P:(h + 1) * P], in0=nd[:, tt, 0:P],
                                                   scalar=S("rd", 2)[:, tt:tt + 1], in1=osig[:, tt, h * P:(h + 1) * P],
                                                   op0=ALU.mult, op1=ALU.mult)
                release(ins, job)

            decay(0)
            decay(1)
            hidden(0)
            decay(2)
            hidden(1)
            decay(3)
            hidden(2)
            hidden(3)
            dve.wait_ge(s["h_sq"], 2)
            dve.tensor_scalar(S("var3", 8), S("ms3", 8), 1.0 / P, EPS, ALU.mult, ALU.add).then_inc(s["var3"], 1)
            dve.wait_ge(s["std3"], 1)
            link(dve.reciprocal(S("r3", 8), S("std3", 8)))
            for tt in range(TT):
                view = osig[:, tt, :].rearrange("p (h n) -> p h n", h=4)
                dve.tensor_tensor(view, view, S("r3", 8)[:, 4 * tt:4 * tt + 4].unsqueeze(2).to_broadcast([P, 4, P]),
                                  ALU.mult).then_inc(s["hn_r"], 1)
            rows(2)
            rows(3)
            dve.wait_ge(gt1_in, 16)
            spread(gt1b, 1)
            B2, A2 = S("B2", KD), S("A2", KD)
            columns(B2, 3)
            dve.tensor_copy(S("B2_r", KD), B2).then_inc(s["mod2"], 1)
            for i in range(4):
                job, view = f"bra{i}", ga[:, 2 * i:2 * i + 2, :]
                dve.wait_ge(*free(f"ga{i}"))
                dve.wait_ge(*full(job))
                release(dve.tensor_tensor(view, pb(job)[:].rearrange("p (a n) -> p a n", a=2), view, ALU.mult), job)
            for i in range(4):
                job, view, va = f"brm{i}", gm2[:, 2 * i:2 * i + 2, :], ga[:, 2 * i:2 * i + 2, :]
                dve.wait_ge(*free(f"gm{i}"))
                dve.wait_ge(*full(job))
                release(dve.tensor_tensor(view, pb(job)[:].rearrange("p (a n) -> p a n", a=2), view, ALU.mult), job)
                dve.wait_ge(*free(job))
                dve.tensor_tensor(va, va, view, ALU.add).then_inc(s["merged"], 1)
            def residual(i):
                dve.wait_ge(*full(f"wo{i}"))
                if i >= 1:
                    dve.wait_ge(s["x2"], i)
                g = gt1b[:, 256 * i:256 * i + 256].unsqueeze(1).to_broadcast([P, TT, 256])
                tv = tmp[:, 0, :].rearrange("p (t n) -> p t n", t=2)
                release(dve.tensor_tensor(tv, pb(f"wo{i}")[:].rearrange("p (t n) -> p t n", t=2), g, ALU.mult), f"wo{i}")
                dve.wait_ge(*free(f"wo{i}"))
                xv = x[:, :, 256 * i:256 * i + 256]
                own(dve.tensor_tensor(xv, xv, tv, ALU.add), "x2", i + 1)

            rows(4)
            residual(0)
            columns(A2, 4)
            own(dve.scalar_tensor_tensor(out=A2, in0=A2, scalar=1.0, in1=col("norm2", 0, 8),
                                         op0=ALU.add, op1=ALU.mult), "mod2", 2)
            residual(1)
            dve.wait_ge(wr_in, 64)
            dve.wait_ge(*full("rb"))
            release(dve.tensor_tensor(rbias[:], pb("rb")[:, 0:G + NE], b_r[:], ALU.add), "rb")
            dve.wait_ge(*free("rb"))
            for k in range(KD):
                dve.tensor_scalar(w_r[:, k, :], w_r[:, k, :], A2[:, k:k + 1], None, ALU.mult).then_inc(s["wr_r"], 1)
            residual(2)
            residual(3)
            dve.wait_ge(s["sq2"], 1)
            link(dve.tensor_reduce(S("ms4s", TT), S("ms4", 8).rearrange("p (i t) -> p t i", t=TT), AX.X, ALU.add))
            dve.tensor_scalar(S("var4", TT), S("ms4s", TT), 1.0 / D, EPS, ALU.mult, ALU.add).then_inc(s["var4"], 1)
            dve.wait_ge(s["std4"], 1)
            link(dve.reciprocal(S("r4", TT), S("std4", TT)))

            lg, g8 = R("lg", TT, 36), R("g8", TT, 8)
            link(dve.memset(g8, -3.0e38))
            dve.wait_ge(*full("lg"))
            release(dve.tensor_tensor(lg, pb("lg")[:, 0:72].rearrange("p (t n) -> p t n", t=2),
                                      S("r4", TT).unsqueeze(2).to_broadcast([P, TT, 36]), ALU.mult), "lg")
            dve.wait_ge(*free("lg"))
            link(dve.tensor_tensor(lg, lg, rbias[:].unsqueeze(1).to_broadcast([P, TT, 36]), ALU.add))
            link(dve.tensor_copy(g8[:, :, 0:G], lg[:, :, 0:G]))
            g_top, e_top, esel = R("g_top", TT, 8), R("e_top", TT, 8), R("esel", TT, 8)
            for tt in range(TT):
                link(dve.max(g_top[:, tt, :], g8[:, tt, :]))
            dve.tensor_scalar(R("ngmax", TT).unsqueeze(2), g_top[:, :, 0:1], -1.0, None, ALU.mult).then_inc(s["lg_r"], 1)
            for tt in range(TT):
                dve.tensor_scalar(xn[:, tt, :], x[:, tt, :], S("r4", TT)[:, tt:tt + 1], None,
                                  ALU.mult).then_inc(s["x2n"], 1)
            for tt in range(TT):
                link(dve.max_index(idx[:, 0, tt, :], g_top[:, tt, :], g8[:, tt, :]))
            gi, ei = R("gi", TT, 8), R("ei", TT, 8)
            link(dve.tensor_copy(gi, idx[:, 0]))
            ohg = R("ohg", TT, G)
            iota8 = K("iota8")
            link(dve.tensor_tensor(ohg, iota8[:, :, 0:G], gi[:, :, 0:1].to_broadcast([P, TT, G]), ALU.is_equal))
            prod = R("prod", TT, G, E)
            e_lg = lg[:, :, G:G + NE].rearrange("p t (g e) -> p t g e", g=G)
            link(dve.tensor_tensor(prod, e_lg, ohg.unsqueeze(3).to_broadcast([P, TT, G, E]), ALU.mult))
            link(dve.tensor_reduce(esel, prod.rearrange("p t g e -> p t e g"), AX.X, ALU.add))
            for tt in range(TT):
                link(dve.max(e_top[:, tt, :], esel[:, tt, :]))
            rows(5)
            own(dve.tensor_tensor(R("dv", TT).unsqueeze(2), e_top[:, :, 1:2], e_top[:, :, 0:1], ALU.subtract), "lg_r", 2)
            for tt in range(TT):
                link(dve.max_index(idx[:, 1, tt, :], e_top[:, tt, :], esel[:, tt, :]))
            link(dve.tensor_copy(ei, idx[:, 1]))
            oh1, oh2 = R("oh1", TT, E), R("oh2", TT, E)
            link(dve.tensor_tensor(oh1, iota8, ei[:, :, 0:1].to_broadcast([P, TT, E]), ALU.is_equal))
            link(dve.tensor_tensor(oh2, iota8, ei[:, :, 1:2].to_broadcast([P, TT, E]), ALU.is_equal))
            m8 = R("m8", TT, E)
            link(dve.tensor_tensor(m8, oh1, oh2, ALU.add))
            mask = R("mask", TT, NE)
            own(dve.tensor_tensor(mask.rearrange("p t (g e) -> p t g e", g=G),
                                  ohg.unsqueeze(3).to_broadcast([P, TT, G, E]),
                                  m8.unsqueeze(2).to_broadcast([P, TT, G, E]), ALU.mult), "mask_r", 1)
            dve.wait_ge(s["rexp"], 3)
            den = R("den", TT)
            link(dve.tensor_scalar(den, R("e2", TT), 1.0, None, ALU.add))
            link(dve.tensor_tensor(den, den, R("gsum", TT), ALU.mult))
            w1, w2 = R("w1", TT), R("w2", TT)
            link(dve.reciprocal(w1, den))
            link(dve.tensor_tensor(w2, w1, R("e2", TT), ALU.mult))
            we = R("we", TT, E)
            link(dve.tensor_tensor(oh1, oh1, w1.unsqueeze(2).to_broadcast([P, TT, E]), ALU.mult))
            link(dve.tensor_tensor(oh2, oh2, w2.unsqueeze(2).to_broadcast([P, TT, E]), ALU.mult))
            link(dve.tensor_tensor(we, oh1, oh2, ALU.add))
            NX = NE + QUAD
            gate, rank = R("gate", TT, NX), R("rank", TT, NX)
            link(dve.tensor_tensor(R("g32", TT, NE).rearrange("p t (g e) -> p t g e", g=G),
                                   ohg.unsqueeze(3).to_broadcast([P, TT, G, E]),
                                   we.unsqueeze(2).to_broadcast([P, TT, G, E]), ALU.mult))
            link(dve.tensor_copy(gate[:, :, 0:NE], R("g32", TT, NE)))
            link(dve.tensor_copy(gate[:, :, NE:NX], gate[:, :, 0:QUAD]))
            dve.wait_ge(gt2_in, 16)
            spread(gt2b, 2)
            dve.wait_ge(*full("rank"))
            link(dve.scalar_tensor_tensor(out=rank[:, :, 0:NE], in0=pb("rank")[:, 0:2 * NE].rearrange("p (t n) -> p t n", t=2),
                                          scalar=1.0, in1=mask, op0=ALU.add, op1=ALU.mult))
            release(dve.reduce_max(S("cmax", 1)[0:1, :], pb("rank")[0:1, 2 * NE:3 * NE], AX.X), "rank")
            dve.wait_ge(*free("rank"))
            dve.tensor_scalar(flag[0:1, :], S("cmax", 1)[0:1, :], CAP + 0.5, None, ALU.is_gt).then_inc(s["flag_r"], 1)
            link(dve.tensor_scalar(rank[:, :, 0:NE], rank[:, :, 0:NE], -1.0, None, ALU.add))
            link(dve.tensor_scalar(rank[:, :, NE:NX], rank[:, :, 0:QUAD], -float(CAP), None, ALU.add))

            dve.memset(ptg[:, 1], 0.0).then_inc(s["pt_evac"], 1)
            dve.memset(outs2[:, 512:1024], 0.0).then_inc(s["o_dve"], 1)
            dve.memset(hid, 0.0).then_inc(s["hid_done"], 1)
            MC = 2

            def one_hot(at, base, c0):
                dve.tensor_tensor(pone[:], K("slot"), rank[:, :, at].unsqueeze(3).to_broadcast([P, TT, QUAD, CAP]),
                                  ALU.is_equal).then_inc(s["moe_chain"], 1)
                dve.wait_ge(s["moe_chain"], base + c0)
                dve.tensor_tensor(pgate[:], pone[:], gate[:, :, at].unsqueeze(3).to_broadcast([P, TT, QUAD, CAP]),
                                  ALU.mult).then_inc(s["pg_ready"], 1)

            def quad(q, it, b):
                dve.wait_ge(s["pt_full"], it + 1)
                one_hot(bass.ds(q * QUAD + QUAD, QUAD), it * MC, 2)
                dve.wait_ge(s["sig_r"], it + 1)
                dve.tensor_tensor(act_a, bank[5][:, 0:F], sig, ALU.mult).then_inc(s["moe_chain"], 1)
                dve.wait_ge(s["moe_chain"], it * MC + 3)
                dve.tensor_tensor(hid, bank[5][:, F:2 * F], act_a, ALU.mult).then_inc(s["hid_done"], 1)
                dve.wait_ge(s["pt_full"], it + 2)
                dve.tensor_copy(hidT.rearrange("p f n -> p (f n)"), bank[4][:, T:2 * T]).then_inc(s["hT_evac"], 1)
                dve.wait_ge(s["scat"], it + 1)
                dve.tensor_copy(ptg[:, 1 - b].rearrange("p t n -> p (t n)"), bank[4][:, 0:T]).then_inc(s["pt_evac"], 1)
                dve.wait_ge(used, it * QU + QU)
                dve.tensor_copy(outs2[:, 512:1024], bank[7][:]).then_inc(s["o_dve"], 1)

            one_hot(slice(0, QUAD), 0, 1)
            dve.wait_ge(s["pt_full"], 1)
            dve.tensor_copy(ptg[:, 0].rearrange("p t n -> p (t n)"), bank[4][:, 0:T]).then_inc(s["pt_evac"], 1)
            with dve.Fori(0, NQ // 2) as i:
                for b in range(2):
                    quad(i * 2 + b, i * 2 + b, b)
            dve.wait_ge(s["flag_r"], 1)
            over = dve.value_load(flag[0:1, 0:1], min_val=0, max_val=1)
            with dve.If(over > 0):
                with dve.Fori(1, PASSES) as p:
                    dve.tensor_scalar(rank, rank, -float(CAP), None, ALU.add).then_inc(s["r_chain"], 1)
                    dve.wait_ge(s["r_chain"], p)
                    dve.tensor_copy(S("one_q", 1), ones[:, 0:1])
                    with dve.Fori(0, NQ // 2) as i:
                        for b in range(2):
                            quad(i * 2 + b, p * NQ + i * 2 + b, b)
            dve.tensor_copy(S("one_p", 1), ones[:, 0:1]).then_inc(s["dve_end"], 1)

            dve.wait_ge(s["y_full"], 1)
            for tt in range(TT):
                for c in range(2):
                    n = 2 * tt + c
                    sl = slice(512 * c, 512 * c + 512)
                    link(dve.tensor_tensor(tmp[:, n % 2, :], bank[n][:], gt2b[:, sl], ALU.mult))
                    own(dve.tensor_tensor(x[:, tt, sl], x[:, tt, sl], tmp[:, n % 2, :], ALU.add), "x3", n + 1)
            dve.wait_ge(s["sq5"], 2)
            dve.tensor_scalar(S("var5", TT), S("ms5", TT), 1.0 / D, EPS, ALU.mult, ALU.add).then_inc(s["var5"], 1)
            dve.wait_ge(s["std5"], 1)
            link(dve.reciprocal(S("r5", TT), S("std5", TT)))
            dve.wait_ge(nf_in, 16)
            for tt in range(TT):
                dve.scalar_tensor_tensor(out=x[:, tt, :], in0=x[:, tt, :], scalar=S("r5", TT)[:, tt:tt + 1], in1=nfb,
                                         op0=ALU.mult, op1=ALU.mult).then_inc(s["y_out"], 1)

        @block.tensor
        def _(pe):
            at = [0]

            def take(job):
                n = JOB[job]
                if n >= 8:
                    pe.wait_ge(bank_free[n % 8], n // 8)
                return bank[n % 8]

            def next_unit(k):
                n = at[0]
                at[0] += 1
                pe.wait_ge(landed[n % RING], 16 * (n // RING + 1))
                return unit(n, k)

            def ada(i):
                ps = take(f"ada{i}")
                w = [next_unit(8) for _ in range(4)]
                for k in range(KD):
                    for u in range(4):
                        ins = pe.matmul(ps[32 * u:32 * u + 32, 0:256], S("cs", 8)[:, k:k + 1].to_broadcast([P, 32]),
                                        w[u][:, k, :], start=(k == 0), stop=(k == KD - 1), tile_position=(0, 32 * u))
                filled(ins, f"ada{i}")

            def ada_turn(i):
                ps = take(f"adaT{i}")
                pe.wait_ge(*free(f"ada{i}"))
                for j in range(2):
                    ins = pe.transpose(ps[:, j * P:(j + 1) * P], arow[:, i % 2, j * P:(j + 1) * P], ident)
                filled(ins, f"adaT{i}")

            def ada_spread(i, g):
                for half in range(2):
                    ps = take(f"gt{g}b{half}")
                    pe.wait_ge(*free(f"ada{i}"))
                    for j in range(2):
                        u = 2 * half + j
                        ins = pe.matmul(ps[:, j * 256:(j + 1) * 256], ident[:, 32 * u:32 * u + 1].to_broadcast([P, P]),
                                        arow[:, i % 2, :], start=True, stop=True)
                    filled(ins, f"gt{g}b{half}")

            def proj_T(job, src, w, j0=0, nk=KD):
                ps = take(job)
                for j in range(2):
                    for k in range(nk):
                        ins = pe.matmul(ps[:, j * T:(j + 1) * T], w[:, k, (j0 + j) * P:(j0 + j + 1) * P], src(k),
                                        start=(k == 0), stop=(k == nk - 1))
                filled(ins, job)

            def proj(job, src, w):
                ps = take(job)
                for tt in range(TT):
                    for k in range(KD):
                        ins = pe.matmul(ps[:, tt * 256:(tt + 1) * 256], src(k)[:, tt * P:(tt + 1) * P], w[:, k, :],
                                        start=(k == 0), stop=(k == KD - 1))
                filled(ins, job)

            hsrc = lambda k: hT[:, k, :]

            pe.wait_ge(const_in, 16)
            pe.wait_ge(c_in, 16)
            filled(pe.transpose(take("cT")[:, 0:8], vrows[0:8, :], ident[0:8, 0:8]), "cT")
            pe.wait_ge(*free("cT"))
            ada(0)
            ada(1)
            pe.wait_ge(vec_in, 112)
            filled(pe.transpose(take("vT")[:, 0:NROWS], vrows[0:NROWS, :], ident[0:NROWS, 0:NROWS]), "vT")
            pe.wait_ge(s["xn_r"], 2)
            for i in range(4):
                ps = take(f"xT{i}")
                for j in range(2):
                    for tt in range(TT):
                        k = 2 * i + j
                        ins = pe.transpose(ps[:, j * T + tt * P:j * T + (tt + 1) * P], xn[:, tt, k * P:(k + 1) * P], ident)
                filled(ins, f"xT{i}")
            ada_turn(0)
            ada_turn(1)
            for i in range(3):
                pe.wait_ge(*free(f"xT{i}"))
            pe.wait_ge(*free("xT3"))
            pe.wait_ge(bc_in, 96)
            ps = take("if")
            for tt in range(TT):
                for k in range(KD):
                    ins = pe.matmul(ps[:, tt * 8:(tt + 1) * 8], hT[:, k, tt * P:(tt + 1) * P], w_if[:, k, :],
                                    start=(k == 0), stop=(k == KD - 1))
            filled(ins, "if")
            for i in range(4):
                if i == 1:
                    ps = take("ifT")
                    pe.wait_ge(*free("if"))
                    for g in range(2):
                        for tt in range(TT):
                            ins = pe.transpose(ps[0:4, g * T + tt * P:g * T + (tt + 1) * P],
                                               S("gpre", 16)[:, tt * 8 + g * 4:tt * 8 + g * 4 + 4], ident)
                    filled(ins, "ifT")
                proj_T(f"qk{i}", hsrc, next_unit(8))
            for i in range(2):
                proj(f"v{i}", hsrc, next_unit(8))
            for i in range(4):
                pe.wait_ge(*free(f"qk{i}"))
            for h in range(HEADS):
                for c in range(2):
                    ps = take(f"s{2 * h + c}")
                    r = slice(64 * c, 64 * c + 64)
                    pe.matmul(ps[:, 0:P], qkT[r, h, 0:P], qkT[r, 4 + h, 0:P], start=True, stop=True)
                    filled(pe.matmul(ps[:, P:384], qkT[r, h, P:T], qkT[r, 4 + h, :], start=True, stop=True),
                           f"s{2 * h + c}")
            for i in range(4):
                proj_T(f"ml{i}", hsrc, next_unit(8))
            ps = take("cols")
            pe.wait_ge(s["grows"], 1)
            pe.wait_ge(const2_in, 16)
            for j, row in enumerate((2, 0)):
                for tt in range(TT):
                    ins = pe.transpose(ps[:, 8 * j + 4 * tt:8 * j + 4 * tt + 4], grow[0:4, row, tt * P:(tt + 1) * P],
                                       ident[0:4, 0:4])
            filled(ins, "cols")
            for i in range(2):
                ps = take(f"Mb{i}")
                for j in range(2):
                    ins = pe.matmul(ps[:, j * T:(j + 1) * T], ident[0:4, 2 * i + j:2 * i + j + 1].to_broadcast([4, P]), grow[0:4, 3, :],
                                    start=True, stop=True)
                filled(ins, f"Mb{i}")
            for i in range(2):
                proj(f"mv{i}", hsrc, next_unit(8))
            po = [take("o0"), take("o1")]
            pe.wait_ge(*free("v0"))
            pe.wait_ge(*free("v1"))

            def transpose_a(h):
                ps = take(f"aT{h}")
                pe.wait_ge(s["a_r"], 2 * h + 2)
                for j in range(3):
                    ins = pe.transpose(ps[:, j * P:(j + 1) * P], a_sb[:, h, j * P:(j + 1) * P], ident)
                filled(ins, f"aT{h}")

            def times_v(h):
                pe.wait_ge(*free(f"aT{h}"))
                hs = slice(h * P, (h + 1) * P)
                ins = pe.matmul(po[0][:, hs], aT[:, h % 2, 0:P], v[:, 0, hs], start=True, stop=True)
                if h == 3:
                    filled(ins, "o0")
                pe.matmul(po[1][:, hs], aT[:, h % 2, P:2 * P], v[:, 0, hs], start=True, stop=False)
                ins = pe.matmul(po[1][:, hs], aT[:, h % 2, 2 * P:384], v[:, 1, hs], start=False, stop=True)
                if h < 3:
                    ins.then_inc(s["pv"], 1)
                else:
                    filled(ins, "o1")

            transpose_a(0)
            transpose_a(1)
            times_v(0)
            proj("mo0", hsrc, next_unit(8))
            transpose_a(2)
            times_v(1)
            transpose_a(3)
            times_v(2)
            proj("mo1", hsrc, next_unit(8))
            times_v(3)
            def mscores(h):
                ps = take(f"ms{h}")
                pe.wait_ge(s["mqk_r"], 4)
                pe.matmul(ps[:, 0:T], mqk[:, 4 + h, 0:P], mqk[:, h, :], start=True, stop=True)
                filled(pe.matmul(ps[:, T:384], mqk[:, 4 + h, P:T], mqk[:, h, P:T], start=True, stop=True), f"ms{h}")

            def numerator(h):
                ps = take(f"num{h}")
                pe.wait_ge(*free(f"ms{h}"))
                pe.wait_ge(*free("mv0"))
                pe.wait_ge(*free("mv1"))
                n = P + 1
                pe.matmul(ps[:, 0:n], wts[h][:, 0:P], vaug[:, 0, h, :], start=True, stop=True)
                pe.matmul(ps[:, n:2 * n], wts[h][:, P:T], vaug[:, 0, h, :], start=True, stop=False)
                filled(pe.matmul(ps[:, n:2 * n], wts[h][:, T:384], vaug[:, 1, h, :], start=False, stop=True),
                       f"num{h}")

            def gate_a(i):
                proj_T(f"ga{i}", hsrc, next_unit(8))

            gate_a(0)
            gate_a(1)
            mscores(0)
            mscores(1)
            gate_a(2)
            numerator(0)
            mscores(2)
            numerator(1)
            mscores(3)
            gate_a(3)
            numerator(2)
            numerator(3)
            for i in range(2):
                ps = take(f"yaT{i}")
                pe.wait_ge(*free("o0"))
                pe.wait_ge(*free("o1"))
                for j in range(2):
                    for tt in range(TT):
                        h = 2 * i + j
                        ins = pe.transpose(ps[:, j * T + tt * P:j * T + (tt + 1) * P], o[:, tt, h * P:(h + 1) * P], ident)
                filled(ins, f"yaT{i}")
            for i in range(4):
                proj_T(f"gm{i}", hsrc, next_unit(8))
            for i in range(2):
                ps = take(f"ymT{i}")
                pe.wait_ge(s["hn_r"], 2)
                for j in range(2):
                    for tt in range(TT):
                        h = 2 * i + j
                        ins = pe.transpose(ps[:, j * T + tt * P:j * T + (tt + 1) * P], osig[:, tt, h * P:(h + 1) * P],
                                           ident)
                filled(ins, f"ymT{i}")
            ada(2)
            ada(3)
            ada_spread(2, 1)
            ada_turn(3)
            for name, y0 in (("a", 0), ("m", 4)):
                pe.wait_ge(*free(f"y{name}T0"))
                pe.wait_ge(*free(f"y{name}T1"))
                for u in range(2):
                    w = next_unit(4)
                    for i in range(2):
                        proj_T(f"br{name}{2 * u + i}", lambda k: yT[:, y0 + k, :], w, 2 * i, 4)
            ada(4)
            pe.wait_ge(s["merged"], 4)

            def out_proj(i):
                proj(f"wo{i}", lambda k: ga[:, k, :], next_unit(8))

            def turn_x(i):
                ps = take(f"x2T{i}")
                pe.wait_ge(s["x2"], i + 1)
                for j in range(2):
                    for tt in range(TT):
                        k = 2 * i + j
                        ins = pe.transpose(ps[:, j * T + tt * P:j * T + (tt + 1) * P], x[:, tt, k * P:(k + 1) * P], ident)
                filled(ins, f"x2T{i}")

            out_proj(0)
            ada_turn(4)
            out_proj(1)
            ps = take("rb")
            pe.wait_ge(wr_in, 64)
            pe.wait_ge(s["mod2"], 1)
            for k in range(KD):
                ins = pe.matmul(ps[:, 0:G + NE], S("B2", KD)[:, k:k + 1].to_broadcast([P, P]), w_r[:, k, :],
                                start=(k == 0), stop=(k == KD - 1))
            filled(ins, "rb")
            out_proj(2)
            turn_x(0)
            out_proj(3)
            turn_x(1)
            ada(5)
            turn_x(2)
            turn_x(3)
            for i in range(4):
                pe.wait_ge(*free(f"x2T{i}"))
            pe.wait_ge(s["wr_r"], KD)
            ps = take("lg")
            for tt in range(TT):
                for k in range(KD):
                    ins = pe.matmul(ps[:, tt * 36:(tt + 1) * 36], hT[:, k, tt * P:(tt + 1) * P], w_r[:, k, :],
                                    start=(k == 0), stop=(k == KD - 1))
            filled(ins, "lg")
            ada_spread(5, 2)
            ps = take("rank")
            pe.wait_ge(s["mask_r"], 1)
            m = R("mask", TT, NE)
            tri = K("tri")
            pe.matmul(ps[:, 0:NE], tri, m[:, 0, :], start=True, stop=True)
            pe.matmul(ps[:, NE:2 * NE], ones, m[:, 0, :], start=True, stop=False)
            pe.matmul(ps[:, NE:2 * NE], tri, m[:, 1, :], start=False, stop=True)
            pe.matmul(ps[0:1, 2 * NE:3 * NE], ones[:, 0:1], m[:, 0, :], start=True, stop=False)
            filled(pe.matmul(ps[0:1, 2 * NE:3 * NE], ones[:, 0:1], m[:, 1, :], start=False, stop=True), "rank")

            for b in range(8):
                uses = len([n for n in range(len(JOBS)) if n % 8 == b])
                pe.wait_ge(bank_free[b], uses)
            pe.wait_ge(s["pt_evac"], 1)
            pe.wait_ge(s["o_act"], 1)
            pe.wait_ge(s["o_dve"], 1)

            def scatter(b, start, stop):
                for tt in range(TT):
                    for c in range(2):
                        ins = pe.matmul(bank[2 * tt + c][:], ptg[:, b, tt, :], outs2[:, 512 * c:512 * c + 512],
                                        start=start, stop=stop, skip_group_check=True)
                return ins

            scatter(1, True, False)

            def gather(half):
                for j in range(4):
                    k = 4 * half + j
                    for tt in range(TT):
                        ins = pe.matmul(bank[4][:, j * P:(j + 1) * P], xn[:, tt, k * P:(k + 1) * P],
                                        pone[:, tt].rearrange("p a n -> p (a n)"), start=(tt == 0), stop=(tt == TT - 1))
                ins.then_inc(s["g_full"], 1)

            def turn(with_hidden):
                for tt in range(TT):
                    ins = pe.transpose(bank[4][:, tt * P:(tt + 1) * P], pgate[:, tt].rearrange("p a n -> p (a n)"), ident)
                if with_hidden:
                    for f in range(2):
                        ins = pe.transpose(bank[4][:, T + f * P:T + (f + 1) * P], hid[:, f * P:(f + 1) * P], ident)
                ins.then_inc(s["pt_full"], 1)

            def arrived(w, e, it):
                n = NPRE + QUAD_POS[(w, e)]
                pe.wait_ge(landed[n % RING], it * 16 + 16 * (n // RING + 1))
                return unit(n, 2 if w == "w2" else 8)

            def up(it, b):
                for m_, w in enumerate(("w1", "w3")):
                    wt = [arrived(w, e, it) for e in range(QUAD)]
                    for k in range(KD):
                        for e in range(QUAD):
                            ins = pe.matmul(bank[5][e * CAP:(e + 1) * CAP, m_ * F:(m_ + 1) * F],
                                            xg[:, b, k, e * CAP:(e + 1) * CAP], wt[e][:, k, :],
                                            start=(k == 0), stop=(k == KD - 1), tile_position=(0, e * CAP))
                            if k == KD - 1:
                                ins.then_inc(used, 1)

            def down(it):
                wt = [arrived("w2", e, it) for e in range(QUAD)]
                for c in range(2):
                    for f in range(2):
                        for e in range(QUAD):
                            ins = pe.matmul(bank[6 + c][e * CAP:(e + 1) * CAP, :], hidT[:, f, e * CAP:(e + 1) * CAP],
                                            wt[e][:, f, 512 * c:512 * c + 512], start=(f == 0), stop=(f == 1),
                                            tile_position=(0, e * CAP))
                            if c == 1 and f == 1:
                                ins.then_inc(used, 1)

            def quad(it, b):
                pe.wait_ge(s["g_evac"], it * 2 + 2)
                pe.wait_ge(s["hid_done"], it + 1)
                up(it, b)
                pe.wait_ge(s["pg_ready"], it + 2)
                pe.wait_ge(s["pt_evac"], it + 2)
                gather(0)
                pe.wait_ge(s["o_act"], it + 1)
                pe.wait_ge(s["o_dve"], it + 1)
                scatter(1 - b, False, False).then_inc(s["scat"], 1)
                pe.wait_ge(s["g_evac"], it * 2 + 3)
                gather(1)
                pe.wait_ge(s["g_evac"], it * 2 + 4)
                pe.wait_ge(s["hid_done"], it + 2)
                turn(True)
                pe.wait_ge(s["hT_evac"], it + 1)
                down(it)

            pe.wait_ge(s["pg_ready"], 1)
            pe.wait_ge(s["x2n"], 2)
            gather(0)
            pe.wait_ge(s["g_evac"], 1)
            gather(1)
            pe.wait_ge(s["g_evac"], 2)
            turn(False)
            with pe.Fori(0, NQ // 2) as i:
                for b in range(2):
                    quad(i * 2 + b, b)
            pe.wait_ge(s["flag_r"], 1)
            over = pe.value_load(flag[0:1, 0:1], min_val=0, max_val=1)
            with pe.If(over > 0):
                with pe.Fori(1, PASSES) as p:
                    with pe.Fori(0, NQ // 2) as i:
                        for b in range(2):
                            quad(p * NQ + i * 2 + b, b)
            pe.wait_ge(s["act_end"], 1)
            pe.wait_ge(s["dve_end"], 1)
            scatter(1, False, True).then_inc(s["y_full"], 1)


_INS = ['x', 'c', 'w_ada', 'b_ada', 'norm1', 'w_in', 'b_if', 'conv_w', 'conv_b', 'lam_q1', 'lam_k1', 'lam_q2',
        'lam_k2', 'diff_norm', 'mlstm_norm', 'w_br_a', 'w_br_m', 'w_out', 'norm2', 'w_rg', 'b_rg', 'w_re', 'b_re',
        'w_e1', 'w_e3', 'w_e2', 'norm_f']


def kernel(**inputs):
    import concourse.bacc as bacc
    from concourse.bass_utils import run_bass_kernel_spmd

    nc = bacc.Bacc("TRN2", target_bir_lowering=False, num_devices=1)
    arrays, aps = {}, {}
    for name in _INS:
        a = np.ascontiguousarray(inputs[name])
        arrays[f"in_{name}"] = a
        aps[name] = nc.dram_tensor(f"in_{name}", a.shape, mybir.dt.from_np(a.dtype), kind="ExternalInput").ap()
    arrays["in_const"] = constants()
    aps["const"] = nc.dram_tensor("in_const", (P, NCONST), F32, kind="ExternalInput").ap()
    out = nc.dram_tensor("out_0", (1, T, D), F32, kind="ExternalOutput").ap()
    build(nc, aps, out)
    result = run_bass_kernel_spmd(nc, [arrays], core_ids=[0])
    return result.results[0]["out_0"]
```

```python
from contextlib import ExitStack

import numpy as np
import concourse.bass as bass
from concourse import mybir

F32 = mybir.dt.float32
F32R = mybir.dt.float32r
BF16 = mybir.dt.bfloat16
I32 = mybir.dt.int32
U32 = mybir.dt.uint32
ALU = mybir.AluOpType
ACT = mybir.ActivationFunctionType
AX = mybir.AxisListType

P = 128
D, T = 1024, 256
KD, TT = D // P, T // P
HEADS, DA_HD = 4, 64
EPS = 1e-6
G, E, F = 4, 8, 256
NE = G * E
QUAD = 4
NQ = NE // QUAD
CAP = P // QUAD
PASSES = T // CAP
LAMBDA_INIT = 0.8 - 0.6 * float(np.exp(-0.3 * 0))
NEG = -1.0e30
RING = 8
HI = 3
SLOTS = RING + HI + 1
UNIT = 2048

ROWS, NROWS = {}, 0
for _name, _n in (("c", 8), ("norm1", 8), ("norm2", 8), ("b_ada", 48), ("conv_w", 32),
                  ("conv_b", 8), ("diff_norm", 1), ("mlstm_norm", 1)):
    ROWS[_name] = (NROWS, NROWS + _n)
    NROWS += _n

C_Q, C_K, C_V, C_MQK, C_MV, C_MO, C_IF, C_GA, C_GM = 0, 512, 1024, 1536, 2560, 3072, 3584, 3592, 4616


def unit_list():
    units = [("ada", 256 * i) for i in range(8)]
    for c0, n in ((C_Q, 2), (C_K, 2), (C_V, 2), (C_MQK, 4), (C_MV, 2), (C_MO, 2), (C_GA, 4), (C_GM, 4)):
        units += [("in", c0 + 256 * i) for i in range(n)]
    units += [("ada", 2048 + 256 * i) for i in range(8)]
    units += [("br_a", 0), ("br_a", 512), ("br_m", 0), ("br_m", 512)]
    units += [("ada", 4096 + 256 * i) for i in range(4)]
    units += [("out", 256 * i) for i in range(4)]
    units += [("ada", 5120 + 256 * i) for i in range(4)]
    return units


def unit_jobs():
    jobs = ["ada0"] * 4 + ["ada1"] * 4
    jobs += [f"qk{i}" for i in range(4)] + ["v0", "v1"] + [f"ml{i}" for i in range(4)]
    jobs += ["mv0", "mv1", "mo0", "mo1"] + [f"ga{i}" for i in range(4)] + [f"gm{i}" for i in range(4)]
    jobs += ["ada2"] * 4 + ["ada3"] * 4 + ["bra1", "bra3", "brm1", "brm3"]
    return jobs + ["ada4"] * 4 + [f"wo{i}" for i in range(4)] + ["ada5"] * 4


UNITS = unit_list()
NPRE = len(UNITS)
DENSE = [n for n, (kind, _) in enumerate(UNITS) if kind != "ada"]
QUAD_UNITS = [(w, e) for w in ("w1", "w3", "w2") for e in range(QUAD)]
UP_UNITS = 8
QU = len(QUAD_UNITS)
assert QU == SLOTS
QUAD_POS = {u: i for i, u in enumerate(QUAD_UNITS)}

JOBS = (["cT", "ada0", "vT"] + [f"xT{i}" for i in range(4)] + ["adaT0", "ada1", "adaT1", "if"]
        + [f"qk{i}" for i in range(4)]
        + ["v0", "v1"] + [f"s{i}" for i in range(8)] + [f"ml{i}" for i in range(4)]
        + ["cols", "Mb0", "Mb1", "mv0", "mv1", "aT0", "aT1", "o0", "o1", "mo0", "aT2", "aT3", "mo1"]
        + ["ga0", "ga1", "ms0", "ms1", "ga2", "num0", "ms2", "num1", "ms3", "ga3", "num2", "num3"]
        + ["yaT0", "yaT1"] + [f"gm{i}" for i in range(4)]
        + ["ymT0", "ymT1", "ada2", "ada3", "gt1b0", "gt1b1", "adaT3"]
        + [f"bra{i}" for i in range(4)] + [f"brm{i}" for i in range(4)]
        + ["ada4", "wo0", "adaT4", "wo1", "rb", "wo2", "x2T0", "wo3", "x2T1", "lg", "x2T2", "x2T3", "ada5", "rank",
           "gt2b0", "gt2b1"])
UNIT_JOB = unit_jobs()
DENSE_JOB = [UNIT_JOB[n] for n in DENSE]
JOB = {n: i for i, n in enumerate(JOBS)}

CONSTS, NCONST = {}, 0
for _name, _shape in (("ident", (P,)), ("ones", (P,)), ("tri", (P,)), ("alibi", (HEADS, 384)), ("mask", (384,)),
                      ("slot", (TT, QUAD, CAP)), ("iota8", (TT, 8))):
    CONSTS[_name] = (NCONST, _shape)
    NCONST += int(np.prod(_shape))


def constants():
    out = np.zeros((P, NCONST), np.float32)

    def put(name, value):
        c0, shape = CONSTS[name]
        out[:, c0:c0 + int(np.prod(shape))] = np.broadcast_to(value, (P,) + shape).reshape(P, -1)

    i = np.arange(P)
    put("ident", np.eye(P))
    put("ones", np.ones((P, P)))
    put("tri", (i[:, None] < i[None, :]) * 1.0)
    slopes = 2.0 ** (-8.0 * np.arange(1, HEADS + 1) / HEADS)
    dist = (P + i)[:, None] - np.arange(2 * P)[None, :]
    ali = np.where(dist >= 0, -slopes[:, None, None] * dist, NEG).transpose(1, 0, 2)
    put("alibi", np.concatenate([ali[:, :, P:], ali], axis=2))
    tri = np.where(i[None, :] >= i[:, None], 0.0, NEG)
    put("mask", np.concatenate([tri, np.zeros((P, P)), tri], axis=1))
    put("slot", np.arange(CAP)[None, None, None, :])
    put("iota8", np.arange(8)[None, None, :])
    return out


def build(nc, t, out):
    with ExitStack() as ctx:
        def sb(name, shape, dt=F32):
            return ctx.enter_context(nc.sbuf_tensor(name, [P] + list(shape), dt))

        def sem(name):
            return ctx.enter_context(nc.semaphore(name))

        def both(name, shape):
            with nc.sbuf_tensor(name + "_r", [P] + list(shape), F32R) as rounded:
                pass
            return sb(name, shape), rounded

        ring, ring_r = both("ring", [SLOTS, UNIT])
        const = sb("const", [NCONST])
        x = sb("x", [TT, D])
        xn = sb("xn", [TT, D])
        hT, hT_lo = both("hT", [KD, T])
        qkT, yT_lo = both("qkT", [8, T])
        v = sb("v", [TT, 512])
        raw, raw_r = both("raw", [8, T + 3])
        gm, merged_lo = both("gm", [KD, T])
        mqk = sb("mqk", [8, T])
        vaug = sb("vaug", [TT, HEADS, P + 1])
        osig = sb("osig", [TT, 512])
        att = sb("att", [3072])
        WT = sb("WT", [2, 384])
        o = sb("o", [TT, 512])
        tmp = sb("tmp", [2, 512])
        vrows = sb("vrows", [P])
        cols = sb("cols", [NROWS])
        w_if, w_if_lo = both("w_if", [KD, 8])
        w_if_hi = sb("w_if_hi", [KD, 8], F32R)
        b_r = sb("b_r", [G + NE])
        w_r = sb("w_r", [KD, G + NE])
        sm = sb("sm", [320])
        router = sb("router", [800])
        flag = sb("flag", [1], I32)
        idx = sb("idx", [2, TT, 8], U32)

        ga = gm
        gm2 = mqk
        sc = att[:, 0:1536].rearrange("p (b c n) -> p b c n", b=2, c=2)
        a_sb = xn[:].rearrange("p a n -> p (a n)")[:, 0:1536].rearrange("p (h n) -> p h n", h=HEADS)
        wts = [WT[:, 0], WT[:, 1], att[:, 1536:1920], att[:, 1920:2304]]
        aT = att[:, 2304:3072].rearrange("p (b n) -> p b n", b=2)
        gt1b = att[:, 0:1024]
        gt2b = att[:, 1024:2048]
        nfb = att[:, 2048:3072]
        yT, yT_hi = qkT, raw_r[:, :, 0:T]
        hT_hi = ring_r[:, SLOTS - 1, :].rearrange("p (k n) -> p k n", k=KD)
        merged_hi = hT_hi
        sig, act_a, hid = tmp[:, 0, 0:F], tmp[:, 0, F:2 * F], tmp[:, 1, 0:F]
        hidT = WT[:].rearrange("p b n -> p (b n)")[:, 0:2 * P].rearrange("p (f n) -> p f n", f=2)
        arow = sb("arow", [2, 256])
        rbias = sb("rbias", [G + NE])
        lamv = tmp[:, 0, 0:4 * DA_HD].rearrange("p (a n) -> p a n", a=4)
        spare = const[:, CONSTS["alibi"][0]:CONSTS["alibi"][0] + 1024]
        pone = spare[:, 0:256].rearrange("p (t e n) -> p t e n", t=TT, e=QUAD)
        pgate = spare[:, 256:512].rearrange("p (t e n) -> p t e n", t=TT, e=QUAD)
        ptg = spare[:, 512:1024].rearrange("p (b t n) -> p b t n", b=2, t=TT)
        grow = o[:].rearrange("p a (b n) -> p (a b) n", b=2)
        xg = raw[:, :, 0:256].rearrange("p k (b n) -> p b k n", b=2)
        outs = v
        outs2 = outs[:].rearrange("p a n -> p (a n)")
        junk = hT[:].rearrange("p a n -> p (a n)")

        def K(name):
            c0, shape = CONSTS[name]
            ap = const[:, c0:c0 + int(np.prod(shape))]
            if len(shape) == 2:
                return ap.rearrange("p (a b) -> p a b", a=shape[0])
            if len(shape) == 3:
                return ap.rearrange("p (a b c) -> p a b c", a=shape[0], b=shape[1])
            return ap

        ident, ones = K("ident"), K("ones")

        def col(name, i=0, n=1):
            r0 = ROWS[name][0]
            return cols[:, r0 + i:r0 + i + n]

        small_at, small = [0], {}

        def S(name, n=1):
            if name not in small:
                small[name] = (small_at[0], n)
                small_at[0] += n
            a, n = small[name]
            return sm[:, a:a + n]

        r_at, r_names = [0], {}

        def R(name, *shape):
            if name not in r_names:
                r_names[name] = (r_at[0], shape)
                r_at[0] += int(np.prod(shape))
            a, shape = r_names[name]
            ap = router[:, a:a + int(np.prod(shape))]
            if len(shape) == 2:
                return ap.rearrange("p (a b) -> p a b", a=shape[0])
            if len(shape) == 3:
                return ap.rearrange("p (a b c) -> p a b c", a=shape[0], b=shape[1])
            return ap

        bank = [ctx.enter_context(nc.psum_tensor(f"bank{i}", [P, 512], F32)) for i in range(8)]
        bank_full = [sem(f"bank_full{i}") for i in range(8)]
        bank_free = [sem(f"bank_free{i}") for i in range(8)]

        def pb(job):
            return bank[JOB[job] % 8]

        def full(job):
            return bank_full[JOB[job] % 8], JOB[job] // 8 + 1

        def free(job):
            return bank_free[JOB[job] % 8], JOB[job] // 8 + 1

        def filled(ins, job):
            ins.then_inc(bank_full[JOB[job] % 8], 1)

        def release(ins, job):
            ins.then_inc(bank_free[JOB[job] % 8], 1)

        y_banks, up_bank, token_bank, out_banks = bank[3:7], bank[0], bank[7], bank[1:3]

        x_in, const_in, const2_in, c_in, vec_in, bc_in, nf_in, gt1_in, gt2_in, wr_in, out_done = (
            sem(n) for n in ("x_in", "const_in", "const2_in", "c_in", "vec_in", "bc_in", "nf_in", "gt1_in", "gt2_in", "wr_in", "out_done"))
        landed = [sem(f"landed{i}") for i in range(SLOTS)]
        used = sem("used")
        dve_chain, act_chain = sem("dve_chain"), sem("act_chain")
        names = ["sq", "var", "std", "xn_r", "cols_r", "mod1", "gates", "gexp", "gln", "grows", "conv_out", "mqk_r",
                 "smax", "pexp", "a_r", "emn", "warg", "wexp", "pv", "h_sq", "var2", "std2", "hn_r", "var3", "std3",
                 "arow_r", "mod2", "wr_r", "merged", "lexp", "lam_e", "x2", "sq2", "var4", "std4", "x2n", "xT_r", "lg_r",
                 "rexp", "mask_r", "flag_r", "pads", "x3", "sq5", "var5", "std5", "y_out",
                 "g_full", "g_evac", "pg_ready", "pt_full", "pt_evac", "sig_r", "hid_done", "hT_evac",
                 "o_act", "o_dve", "scat", "act_end", "dve_end", "moe_chain", "y_full", "r_chain", "w_hi", "w_lo", "h_lo", "h_lo_pool", "if_hi", "y_lo", "m_hi", "m_lo", "r4", "sel_r"]
        s = {n: sem(n) for n in names}

        w_ada = t["w_ada"][0].rearrange("(k p) n -> p k n", p=P)
        w_in = t["w_in"][0].rearrange("(k p) n -> p k n", p=P)
        w_bra = t["w_br_a"][0].rearrange("(k p) n -> p k n", p=P)
        w_brm = t["w_br_m"][0].rearrange("(k p) n -> p k n", p=P)
        w_out = t["w_out"][0].rearrange("(k p) n -> p k n", p=P)
        w_e = {"w1": t["w_e1"].rearrange("l g e (k p) f -> (l g e) p k f", p=P),
               "w3": t["w_e3"].rearrange("l g e (k p) f -> (l g e) p k f", p=P),
               "w2": t["w_e2"].rearrange("l g e (k p) n -> (l g e) p k n", p=P)}

        def slot_of(n):
            return n % RING if n < NPRE + RING else n - NPRE

        def landed_value(n):
            return 16 * sum(slot_of(m) == slot_of(n) for m in range(n + 1))

        def unit(n, k):
            return ring[:, slot_of(n), :].rearrange("p (k n) -> p k n", k=k)

        def hi(d):
            return ring_r[:, RING + d % HI, :]

        block = ctx.enter_context(nc.Block())

        @block.sync
        def _(sp):
            sp.dma_start(vrows[ROWS["c"][0]:ROWS["c"][1], :], t["c"].rearrange("l (r n) -> (l r) n", n=P)
                         ).then_inc(c_in, 16)
            sp.dma_start(const[:, 0:2 * P], t["const"][:, 0:2 * P]).then_inc(const_in, 16)
            for tt in range(TT):
                sp.dma_start(x[:, tt, :], t["x"][0, tt * P:(tt + 1) * P, :]).then_inc(x_in, 16)
            src = {"ada": w_ada, "in": w_in, "br_a": w_bra, "br_m": w_brm, "out": w_out}
            for n, (kind, c0) in enumerate(UNITS):
                if n >= RING:
                    sp.wait_ge(*full(UNIT_JOB[n - RING]))
                k = 4 if kind in ("br_a", "br_m") else 8
                w = UNIT // k
                sp.dma_start(unit(n, k), src[kind][:, :, c0:c0 + w]).then_inc(landed[slot_of(n)], 16)

            def load(q, u):
                w, e = QUAD_UNITS[u]
                n = NPRE + u
                k = 2 if w == "w2" else 8
                expert = w_e[w][q * QUAD + e] if isinstance(q, int) else \
                    w_e[w][bass.ds(q * QUAD + e, 1)].rearrange("a p k n -> p (a k) n")
                sp.dma_start(unit(n, k), expert).then_inc(landed[slot_of(n)], 16)

            def load_quad(q, it):
                for u in range(QU):
                    sp.wait_ge(used, it * QU + (u - QU + 1))
                    load(q, u)

            for u in range(QU):
                sp.wait_ge(*full(UNIT_JOB[NPRE + u - RING] if u < RING else "wo3"))
                load(0, u)
            with sp.Fori(1, NQ) as q:
                load_quad(q, q)
            sp.wait_ge(s["flag_r"], 1)
            over = sp.value_load(flag[0:1, 0:1], min_val=0, max_val=1)
            with sp.If(over > 0):
                with sp.Fori(1, PASSES) as p:
                    with sp.Fori(0, NQ) as q:
                        load_quad(q, p * NQ + q)
            for tt in range(TT):
                sp.wait_ge(s["y_out"], tt + 1)
                sp.dma_start(out[0, tt * P:(tt + 1) * P, :], x[:, tt, :]).then_inc(out_done, 16)
            sp.wait_ge(out_done, 16 * TT)

        @block.gpsimd
        def _(pool):
            pool.memset(raw[:, :, 0:3], 0.0).then_inc(s["pads"], 1)
            pool.memset(vaug[:, :, :, P:P + 1], 1.0).then_inc(s["pads"], 1)
            pool.wait_ge(*free("xT0"))
            pool.wait_ge(*free("xT1"))
            pool.tensor_tensor(hT_lo[:, 0:4, :], hT[:, 0:4, :], hT_hi[:, 0:4, :].bitcast(F32),
                               ALU.subtract).then_inc(s["h_lo_pool"], 1)
            for d, n in enumerate(DENSE):
                pool.wait_ge(s["w_hi"], d + 1)
                pool.tensor_tensor(ring_r[:, slot_of(n), :], ring[:, slot_of(n), :], hi(d).bitcast(F32),
                                   ALU.subtract).then_inc(s["w_lo"], 1)

        @block.scalar
        def _(act):
            chain = [0]

            def link(ins):
                chain[0] += 1
                ins.then_inc(act_chain, 1)
                act.wait_ge(act_chain, chain[0])

            for name, src in (("norm1", t["norm1"]), ("norm2", t["norm2"]), ("b_ada", t["b_ada"]),
                              ("conv_w", t["conv_w"].rearrange("l j n -> l (j n)")), ("conv_b", t["conv_b"]),
                              ("diff_norm", t["diff_norm"]), ("mlstm_norm", t["mlstm_norm"])):
                r0, r1 = ROWS[name]
                act.dma_start(vrows[r0:r1, :], src.rearrange("l (r n) -> (l r) n", n=P)).then_inc(vec_in, 16)
            act.wait_ge(*full("cT"))
            release(act.activation(S("cs", 8), pb("cT")[:, 0:8], ACT.Silu), "cT")
            act.dma_start(w_if[:], w_in[:, :, C_IF:C_IF + 8]).then_inc(bc_in, 16)
            for g in range(2):
                act.dma_start(S("b_if", 2)[0:4, g:g + 1], t["b_if"][0, 4 * g:4 * g + 4].rearrange("(p o) -> p o", o=1)).then_inc(bc_in, 16)
            for i, n in enumerate(("lam_q1", "lam_k1", "lam_q2", "lam_k2")):
                act.dma_start(lamv[:, i, :], t[n][0].partition_broadcast(P)).then_inc(bc_in, 16)
            act.dma_start(const[:, 2 * P:NCONST], t["const"][:, 2 * P:NCONST]).then_inc(const2_in, 16)
            act.dma_start(b_r[:, 0:G], t["b_rg"][0].partition_broadcast(P)).then_inc(wr_in, 16)
            act.dma_start(b_r[:, G:G + NE], t["b_re"][0].partition_broadcast(P)).then_inc(wr_in, 16)
            act.dma_start(w_r[:, :, 0:G], t["w_rg"][0].rearrange("(k p) n -> p k n", p=P)).then_inc(wr_in, 16)
            act.dma_start(w_r[:, :, G:G + NE], t["w_re"][0].rearrange("(k p) n -> p k n", p=P)).then_inc(wr_in, 16)


            def split(d):
                n = DENSE[d]
                act.wait_ge(landed[slot_of(n)], landed_value(n))
                if d >= HI:
                    act.wait_ge(*full(DENSE_JOB[d - HI]))
                act.activation(hi(d), ring[:, slot_of(n), :], ACT.Copy).then_inc(s["w_hi"], 1)

            act.wait_ge(x_in, 16 * TT)
            for tt in range(TT):
                act.activation(junk[:, tt * D:(tt + 1) * D], x[:, tt, :], ACT.Square,
                               accum_out=S("ms1", TT)[:, tt:tt + 1]).then_inc(s["sq"], 1)
            act.wait_ge(s["var"], 1)
            act.activation(S("std1", TT), S("var1", TT), ACT.Sqrt).then_inc(s["std"], 1)
            act.wait_ge(bc_in, 112)
            act.activation(w_if_hi[:], w_if[:], ACT.Copy).then_inc(s["if_hi"], 1)
            split(0)
            act.wait_ge(s["mod1"], 2)
            for i in range(2):
                act.wait_ge(*full(f"xT{i}"))
                for dst in (hT_hi, hT):
                    for j in range(2):
                        k = 2 * i + j
                        ins = act.activation(dst[:, k, :], pb(f"xT{i}")[:, j * T:(j + 1) * T], ACT.Identity,
                                             bias=S("B1", KD)[:, k:k + 1], scale=S("A1", KD)[:, k:k + 1])
                release(ins, f"xT{i}")
            split(1)
            split(2)
            act.wait_ge(s["lam_e"], 1)
            act.activation(S("lexp", 2), S("ldot", 2), ACT.Exp).then_inc(s["lexp"], 1)
            for i in range(4):
                act.wait_ge(*full(f"qk{i}"))
                release(act.activation(qkT[:, 2 * i:2 * i + 2, :], pb(f"qk{i}")[:].rearrange("p (a n) -> p a n", a=2),
                                       ACT.Copy), f"qk{i}")
                split(3 + i)
                if i == 1:
                    act.wait_ge(s["gates"], 2)
                    act.activation(grow[0:4, 2, :], grow[0:4, 2, :], ACT.Exp).then_inc(s["gexp"], 1)
                    act.wait_ge(s["gexp"], 1)
                    act.activation(grow[0:4, 2, :], grow[0:4, 2, :], ACT.Ln, bias=1.0).then_inc(s["gln"], 1)
            split(7)
            split(8)
            for h in range(HEADS):
                for c in range(2):
                    act.wait_ge(s["smax"], 2 * h + c + 1)
                    act.activation(sc[:, h % 2, c, 0:P], sc[:, h % 2, c, 0:P], ACT.Exp,
                                   bias=S(f"nmx{h % 2}", 4)[:, 2 * c:2 * c + 1],
                                   accum_out=S(f"Z{h % 2}", 4)[:, 2 * c:2 * c + 1])
                    act.activation(sc[:, h % 2, c, P:384], sc[:, h % 2, c, P:384], ACT.Exp,
                                   bias=S(f"nmx{h % 2}", 4)[:, 2 * c + 1:2 * c + 2],
                                   accum_out=S(f"Z{h % 2}", 4)[:, 2 * c + 1:2 * c + 2]).then_inc(s["pexp"], 1)
                act.wait_ge(s["pads"], 1)
                act.wait_ge(*full(f"ml{h}"))
                release(act.activation(raw[:, 2 * h:2 * h + 2, 3:T + 3],
                                       pb(f"ml{h}")[:].rearrange("p (a n) -> p a n", a=2), ACT.Copy), f"ml{h}")
                split(9 + h)
            act.wait_ge(s["pads"], 2)
            for i in range(2):
                act.wait_ge(*full(f"mv{i}"))
                release(act.activation(vaug[:, :, 2 * i:2 * i + 2, 0:P],
                                       pb(f"mv{i}")[:].rearrange("p (t h n) -> p t h n", t=2, h=2), ACT.Copy), f"mv{i}")
                split(13 + i)

            def copy_a(h):
                act.wait_ge(*full(f"aT{h}"))
                if h >= 2:
                    act.wait_ge(s["pv"], h - 1)
                release(act.activation(aT[:, h % 2, :], pb(f"aT{h}")[:, 0:384], ACT.Copy), f"aT{h}")

            copy_a(0)
            copy_a(1)
            act.wait_ge(*free("cols"))
            act.activation(S("emn", 8), S("ccol", 16)[:, 8:16], ACT.Exp).then_inc(s["emn"], 1)
            for h in range(HEADS):
                if h % 2:
                    act.wait_ge(*free(f"Mb{h // 2}"))
                else:
                    act.wait_ge(s["warg"], h // 2 + 1)
                act.activation(wts[h][:, 0:T], wts[h][:, 0:T], ACT.Exp, bias=S("ccol", 16)[:, h:h + 1])
                act.activation(wts[h][:, T:384], wts[h][:, T:384], ACT.Exp,
                               bias=S("ccol", 16)[:, 4 + h:5 + h]).then_inc(s["wexp"], 1)
            split(15)
            copy_a(2)
            copy_a(3)
            for i in range(4):
                act.wait_ge(s["conv_out"], i + 1)
                pair = mqk[:, 2 * i:2 * i + 2, :].rearrange("p a n -> p (a n)")
                act.activation(pair, pair, ACT.Silu).then_inc(s["mqk_r"], 1)
            for i in range(2):
                act.wait_ge(*full(f"mo{i}"))
                release(act.activation(osig[:, :, 256 * i:256 * i + 256],
                                       pb(f"mo{i}")[:].rearrange("p (t n) -> p t n", t=2), ACT.Sigmoid), f"mo{i}")
            split(16)
            act.wait_ge(s["a_r"], 8)
            act.dma_start(gt1b, t["b_ada"][0, 2 * D:3 * D].partition_broadcast(P)).then_inc(gt1_in, 16)
            for tt in range(TT):
                act.wait_ge(*full(f"o{tt}"))
                for h in range(HEADS):
                    ins = act.activation(o[:, tt, h * P:(h + 1) * P], pb(f"o{tt}")[:, h * P:(h + 1) * P], ACT.Square,
                                         accum_out=S("ms2", 8)[:, tt * 4 + h:tt * 4 + h + 1])
            ins.then_inc(s["h_sq"], 1)
            act.wait_ge(s["var2"], 1)
            act.activation(S("std2", 8), S("var2", 8), ACT.Sqrt).then_inc(s["std2"], 1)
            for i in range(4):
                act.wait_ge(*full(f"ga{i}"))
                release(act.activation(ga[:, 2 * i:2 * i + 2, :], pb(f"ga{i}")[:].rearrange("p (a n) -> p a n", a=2),
                                       ACT.Sigmoid), f"ga{i}")
                split(17 + i)
            for h in range(HEADS):
                act.wait_ge(*free(f"num{h}"))
                for tt in range(TT):
                    ins = act.activation(tmp[:, 0, (2 * h + tt) % 4 * P:((2 * h + tt) % 4 + 1) * P],
                                         osig[:, tt, h * P:(h + 1) * P], ACT.Square,
                                         accum_out=S("ms3", 8)[:, tt * 4 + h:tt * 4 + h + 1])
                    if h == 3 and tt == 1:
                        ins.then_inc(s["h_sq"], 1)
                    else:
                        link(ins)
            act.wait_ge(s["var3"], 1)
            act.activation(S("std3", 8), S("var3", 8), ACT.Sqrt).then_inc(s["std3"], 1)
            for i in range(2):
                act.wait_ge(*full(f"yaT{i}"))
                for dst in (yT, yT_hi):
                    ins = act.activation(dst[:, 2 * i:2 * i + 2, :], pb(f"yaT{i}")[:].rearrange("p (a n) -> p a n", a=2),
                                         ACT.Identity, scale=S("dgain", 1), bias=0.0)
                release(ins, f"yaT{i}")
            act.wait_ge(*full("num2"))
            act.wait_ge(*full("num3"))
            act.dma_start(gt2b, t["b_ada"][0, 5 * D:6 * D].partition_broadcast(P)).then_inc(gt2_in, 16)
            act.dma_start(nfb, t["norm_f"].partition_broadcast(P)).then_inc(nf_in, 16)
            for i in range(4):
                act.wait_ge(*full(f"gm{i}"))
                release(act.activation(gm2[:, 2 * i:2 * i + 2, :], pb(f"gm{i}")[:].rearrange("p (a n) -> p a n", a=2),
                                       ACT.Sigmoid), f"gm{i}")
                split(21 + i)
            for i in range(2):
                act.wait_ge(*full(f"ymT{i}"))
                for dst in (yT, yT_hi):
                    ins = act.activation(dst[:, 4 + 2 * i:6 + 2 * i, :], pb(f"ymT{i}")[:].rearrange("p (a n) -> p a n", a=2),
                                         ACT.Identity, scale=col("mlstm_norm"), bias=0.0)
                release(ins, f"ymT{i}")
            split(25)
            split(26)
            split(27)
            for i in range(4):
                act.wait_ge(s["merged"], i + 1)
                act.activation(merged_hi[:, 2 * i:2 * i + 2, :], ga[:, 2 * i:2 * i + 2, :], ACT.Copy).then_inc(s["m_hi"], 1)
            split(28)
            split(29)
            act.memzero(outs2[:, 0:512]).then_inc(s["o_act"], 1)
            act.activation(S("table", 1), S("std1", TT)[:, 0:1], ACT.Sqrt)

            def square(i):
                act.wait_ge(s["x2"], i + 1)
                for tt in range(TT):
                    ins = act.activation(o[:, tt, 256 * (i % 2):256 * (i % 2) + 256], x[:, tt, 256 * i:256 * i + 256],
                                         ACT.Square, accum_out=S("ms4", 8)[:, 2 * i + tt:2 * i + tt + 1])
                    if i < 3 or tt == 0:
                        link(ins)
                if i == 3:
                    ins.then_inc(s["sq2"], 1)

            def copy_x(i):
                act.wait_ge(*full(f"x2T{i}"))
                release(act.activation(hT[:, 2 * i:2 * i + 2, :], pb(f"x2T{i}")[:].rearrange("p (a n) -> p a n", a=2),
                                       ACT.Copy), f"x2T{i}")

            square(0)
            copy_x(0)
            square(1)
            copy_x(1)
            square(2)
            copy_x(2)
            square(3)
            copy_x(3)
            act.wait_ge(s["var4"], 1)
            act.activation(S("std4", TT), S("var4", TT), ACT.Sqrt).then_inc(s["std4"], 1)
            act.wait_ge(s["r4"], 1)
            for tt in range(TT):
                act.activation(xn[:, tt, :], x[:, tt, :], ACT.Identity, bias=0.0,
                               scale=S("r4", TT)[:, tt:tt + 1]).then_inc(s["x2n"], 1)
            act.wait_ge(s["lg_r"], 1)
            for tt in range(TT):
                act.activation(R("gexp", TT, G)[:, tt, :], R("lg", TT, 36)[:, tt, 0:G], ACT.Exp,
                               bias=R("ngmax", TT)[:, tt:tt + 1],
                               accum_out=R("gsum", TT)[:, tt:tt + 1]).then_inc(s["rexp"], 1)
            act.wait_ge(s["lg_r"], 2)
            act.activation(R("e2", TT), R("dv", TT), ACT.Exp).then_inc(s["rexp"], 1)


            def gather_half(b, half, count):
                act.wait_ge(s["g_full"], count)
                for j in range(4):
                    k = 4 * half + j
                    ins = act.activation(xg[:, b, k, :], token_bank[:, j * P:(j + 1) * P], ACT.Identity,
                                         bias=S("B2", KD)[:, k:k + 1], scale=S("A2", KD)[:, k:k + 1])
                ins.then_inc(s["g_evac"], 1)

            def quad(it, b):
                act.wait_ge(used, it * QU + UP_UNITS)
                act.activation(sig, up_bank[:, 0:F], ACT.Sigmoid).then_inc(s["sig_r"], 1)
                gather_half(1 - b, 0, it * 2 + 3)
                gather_half(1 - b, 1, it * 2 + 4)
                act.wait_ge(used, it * QU + QU)
                act.wait_ge(s["scat"], it + 1)
                act.activation(outs2[:, 0:512], out_banks[0][:], ACT.Copy).then_inc(s["o_act"], 1)

            gather_half(0, 0, 1)
            gather_half(0, 1, 2)
            with act.Fori(0, NQ // 2) as i:
                for b in range(2):
                    quad(i * 2 + b, b)
            act.wait_ge(s["flag_r"], 1)
            over = act.value_load(flag[0:1, 0:1], min_val=0, max_val=1)
            with act.If(over > 0):
                with act.Fori(1, PASSES) as p:
                    with act.Fori(0, NQ // 2) as i:
                        for b in range(2):
                            quad(p * NQ + i * 2 + b, b)
            act.activation(S("one_k", 1), ones[:, 0:1], ACT.Copy).then_inc(s["act_end"], 1)

            for tt in range(TT):
                act.wait_ge(s["x3"], 2 * tt + 2)
                act.activation(junk[:, tt * D:(tt + 1) * D], x[:, tt, :], ACT.Square,
                               accum_out=S("ms5", TT)[:, tt:tt + 1]).then_inc(s["sq5"], 1)
            act.wait_ge(s["var5"], 1)
            act.activation(S("std5", TT), S("var5", TT), ACT.Sqrt).then_inc(s["std5"], 1)

        @block.vector
        def _(dve):
            chain = [0]

            def link(ins):
                chain[0] += 1
                ins.then_inc(dve_chain, 1)
                dve.wait_ge(dve_chain, chain[0])

            def own(ins, name, n):
                ins.then_inc(s[name], 1)
                dve.wait_ge(s[name], n)

            def rows(i):
                dve.wait_ge(*full(f"ada{i}"))
                if i >= 2:
                    last = {2: "adaT0", 3: "adaT1", 4: "gt1b1", 5: "adaT3"}[i]
                    dve.wait_ge(*full(last))
                release(dve.tensor_copy(arow[:, i % 2, :], pb(f"ada{i}")[:, 0:256]), f"ada{i}")

            def columns(dst, i):
                dve.wait_ge(*full(f"adaT{i}"))
                turned = pb(f"adaT{i}")[:, 0:256].rearrange("p (j u r) -> p u j r", j=2, u=4)[:, :, :, 0]
                release(dve.tensor_tensor(dst.rearrange("p (u j) -> p u j", u=4), turned,
                                          col("b_ada", 8 * i, 8).rearrange("p (u j) -> p u j", u=4), ALU.add),
                        f"adaT{i}")
                dve.wait_ge(*free(f"adaT{i}"))

            def spread(dst, g):
                for i in range(2):
                    job, sl = f"gt{g}b{i}", slice(512 * i, 512 * i + 512)
                    dve.wait_ge(*full(job))
                    release(dve.tensor_tensor(dst[:, sl], pb(job)[:], dst[:, sl], ALU.add), job)

            dve.wait_ge(s["sq"], 2)
            dve.tensor_scalar(S("var1", TT), S("ms1", TT), 1.0 / D, EPS, ALU.mult, ALU.add).then_inc(s["var"], 1)
            dve.wait_ge(s["std"], 1)
            link(dve.reciprocal(S("r1", TT), S("std1", TT)))
            for tt in range(TT):
                dve.tensor_scalar(xn[:, tt, :], x[:, tt, :], S("r1", TT)[:, tt:tt + 1], None,
                                  ALU.mult).then_inc(s["xn_r"], 1)
            dve.wait_ge(*full("vT"))
            release(dve.tensor_copy(cols[:], pb("vT")[:, 0:NROWS]), "vT")
            dve.wait_ge(*free("vT"))
            dve.tensor_scalar(S("dgain", 1), col("diff_norm"), 1.0 - LAMBDA_INIT, None, ALU.mult).then_inc(s["cols_r"], 1)
            rows(0)
            m1 = S("m1", 16)
            columns(m1[:, 0:8], 0)
            dve.tensor_copy(S("B1", KD), m1[:, 0:8]).then_inc(s["mod1"], 1)
            dve.wait_ge(s["if_hi"], 1)
            dve.tensor_tensor(w_if_lo[:], w_if[:], w_if_hi[:].bitcast(F32), ALU.subtract).then_inc(s["if_hi"], 1)
            dve.wait_ge(bc_in, 112)
            for i in range(2):
                ins = dve.tensor_tensor_reduce(lamv[:, 2 * i, :], lamv[:, 2 * i, :], lamv[:, 2 * i + 1, :], 1.0, 0.0,
                                               ALU.mult, ALU.add, S("ldot", 2)[:, i:i + 1])
            ins.then_inc(s["lam_e"], 1)
            rows(1)
            columns(m1[:, 8:16], 1)
            dve.scalar_tensor_tensor(out=S("A1", KD), in0=m1[:, 8:16], scalar=1.0, in1=col("norm1", 0, 8),
                                     op0=ALU.add, op1=ALU.mult).then_inc(s["mod1"], 1)
            dve.wait_ge(s["mod1"], 2)
            for i in range(2, 4):
                dve.wait_ge(*full(f"xT{i}"))
                for dst in (hT_hi, hT):
                    for j in range(2):
                        k = 2 * i + j
                        ins = dve.tensor_scalar(dst[:, k, :], pb(f"xT{i}")[:, j * T:(j + 1) * T], S("A1", KD)[:, k:k + 1],
                                                S("B1", KD)[:, k:k + 1], ALU.mult, ALU.add)
                release(ins, f"xT{i}")
            dve.wait_ge(*free("xT3"))
            dve.tensor_tensor(hT_lo[:, 4:8, :], hT[:, 4:8, :], hT_hi[:, 4:8, :].bitcast(F32),
                              ALU.subtract).then_inc(s["h_lo"], 1)
            dve.wait_ge(s["lexp"], 1)
            link(dve.tensor_tensor(S("nlam", 1), S("lexp", 2)[:, 1:2], S("lexp", 2)[:, 0:1], ALU.subtract))
            link(dve.tensor_scalar(S("nlam2", 1), S("nlam", 1), -LAMBDA_INIT, None, ALU.add))
            dve.wait_ge(*full("if"))
            dve.tensor_scalar(grow[0:4, 0, :], pb("if")[0:4, 0:T], S("b_if", 2)[0:4, 0:1], None, ALU.add)
            release(dve.tensor_scalar(grow[0:4, 1, :], pb("if")[0:4, T:2 * T], S("b_if", 2)[0:4, 1:2], None, ALU.add), "if")
            dve.wait_ge(*free("if"))
            link(dve.tensor_scalar(grow[0:4, 3, :], grow[0:4, 1, :], -1.0, None, ALU.mult))
            own(dve.tensor_tensor(grow[0:4, 2, :], grow[0:4, 3, :], grow[0:4, 1, :], ALU.min), "gates", 1)
            own(dve.tensor_scalar(grow[0:4, 3, :], grow[0:4, 1, :], 0.0, None, ALU.min), "gates", 2)
            for i in range(2):
                dve.wait_ge(*full(f"v{i}"))
                release(dve.tensor_copy(v[:, :, 256 * i:256 * i + 256],
                                        pb(f"v{i}")[:].rearrange("p (t n) -> p t n", t=2)), f"v{i}")
            dve.wait_ge(*free("v1"))
            dve.wait_ge(const2_in, 16)
            dve.wait_ge(s["gln"], 1)
            link(dve.tensor_tensor(grow[0:4, 3, :], grow[0:4, 3, :], grow[0:4, 2, :], ALU.subtract))
            link(dve.tensor_tensor_scan(grow[0:4, 1, :], ones[0:4, 0:1].to_broadcast([4, T]), grow[0:4, 3, :], 0.0, ALU.mult, ALU.add))
            link(dve.tensor_tensor(grow[0:4, 2, :], grow[0:4, 0, :], grow[0:4, 1, :], ALU.subtract))
            link(dve.tensor_tensor_scan(grow[0:4, 3, :], K("mask")[0:4, P:P + 1].to_broadcast([4, T]), grow[0:4, 2, :], 0.0, ALU.add, ALU.max))
            dve.scalar_tensor_tensor(out=grow[0:4, 0, :], in0=grow[0:4, 1, :], scalar=-1.0, in1=grow[0:4, 3, :],
                                     op0=ALU.mult, op1=ALU.subtract).then_inc(s["grows"], 1)

            def scores(h):
                if h >= 2:
                    dve.wait_ge(s["a_r"], 2 * h - 2)
                for c in range(2):
                    job = f"s{2 * h + c}"
                    dve.wait_ge(*full(job))
                    release(dve.scalar_tensor_tensor(out=sc[:, h % 2, c, :], in0=pb(job)[:, 0:384], scalar=DA_HD ** -0.5,
                                                     in1=K("alibi")[:, h, :], op0=ALU.mult, op1=ALU.add), job)
                    dve.wait_ge(*free(job))
                    dve.tensor_reduce(S(f"nmx{h % 2}", 4)[:, 2 * c:2 * c + 1], sc[:, h % 2, c, 0:P], AX.X, ALU.max, negate=True)
                    dve.tensor_reduce(S(f"nmx{h % 2}", 4)[:, 2 * c + 1:2 * c + 2], sc[:, h % 2, c, P:384], AX.X, ALU.max,
                                      negate=True).then_inc(s["smax"], 1)

            def combine(h):
                dve.wait_ge(s["pexp"], 2 * h + 2)
                link(dve.reciprocal(S(f"rZ{h % 2}", 4), S(f"Z{h % 2}", 4)))
                link(dve.tensor_scalar(S("rZl", 2), S(f"rZ{h % 2}", 4)[:, 2:4], S("nlam2", 1), None, ALU.mult))
                for i, (a, b) in enumerate(((0, P), (P, 384))):
                    link(dve.tensor_scalar(a_sb[:, h, a:b], sc[:, h % 2, 1, a:b], S("rZl", 2)[:, i:i + 1], None,
                                           ALU.mult))
                    dve.scalar_tensor_tensor(out=a_sb[:, h, a:b], in0=sc[:, h % 2, 0, a:b],
                                             scalar=S(f"rZ{h % 2}", 4)[:, i:i + 1], in1=a_sb[:, h, a:b],
                                             op0=ALU.mult, op1=ALU.add).then_inc(s["a_r"], 1)

            def conv(i):
                dve.wait_ge(*free(f"ml{i}"))
                for k in (2 * i, 2 * i + 1):
                    link(dve.tensor_scalar(mqk[:, k, :], raw[:, k, 3:T + 3], col("conv_w", 24 + k), col("conv_b", k),
                                           ALU.mult, ALU.add))
                    for j in range(3):
                        ins = dve.scalar_tensor_tensor(out=mqk[:, k, :], in0=raw[:, k, j:j + T],
                                                       scalar=col("conv_w", 8 * j + k), in1=mqk[:, k, :],
                                                       op0=ALU.mult, op1=ALU.add)
                        if j < 2:
                            link(ins)
                    if k % 2 == 0:
                        link(ins)
                ins.then_inc(s["conv_out"], 1)

            scores(0)
            scores(1)
            combine(0)
            scores(2)
            combine(1)
            scores(3)
            conv(0)
            combine(2)
            conv(1)
            combine(3)
            conv(2)
            dve.wait_ge(*full("cols"))
            release(dve.tensor_copy(S("ccol", 16), pb("cols")[:, 0:16]), "cols")

            def decay_arg(h):
                job = f"Mb{h // 2}"
                dve.wait_ge(*full(job))
                m = pb(job)[:, (h % 2) * T:(h % 2) * T + T]
                dve.tensor_tensor(wts[h][:, 0:T], K("mask")[:, 0:T], m, ALU.subtract)
                ins = dve.tensor_tensor(wts[h][:, T:384], K("mask")[:, T:384], m[:, P:T], ALU.subtract)
                if h % 2:
                    release(ins, job)
                else:
                    ins.then_inc(s["warg"], 1)

            for h in range(HEADS):
                decay_arg(h)
            conv(3)
            dve.wait_ge(s["h_sq"], 1)
            dve.tensor_scalar(S("var2", 8), S("ms2", 8), 1.0 / P, EPS, ALU.mult, ALU.add).then_inc(s["var2"], 1)
            dve.wait_ge(s["std2"], 1)
            link(dve.reciprocal(S("r2", 8), S("std2", 8)))
            for tt in range(TT):
                release(dve.tensor_tensor(o[:, tt, :].rearrange("p (h n) -> p h n", h=4),
                                          pb(f"o{tt}")[:].rearrange("p (h n) -> p h n", h=4),
                                          S("r2", 8)[:, 4 * tt:4 * tt + 4].unsqueeze(2).to_broadcast([P, 4, P]),
                                          ALU.mult), f"o{tt}")

            def decay(h):
                dve.wait_ge(s["wexp"], h + 1)
                job = f"ms{h}"
                dve.wait_ge(*full(job))
                release(dve.scalar_tensor_tensor(out=wts[h], in0=pb(job)[:, 0:384], scalar=P ** -0.5,
                                                 in1=wts[h], op0=ALU.mult, op1=ALU.mult), job)

            def hidden(h):
                job = f"num{h}"
                dve.wait_ge(*full(job))
                dve.wait_ge(s["emn"], 1)
                nd = pb(job)[:, 0:2 * (P + 1)].rearrange("p (t n) -> p t n", t=2)
                den, em = nd[:, :, P:P + 1], S("emn", 8).rearrange("p (t n) -> p t n", t=2)[:, :, h:h + 1]
                d1, d2 = (S(n, 2).rearrange("p (t n) -> p t n", t=2) for n in ("d1", "d2"))
                link(dve.scalar_tensor_tensor(out=d1, in0=den, scalar=-1.0, in1=em, op0=ALU.mult, op1=ALU.max))
                link(dve.tensor_tensor(d2, den, d1, ALU.max))
                link(dve.reciprocal(S("rd", 2), S("d2", 2)))
                for tt in range(TT):
                    ins = dve.scalar_tensor_tensor(out=osig[:, tt, h * P:(h + 1) * P], in0=nd[:, tt, 0:P],
                                                   scalar=S("rd", 2)[:, tt:tt + 1], in1=osig[:, tt, h * P:(h + 1) * P],
                                                   op0=ALU.mult, op1=ALU.mult)
                release(ins, job)

            decay(0)
            decay(1)
            hidden(0)
            decay(2)
            hidden(1)
            decay(3)
            hidden(2)
            hidden(3)
            dve.wait_ge(s["h_sq"], 2)
            dve.tensor_scalar(S("var3", 8), S("ms3", 8), 1.0 / P, EPS, ALU.mult, ALU.add).then_inc(s["var3"], 1)
            dve.wait_ge(s["std3"], 1)
            link(dve.reciprocal(S("r3", 8), S("std3", 8)))
            for tt in range(TT):
                view = osig[:, tt, :].rearrange("p (h n) -> p h n", h=4)
                dve.tensor_tensor(view, view, S("r3", 8)[:, 4 * tt:4 * tt + 4].unsqueeze(2).to_broadcast([P, 4, P]),
                                  ALU.mult).then_inc(s["hn_r"], 1)

            def y_low(name, i):
                dve.wait_ge(*free(f"y{name}T{i}"))
                a = 2 * i + (4 if name == "m" else 0)
                dve.tensor_tensor(yT_lo[:, a:a + 2, :], yT[:, a:a + 2, :], yT_hi[:, a:a + 2, :].bitcast(F32),
                                  ALU.subtract).then_inc(s["y_lo"], 1)

            for name in ("a", "m"):
                for i in range(2):
                    y_low(name, i)
            rows(2)
            rows(3)
            dve.wait_ge(gt1_in, 16)
            spread(gt1b, 1)
            B2, A2 = S("B2", KD), S("A2", KD)
            columns(B2, 3)
            dve.tensor_copy(S("B2_r", KD), B2).then_inc(s["mod2"], 1)
            for i in range(4):
                job, view = f"bra{i}", ga[:, 2 * i:2 * i + 2, :]
                dve.wait_ge(*free(f"ga{i}"))
                dve.wait_ge(*full(job))
                release(dve.tensor_tensor(view, pb(job)[:].rearrange("p (a n) -> p a n", a=2), view, ALU.mult), job)

            def merged_low(i):
                two = slice(2 * i, 2 * i + 2)
                dve.wait_ge(s["m_hi"], i + 1)
                dve.tensor_tensor(merged_lo[:, two, :], ga[:, two, :], merged_hi[:, two, :].bitcast(F32),
                                  ALU.subtract).then_inc(s["m_lo"], 1)

            for i in range(4):
                job, view, va = f"brm{i}", gm2[:, 2 * i:2 * i + 2, :], ga[:, 2 * i:2 * i + 2, :]
                dve.wait_ge(*free(f"gm{i}"))
                dve.wait_ge(*full(job))
                release(dve.tensor_tensor(view, pb(job)[:].rearrange("p (a n) -> p a n", a=2), view, ALU.mult), job)
                dve.wait_ge(*free(job))
                own(dve.tensor_tensor(va, va, view, ALU.add), "merged", i + 1)
                if i:
                    merged_low(i - 1)
            merged_low(3)

            def residual(i):
                dve.wait_ge(*full(f"wo{i}"))
                if i >= 1:
                    dve.wait_ge(s["x2"], i)
                g = gt1b[:, 256 * i:256 * i + 256].unsqueeze(1).to_broadcast([P, TT, 256])
                tv = tmp[:, 0, :].rearrange("p (t n) -> p t n", t=2)
                release(dve.tensor_tensor(tv, pb(f"wo{i}")[:].rearrange("p (t n) -> p t n", t=2), g, ALU.mult), f"wo{i}")
                dve.wait_ge(*free(f"wo{i}"))
                xv = x[:, :, 256 * i:256 * i + 256]
                own(dve.tensor_tensor(xv, xv, tv, ALU.add), "x2", i + 1)

            rows(4)
            residual(0)
            columns(A2, 4)
            own(dve.scalar_tensor_tensor(out=A2, in0=A2, scalar=1.0, in1=col("norm2", 0, 8),
                                         op0=ALU.add, op1=ALU.mult), "mod2", 2)
            residual(1)
            dve.wait_ge(wr_in, 64)
            dve.wait_ge(*full("rb"))
            release(dve.tensor_tensor(rbias[:], pb("rb")[:, 0:G + NE], b_r[:], ALU.add), "rb")
            dve.wait_ge(*free("rb"))
            for k in range(KD):
                dve.tensor_scalar(w_r[:, k, :], w_r[:, k, :], A2[:, k:k + 1], None, ALU.mult).then_inc(s["wr_r"], 1)
            residual(2)
            residual(3)
            dve.memset(ptg[:, 1], 0.0).then_inc(s["pt_evac"], 1)
            dve.memset(outs2[:, 512:1024], 0.0).then_inc(s["o_dve"], 1)
            dve.memset(hid, 0.0).then_inc(s["hid_done"], 1)
            dve.wait_ge(s["sq2"], 1)
            link(dve.tensor_reduce(S("ms4s", TT), S("ms4", 8).rearrange("p (i t) -> p t i", t=TT), AX.X, ALU.add))
            dve.tensor_scalar(S("var4", TT), S("ms4s", TT), 1.0 / D, EPS, ALU.mult, ALU.add).then_inc(s["var4"], 1)
            dve.wait_ge(s["std4"], 1)
            own(dve.reciprocal(S("r4", TT), S("std4", TT)), "r4", 1)

            lg, g8 = R("lg", TT, 36), R("g8", TT, 8)
            link(dve.memset(g8, -3.0e38))
            dve.wait_ge(*full("lg"))
            release(dve.tensor_tensor(lg, pb("lg")[:, 0:72].rearrange("p (t n) -> p t n", t=2),
                                      S("r4", TT).unsqueeze(2).to_broadcast([P, TT, 36]), ALU.mult), "lg")
            dve.wait_ge(*free("lg"))
            link(dve.tensor_tensor(lg, lg, rbias[:].unsqueeze(1).to_broadcast([P, TT, 36]), ALU.add))
            link(dve.tensor_copy(g8[:, :, 0:G], lg[:, :, 0:G]))
            g_top, e_top, esel = R("g_top", TT, 8), R("e_top", TT, 8), R("esel", TT, 8)
            for tt in range(TT):
                ins = dve.max(g_top[:, tt, :], g8[:, tt, :])
            link(ins)
            dve.tensor_scalar(R("ngmax", TT).unsqueeze(2), g_top[:, :, 0:1], -1.0, None, ALU.mult).then_inc(s["lg_r"], 1)
            for tt in range(TT):
                ins = dve.max_index(idx[:, 0, tt, :], g_top[:, tt, :], g8[:, tt, :])
            link(ins)
            gi, ei = R("gi", TT, 8), R("ei", TT, 8)
            link(dve.tensor_copy(gi, idx[:, 0]))
            ohg = R("ohg", TT, G)
            iota8 = K("iota8")
            link(dve.tensor_tensor(ohg, iota8[:, :, 0:G], gi[:, :, 0:1].to_broadcast([P, TT, G]), ALU.is_equal))
            prod = R("prod", TT, G, E)
            e_lg = lg[:, :, G:G + NE].rearrange("p t (g e) -> p t g e", g=G)
            link(dve.tensor_tensor(prod, e_lg, ohg.unsqueeze(3).to_broadcast([P, TT, G, E]), ALU.mult))
            link(dve.tensor_reduce(esel, prod.rearrange("p t g e -> p t e g"), AX.X, ALU.add))
            for tt in range(TT):
                ins = dve.max(e_top[:, tt, :], esel[:, tt, :])
            link(ins)
            own(dve.tensor_tensor(R("dv", TT).unsqueeze(2), e_top[:, :, 1:2], e_top[:, :, 0:1], ALU.subtract), "lg_r", 2)
            for tt in range(TT):
                ins = dve.max_index(idx[:, 1, tt, :], e_top[:, tt, :], esel[:, tt, :])
            link(ins)
            link(dve.tensor_copy(ei, idx[:, 1]))
            oh1, oh2 = R("oh1", TT, E), R("oh2", TT, E)
            dve.tensor_tensor(oh1, iota8, ei[:, :, 0:1].to_broadcast([P, TT, E]), ALU.is_equal)
            link(dve.tensor_tensor(oh2, iota8, ei[:, :, 1:2].to_broadcast([P, TT, E]), ALU.is_equal))
            m8 = R("m8", TT, E)
            link(dve.tensor_tensor(m8, oh1, oh2, ALU.add))
            mask = R("mask", TT, NE)
            own(dve.tensor_tensor(mask.rearrange("p t (g e) -> p t g e", g=G),
                                  ohg.unsqueeze(3).to_broadcast([P, TT, G, E]),
                                  m8.unsqueeze(2).to_broadcast([P, TT, G, E]), ALU.mult), "mask_r", 1)
            rows(5)
            NX = NE + QUAD
            gate, rank = R("gate", TT, NX), R("rank", TT, NX)
            dve.wait_ge(*full("rank"))
            link(dve.scalar_tensor_tensor(out=rank[:, :, 0:NE], in0=pb("rank")[:, 0:2 * NE].rearrange("p (t n) -> p t n", t=2),
                                          scalar=1.0, in1=mask, op0=ALU.add, op1=ALU.mult))
            link(dve.tensor_scalar(rank[:, :, 0:NE], rank[:, :, 0:NE], -1.0, None, ALU.add))
            dve.tensor_tensor(pone[:], K("slot"), rank[:, :, 0:QUAD].unsqueeze(3).to_broadcast([P, TT, QUAD, CAP]),
                              ALU.is_equal).then_inc(s["moe_chain"], 1)
            link(dve.tensor_scalar(rank[:, :, NE:NX], rank[:, :, 0:QUAD], -float(CAP), None, ALU.add))
            dve.wait_ge(s["rexp"], 3)
            den = R("den", TT)
            link(dve.tensor_scalar(den, R("e2", TT), 1.0, None, ALU.add))
            link(dve.tensor_tensor(den, den, R("gsum", TT), ALU.mult))
            w1, w2 = R("w1", TT), R("w2", TT)
            link(dve.reciprocal(w1, den))
            link(dve.tensor_tensor(w2, w1, R("e2", TT), ALU.mult))
            we = R("we", TT, E)
            dve.tensor_tensor(oh1, oh1, w1.unsqueeze(2).to_broadcast([P, TT, E]), ALU.mult)
            link(dve.tensor_tensor(oh2, oh2, w2.unsqueeze(2).to_broadcast([P, TT, E]), ALU.mult))
            link(dve.tensor_tensor(we, oh1, oh2, ALU.add))
            link(dve.tensor_tensor(R("g32", TT, NE).rearrange("p t (g e) -> p t g e", g=G),
                                   ohg.unsqueeze(3).to_broadcast([P, TT, G, E]),
                                   we.unsqueeze(2).to_broadcast([P, TT, G, E]), ALU.mult))
            link(dve.tensor_copy(gate[:, :, 0:NE], R("g32", TT, NE)))
            link(dve.tensor_copy(gate[:, :, NE:NX], gate[:, :, 0:QUAD]))
            dve.wait_ge(s["moe_chain"], 1)
            dve.tensor_tensor(pgate[:], pone[:], gate[:, :, 0:QUAD].unsqueeze(3).to_broadcast([P, TT, QUAD, CAP]),
                              ALU.mult).then_inc(s["pg_ready"], 1)
            release(dve.reduce_max(S("cmax", 1)[0:1, :], pb("rank")[0:1, 2 * NE:3 * NE], AX.X), "rank")
            dve.wait_ge(*free("rank"))
            dve.tensor_scalar(flag[0:1, :], S("cmax", 1)[0:1, :], CAP + 0.5, None, ALU.is_gt).then_inc(s["flag_r"], 1)
            dve.wait_ge(gt2_in, 16)
            spread(gt2b, 2)

            MC = 2

            def one_hot(at, base, c0):
                dve.tensor_tensor(pone[:], K("slot"), rank[:, :, at].unsqueeze(3).to_broadcast([P, TT, QUAD, CAP]),
                                  ALU.is_equal).then_inc(s["moe_chain"], 1)
                dve.wait_ge(s["moe_chain"], base + c0)
                dve.tensor_tensor(pgate[:], pone[:], gate[:, :, at].unsqueeze(3).to_broadcast([P, TT, QUAD, CAP]),
                                  ALU.mult).then_inc(s["pg_ready"], 1)

            def quad(q, it, b):
                dve.wait_ge(s["pt_full"], it + 1)
                one_hot(bass.ds(q * QUAD + QUAD, QUAD), it * MC, 2)
                dve.wait_ge(s["sig_r"], it + 1)
                dve.tensor_tensor(act_a, up_bank[:, 0:F], sig, ALU.mult).then_inc(s["moe_chain"], 1)
                dve.wait_ge(s["moe_chain"], it * MC + 3)
                dve.tensor_tensor(hid, up_bank[:, F:2 * F], act_a, ALU.mult).then_inc(s["hid_done"], 1)
                dve.wait_ge(s["pt_full"], it + 2)
                dve.tensor_copy(hidT.rearrange("p f n -> p (f n)"), token_bank[:, T:2 * T]).then_inc(s["hT_evac"], 1)
                dve.wait_ge(s["scat"], it + 1)
                dve.tensor_copy(ptg[:, 1 - b].rearrange("p t n -> p (t n)"), token_bank[:, 0:T]).then_inc(s["pt_evac"], 1)
                dve.wait_ge(used, it * QU + QU)
                dve.tensor_copy(outs2[:, 512:1024], out_banks[1][:]).then_inc(s["o_dve"], 1)

            dve.wait_ge(s["pt_full"], 1)
            dve.tensor_copy(ptg[:, 0].rearrange("p t n -> p (t n)"), token_bank[:, 0:T]).then_inc(s["pt_evac"], 1)
            with dve.Fori(0, NQ // 2) as i:
                for b in range(2):
                    quad(i * 2 + b, i * 2 + b, b)
            dve.wait_ge(s["flag_r"], 1)
            over = dve.value_load(flag[0:1, 0:1], min_val=0, max_val=1)
            with dve.If(over > 0):
                with dve.Fori(1, PASSES) as p:
                    dve.tensor_scalar(rank, rank, -float(CAP), None, ALU.add).then_inc(s["r_chain"], 1)
                    dve.wait_ge(s["r_chain"], p)
                    dve.tensor_copy(S("one_q", 1), ones[:, 0:1])
                    with dve.Fori(0, NQ // 2) as i:
                        for b in range(2):
                            quad(i * 2 + b, p * NQ + i * 2 + b, b)
            dve.tensor_copy(S("one_p", 1), ones[:, 0:1]).then_inc(s["dve_end"], 1)

            dve.wait_ge(s["y_full"], 1)
            for tt in range(TT):
                for c in range(2):
                    n = 2 * tt + c
                    sl = slice(512 * c, 512 * c + 512)
                    link(dve.tensor_tensor(tmp[:, n % 2, :], y_banks[n][:], gt2b[:, sl], ALU.mult))
                    own(dve.tensor_tensor(x[:, tt, sl], x[:, tt, sl], tmp[:, n % 2, :], ALU.add), "x3", n + 1)
            dve.wait_ge(s["sq5"], 2)
            dve.tensor_scalar(S("var5", TT), S("ms5", TT), 1.0 / D, EPS, ALU.mult, ALU.add).then_inc(s["var5"], 1)
            dve.wait_ge(s["std5"], 1)
            link(dve.reciprocal(S("r5", TT), S("std5", TT)))
            dve.wait_ge(nf_in, 16)
            for tt in range(TT):
                dve.scalar_tensor_tensor(out=x[:, tt, :], in0=x[:, tt, :], scalar=S("r5", TT)[:, tt:tt + 1], in1=nfb,
                                         op0=ALU.mult, op1=ALU.mult).then_inc(s["y_out"], 1)

        @block.tensor
        def _(pe):
            at = [0]

            def take(job):
                n = JOB[job]
                if n >= 8:
                    pe.wait_ge(bank_free[n % 8], n // 8)
                return bank[n % 8]

            def next_unit(k):
                n = at[0]
                at[0] += 1
                pe.wait_ge(landed[slot_of(n)], landed_value(n))
                return unit(n, k)

            def ada(i):
                ps = take(f"ada{i}")
                w = [next_unit(8) for _ in range(4)]
                for k in range(KD):
                    for u in range(4):
                        ins = pe.matmul(ps[32 * u:32 * u + 32, 0:256], S("cs", 8)[:, k:k + 1].to_broadcast([P, 32]),
                                        w[u][:, k, :], start=(k == 0), stop=(k == KD - 1), tile_position=(0, 32 * u))
                filled(ins, f"ada{i}")

            def ada_turn(i):
                ps = take(f"adaT{i}")
                pe.wait_ge(*free(f"ada{i}"))
                for j in range(2):
                    ins = pe.transpose(ps[:, j * P:(j + 1) * P], arow[:, i % 2, j * P:(j + 1) * P], ident)
                filled(ins, f"adaT{i}")

            def ada_spread(i, g, half):
                ps = take(f"gt{g}b{half}")
                pe.wait_ge(*free(f"ada{i}"))
                for j in range(2):
                    u = 2 * half + j
                    ins = pe.matmul(ps[:, j * 256:(j + 1) * 256], ident[:, 32 * u:32 * u + 1].to_broadcast([P, P]),
                                    arow[:, i % 2, :], start=True, stop=True)
                filled(ins, f"gt{g}b{half}")

            dense = [0]

            def next_dense(k):
                d = dense[0]
                dense[0] += 1
                n = DENSE[d]
                assert n == at[0]
                at[0] += 1
                pe.wait_ge(s["w_hi"], d + 1)
                return hi(d).rearrange("p (k n) -> p k n", k=k), \
                    ring_r[:, slot_of(n), :].rearrange("p (k n) -> p k n", k=k), ((s["w_lo"], d + 1),)

            def product(out, a, b, nk):
                passes = ((a[0], b[0]), (a[1], b[0]), (a[0], b[1]))
                for i, (left, right) in enumerate(passes):
                    if i == 1:
                        for needed in a[2]:
                            pe.wait_ge(*needed)
                    if i == 2:
                        for needed in b[2]:
                            pe.wait_ge(*needed)
                    for k in range(nk):
                        ins = pe.matmul(out, left(k), right(k), start=(i == 0 and k == 0), stop=(i == 2 and k == nk - 1))
                return ins

            def proj_T(job, src, w, j0=0, nk=KD):
                ps = take(job)
                for j in range(2):
                    c = slice((j0 + j) * P, (j0 + j + 1) * P)
                    ins = product(ps[:, j * T:(j + 1) * T], (lambda k: w[0][:, k, c], lambda k: w[1][:, k, c], w[2]), src, nk)
                filled(ins, job)

            def proj(job, src, w):
                ps = take(job)
                for tt in range(TT):
                    c = slice(tt * P, (tt + 1) * P)
                    ins = product(ps[:, tt * 256:(tt + 1) * 256],
                                  (lambda k: src[0](k)[:, c], lambda k: src[1](k)[:, c], src[2]),
                                  (lambda k: w[0][:, k, :], lambda k: w[1][:, k, :], w[2]), KD)
                filled(ins, job)

            hsrc = (lambda k: hT_hi[:, k, :], lambda k: hT_lo[:, k, :],
                    ((s["h_lo"], 1), (s["h_lo_pool"], 1)))

            pe.wait_ge(const_in, 16)
            pe.wait_ge(c_in, 16)
            filled(pe.transpose(take("cT")[:, 0:8], vrows[0:8, :], ident[0:8, 0:8]), "cT")
            pe.wait_ge(*free("cT"))
            ada(0)
            pe.wait_ge(vec_in, 112)
            filled(pe.transpose(take("vT")[:, 0:NROWS], vrows[0:NROWS, :], ident[0:NROWS, 0:NROWS]), "vT")
            pe.wait_ge(s["xn_r"], 2)
            for i in range(4):
                ps = take(f"xT{i}")
                for j in range(2):
                    for tt in range(TT):
                        k = 2 * i + j
                        ins = pe.transpose(ps[:, j * T + tt * P:j * T + (tt + 1) * P], xn[:, tt, k * P:(k + 1) * P], ident)
                filled(ins, f"xT{i}")
            ada_turn(0)
            ada(1)
            ada_turn(1)
            ps = take("if")
            pe.wait_ge(s["if_hi"], 2)
            for i in range(4):
                pe.wait_ge(*free(f"xT{i}"))
            for g in range(2):
                c = slice(4 * g, 4 * g + 4)
                ins = product(ps[0:4, g * T:(g + 1) * T],
                              (lambda k: w_if_hi[:, k, c], lambda k: w_if_lo[:, k, c], ((s["if_hi"], 2),)), hsrc, KD)
            filled(ins, "if")
            for i in range(4):
                proj_T(f"qk{i}", hsrc, next_dense(8))
            for i in range(2):
                proj(f"v{i}", hsrc, next_dense(8))
            for i in range(4):
                pe.wait_ge(*free(f"qk{i}"))
            for h in range(HEADS):
                for c in range(2):
                    ps = take(f"s{2 * h + c}")
                    r = slice(64 * c, 64 * c + 64)
                    pe.matmul(ps[:, 0:P], qkT[r, h, 0:P], qkT[r, 4 + h, 0:P], start=True, stop=True)
                    filled(pe.matmul(ps[:, P:384], qkT[r, h, P:T], qkT[r, 4 + h, :], start=True, stop=True),
                           f"s{2 * h + c}")
            for i in range(4):
                proj_T(f"ml{i}", hsrc, next_dense(8))
            ps = take("cols")
            pe.wait_ge(s["grows"], 1)
            pe.wait_ge(const2_in, 16)
            for j, row in enumerate((2, 0)):
                for tt in range(TT):
                    ins = pe.transpose(ps[:, 8 * j + 4 * tt:8 * j + 4 * tt + 4], grow[0:4, row, tt * P:(tt + 1) * P],
                                       ident[0:4, 0:4])
            filled(ins, "cols")
            for i in range(2):
                ps = take(f"Mb{i}")
                for j in range(2):
                    ins = pe.matmul(ps[:, j * T:(j + 1) * T], ident[0:4, 2 * i + j:2 * i + j + 1].to_broadcast([4, P]), grow[0:4, 3, :],
                                    start=True, stop=True)
                filled(ins, f"Mb{i}")
            for i in range(2):
                proj(f"mv{i}", hsrc, next_dense(8))
            pe.wait_ge(*free("v0"))
            pe.wait_ge(*free("v1"))

            def transpose_a(h):
                ps = take(f"aT{h}")
                pe.wait_ge(s["a_r"], 2 * h + 2)
                for j in range(3):
                    ins = pe.transpose(ps[:, j * P:(j + 1) * P], a_sb[:, h, j * P:(j + 1) * P], ident)
                filled(ins, f"aT{h}")

            def times_v(h):
                pe.wait_ge(*free(f"aT{h}"))
                hs = slice(h * P, (h + 1) * P)
                ins = pe.matmul(po[0][:, hs], aT[:, h % 2, 0:P], v[:, 0, hs], start=True, stop=True)
                if h == 3:
                    filled(ins, "o0")
                pe.matmul(po[1][:, hs], aT[:, h % 2, P:2 * P], v[:, 0, hs], start=True, stop=False)
                ins = pe.matmul(po[1][:, hs], aT[:, h % 2, 2 * P:384], v[:, 1, hs], start=False, stop=True)
                if h < 3:
                    ins.then_inc(s["pv"], 1)
                else:
                    filled(ins, "o1")

            transpose_a(0)
            transpose_a(1)
            po = [take("o0"), take("o1")]
            times_v(0)
            proj("mo0", hsrc, next_dense(8))
            transpose_a(2)
            times_v(1)
            transpose_a(3)
            times_v(2)
            proj("mo1", hsrc, next_dense(8))
            times_v(3)
            def mscores(h):
                ps = take(f"ms{h}")
                pe.wait_ge(s["mqk_r"], 4)
                pe.matmul(ps[:, 0:T], mqk[:, 4 + h, 0:P], mqk[:, h, :], start=True, stop=True)
                filled(pe.matmul(ps[:, T:384], mqk[:, 4 + h, P:T], mqk[:, h, P:T], start=True, stop=True), f"ms{h}")

            def numerator(h):
                ps = take(f"num{h}")
                pe.wait_ge(*free(f"ms{h}"))
                pe.wait_ge(*free("mv0"))
                pe.wait_ge(*free("mv1"))
                n = P + 1
                pe.matmul(ps[:, 0:n], wts[h][:, 0:P], vaug[:, 0, h, :], start=True, stop=True)
                pe.matmul(ps[:, n:2 * n], wts[h][:, P:T], vaug[:, 0, h, :], start=True, stop=False)
                filled(pe.matmul(ps[:, n:2 * n], wts[h][:, T:384], vaug[:, 1, h, :], start=False, stop=True),
                       f"num{h}")

            def gate_a(i):
                proj_T(f"ga{i}", hsrc, next_dense(8))

            gate_a(0)
            gate_a(1)
            mscores(0)
            mscores(1)
            gate_a(2)
            numerator(0)
            mscores(2)
            numerator(1)
            mscores(3)
            gate_a(3)
            numerator(2)
            numerator(3)
            for i in range(2):
                ps = take(f"yaT{i}")
                pe.wait_ge(*free("o0"))
                pe.wait_ge(*free("o1"))
                for j in range(2):
                    for tt in range(TT):
                        h = 2 * i + j
                        ins = pe.transpose(ps[:, j * T + tt * P:j * T + (tt + 1) * P], o[:, tt, h * P:(h + 1) * P], ident)
                filled(ins, f"yaT{i}")
            for i in range(4):
                proj_T(f"gm{i}", hsrc, next_dense(8))
            for i in range(2):
                ps = take(f"ymT{i}")
                pe.wait_ge(s["hn_r"], 2)
                for j in range(2):
                    for tt in range(TT):
                        h = 2 * i + j
                        ins = pe.transpose(ps[:, j * T + tt * P:j * T + (tt + 1) * P], osig[:, tt, h * P:(h + 1) * P],
                                           ident)
                filled(ins, f"ymT{i}")
            ada(2)
            ada(3)
            ada_spread(2, 1, 0)
            ada_spread(2, 1, 1)
            ada_turn(3)
            for name, y0 in (("a", 0), ("m", 4)):
                low = (s["y_lo"], 2 if name == "a" else 4)
                pe.wait_ge(*low)
                src = (lambda k: yT_hi[:, y0 + k, :], lambda k: yT_lo[:, y0 + k, :], (low,))
                for u in range(2):
                    w = next_dense(4)
                    for i in range(2):
                        proj_T(f"br{name}{2 * u + i}", src, w, 2 * i, 4)
            ada(4)
            pe.wait_ge(s["m_hi"], 4)
            merged_src = (lambda k: merged_hi[:, k, :], lambda k: merged_lo[:, k, :], ((s["m_lo"], 4),))

            def out_proj(i):
                proj(f"wo{i}", merged_src, next_dense(8))

            def turn_x(i):
                ps = take(f"x2T{i}")
                pe.wait_ge(s["x2"], i + 1)
                for j in range(2):
                    for tt in range(TT):
                        k = 2 * i + j
                        ins = pe.transpose(ps[:, j * T + tt * P:j * T + (tt + 1) * P], x[:, tt, k * P:(k + 1) * P], ident)
                filled(ins, f"x2T{i}")

            out_proj(0)
            ada_turn(4)
            out_proj(1)
            ps = take("rb")
            pe.wait_ge(wr_in, 64)
            pe.wait_ge(s["mod2"], 1)
            for k in range(KD):
                ins = pe.matmul(ps[:, 0:G + NE], S("B2", KD)[:, k:k + 1].to_broadcast([P, P]), w_r[:, k, :],
                                start=(k == 0), stop=(k == KD - 1))
            filled(ins, "rb")
            out_proj(2)
            turn_x(0)
            out_proj(3)
            turn_x(1)
            pe.wait_ge(s["wr_r"], KD)
            ps = take("lg")

            def logits(tt, ks):
                for k in ks:
                    ins = pe.matmul(ps[:, tt * 36:(tt + 1) * 36], hT[:, k, tt * P:(tt + 1) * P], w_r[:, k, :],
                                    start=(k == 0), stop=(k == KD - 1))
                return ins

            pe.wait_ge(*free("x2T0"))
            pe.wait_ge(*free("x2T1"))
            logits(0, range(0, 4))
            turn_x(2)
            turn_x(3)
            pe.wait_ge(*free("x2T2"))
            pe.wait_ge(*free("x2T3"))
            logits(0, range(4, 8))
            ins = logits(1, range(0, 8))
            filled(ins, "lg")
            ada(5)
            for job in ("x2T1", "lg", "x2T2", "x2T3"):
                assert pb(job) in y_banks
                pe.wait_ge(*free(job))
            pe.wait_ge(s["pt_evac"], 1)
            zeros = ptg[:, 1].rearrange("p t n -> p (t n)").bitcast(BF16)
            for b in y_banks:
                pe.matmul(b[:], zeros[:, 0:P], zeros, start=True, stop=False, skip_group_check=True)
            ps = take("rank")
            pe.wait_ge(s["mask_r"], 1)
            m = R("mask", TT, NE)
            tri = K("tri")
            pe.matmul(ps[:, 0:NE], tri, m[:, 0, :], start=True, stop=True)
            pe.matmul(ps[:, NE:2 * NE], ones, m[:, 0, :], start=True, stop=False)
            pe.matmul(ps[:, NE:2 * NE], tri, m[:, 1, :], start=False, stop=True)
            pe.matmul(ps[0:1, 2 * NE:3 * NE], ones[:, 0:1], m[:, 0, :], start=True, stop=False)
            filled(pe.matmul(ps[0:1, 2 * NE:3 * NE], ones[:, 0:1], m[:, 1, :], start=False, stop=True), "rank")

            ada_spread(5, 2, 0)

            def scatter(b, stop):
                for tt in range(TT):
                    for c in range(2):
                        ins = pe.matmul(y_banks[2 * tt + c][:], ptg[:, b, tt, :], outs2[:, 512 * c:512 * c + 512],
                                        start=False, stop=stop, skip_group_check=True)
                return ins

            def gather(half):
                for j in range(4):
                    k = 4 * half + j
                    for tt in range(TT):
                        ins = pe.matmul(token_bank[:, j * P:(j + 1) * P], xn[:, tt, k * P:(k + 1) * P],
                                        pone[:, tt].rearrange("p a n -> p (a n)"), start=(tt == 0), stop=(tt == TT - 1))
                ins.then_inc(s["g_full"], 1)

            def turn(with_hidden):
                for tt in range(TT):
                    ins = pe.transpose(token_bank[:, tt * P:(tt + 1) * P], pgate[:, tt].rearrange("p a n -> p (a n)"), ident)
                if with_hidden:
                    for f in range(2):
                        ins = pe.transpose(token_bank[:, T + f * P:T + (f + 1) * P], hid[:, f * P:(f + 1) * P], ident)
                ins.then_inc(s["pt_full"], 1)

            def arrived(w, e, it):
                n = NPRE + QUAD_POS[(w, e)]
                pe.wait_ge(landed[slot_of(n)], it * 16 + landed_value(n))
                return unit(n, 2 if w == "w2" else 8)

            def up(it, b):
                for m_, w in enumerate(("w1", "w3")):
                    wt = [arrived(w, e, it) for e in range(QUAD)]
                    for k in range(KD):
                        for e in range(QUAD):
                            ins = pe.matmul(up_bank[e * CAP:(e + 1) * CAP, m_ * F:(m_ + 1) * F],
                                            xg[:, b, k, e * CAP:(e + 1) * CAP], wt[e][:, k, :],
                                            start=(k == 0), stop=(k == KD - 1), tile_position=(0, e * CAP))
                            if k == KD - 1:
                                ins.then_inc(used, 1)

            def down(it):
                wt = [arrived("w2", e, it) for e in range(QUAD)]
                for c in range(2):
                    for f in range(2):
                        for e in range(QUAD):
                            ins = pe.matmul(out_banks[c][e * CAP:(e + 1) * CAP, :], hidT[:, f, e * CAP:(e + 1) * CAP],
                                            wt[e][:, f, 512 * c:512 * c + 512], start=(f == 0), stop=(f == 1),
                                            tile_position=(0, e * CAP))
                            if c == 1 and f == 1:
                                ins.then_inc(used, 1)

            def quad(it, b):
                pe.wait_ge(s["g_evac"], it * 2 + 2)
                pe.wait_ge(s["hid_done"], it + 1)
                up(it, b)
                pe.wait_ge(s["pg_ready"], it + 2)
                pe.wait_ge(s["pt_evac"], it + 2)
                gather(0)
                pe.wait_ge(s["o_act"], it + 1)
                pe.wait_ge(s["o_dve"], it + 1)
                scatter(1 - b, False).then_inc(s["scat"], 1)
                pe.wait_ge(s["g_evac"], it * 2 + 3)
                gather(1)
                pe.wait_ge(s["g_evac"], it * 2 + 4)
                pe.wait_ge(s["hid_done"], it + 2)
                turn(True)
                pe.wait_ge(s["hT_evac"], it + 1)
                down(it)

            pe.wait_ge(s["moe_chain"], 1)
            pe.wait_ge(s["x2n"], 2)
            pe.wait_ge(*free("ada5"))
            gather(0)
            ada_spread(5, 2, 1)
            pe.wait_ge(s["g_evac"], 1)
            gather(1)
            pe.wait_ge(s["g_evac"], 2)
            pe.wait_ge(s["pg_ready"], 1)
            turn(False)
            pe.wait_ge(*free("rank"))
            pe.wait_ge(*free("gt2b0"))
            pe.wait_ge(*free("gt2b1"))
            pe.wait_ge(s["o_act"], 1)
            pe.wait_ge(s["o_dve"], 1)
            with pe.Fori(0, NQ // 2) as i:
                for b in range(2):
                    quad(i * 2 + b, b)
            pe.wait_ge(s["flag_r"], 1)
            over = pe.value_load(flag[0:1, 0:1], min_val=0, max_val=1)
            with pe.If(over > 0):
                with pe.Fori(1, PASSES) as p:
                    with pe.Fori(0, NQ // 2) as i:
                        for b in range(2):
                            quad(p * NQ + i * 2 + b, b)
            pe.wait_ge(s["act_end"], 1)
            pe.wait_ge(s["dve_end"], 1)
            scatter(1, True).then_inc(s["y_full"], 1)


_INS = ['x', 'c', 'w_ada', 'b_ada', 'norm1', 'w_in', 'b_if', 'conv_w', 'conv_b', 'lam_q1', 'lam_k1', 'lam_q2',
        'lam_k2', 'diff_norm', 'mlstm_norm', 'w_br_a', 'w_br_m', 'w_out', 'norm2', 'w_rg', 'b_rg', 'w_re', 'b_re',
        'w_e1', 'w_e3', 'w_e2', 'norm_f']


def kernel(**inputs):
    import concourse.bacc as bacc
    from concourse.bass_utils import run_bass_kernel_spmd

    nc = bacc.Bacc("TRN2", target_bir_lowering=False, num_devices=1)
    arrays, aps = {}, {}
    for name in _INS:
        a = np.ascontiguousarray(inputs[name])
        arrays[f"in_{name}"] = a
        aps[name] = nc.dram_tensor(f"in_{name}", a.shape, mybir.dt.from_np(a.dtype), kind="ExternalInput").ap()
    arrays["in_const"] = constants()
    aps["const"] = nc.dram_tensor("in_const", (P, NCONST), F32, kind="ExternalInput").ap()
    out = nc.dram_tensor("out_0", (1, T, D), F32, kind="ExternalOutput").ap()
    build(nc, aps, out)
    result = run_bass_kernel_spmd(nc, [arrays], core_ids=[0])
    return result.results[0]["out_0"]
```

```python
from contextlib import ExitStack

import numpy as np
import concourse.bass as bass
from concourse import mybir

F32 = mybir.dt.float32
F32R = mybir.dt.float32r
I32 = mybir.dt.int32
U32 = mybir.dt.uint32
ALU = mybir.AluOpType
ACT = mybir.ActivationFunctionType
AX = mybir.AxisListType

P = 128
D, T = 1024, 256
KD, TT = D // P, T // P
HEADS, DA_HD = 4, 64
EPS = 1e-6
G, E, F = 4, 8, 256
NE = G * E
QUAD = 4
NQ = NE // QUAD
CAP = P // QUAD
PASSES = T // CAP
LAMBDA_INIT = 0.8 - 0.6 * float(np.exp(-0.3 * 0))
NEG = -1.0e30
RING = 8
HI = 3
SLOTS = RING + HI + 1
UNIT = 2048

ROWS, NROWS = {}, 0
for _name, _n in (("c", 8), ("norm1", 8), ("norm2", 8), ("b_ada", 48), ("conv_w", 32),
                  ("conv_b", 8), ("diff_norm", 1), ("mlstm_norm", 1)):
    ROWS[_name] = (NROWS, NROWS + _n)
    NROWS += _n

C_Q, C_K, C_V, C_MQK, C_MV, C_MO, C_IF, C_GA, C_GM = 0, 512, 1024, 1536, 2560, 3072, 3584, 3592, 4616


def unit_list():
    def ada(i):
        return [("ada", (i, k)) for k in range(0, KD, 2)]

    def w_in(c0, n):
        return [("in", c0 + 256 * i) for i in range(n)]

    units = ada(0) + ada(1)
    units += w_in(C_Q, 2) + w_in(C_K, 2) + ada(3) + w_in(C_V, 2)
    units += w_in(C_MQK, 2) + ada(4) + w_in(C_MQK + 512, 2)
    units += w_in(C_MV, 2) + ada(2) + w_in(C_MO, 2) + w_in(C_GA, 4)
    units += w_in(C_GM, 4)
    units += [("br_a", 0), ("br_a", 512), ("br_m", 0), ("br_m", 512)] + ada(5)
    units += [("out", 256 * i) for i in range(4)]
    return units


def unit_jobs():
    jobs = ["ada0"] * 4 + ["ada1"] * 4 + [f"qk{i}" for i in range(4)] + ["ada3"] * 4 + ["v0", "v1"]
    jobs += ["ml0", "ml1"] + ["ada4"] * 4 + ["ml2", "ml3", "mv0", "mv1"] + ["ada2"] * 4 + ["mo0", "mo1"]
    jobs += [f"ga{i}" for i in range(4)] + [f"gm{i}" for i in range(4)]
    return jobs + ["bra1", "bra3", "brm1", "brm3"] + ["ada5"] * 4 + [f"wo{i}" for i in range(4)]


UNITS = unit_list()
NPRE = len(UNITS)
DENSE = [n for n, (kind, _) in enumerate(UNITS) if kind != "ada"]
QUAD_UNITS = [(w, e) for w in ("w1", "w3", "w2") for e in range(QUAD)]
UP_UNITS = 8
QU = len(QUAD_UNITS)
XSLOTS = SLOTS + 4
LOOP = 4
assert LOOP * QU % XSLOTS == 0 and NQ % LOOP == 0
TURNS = LOOP * QU // XSLOTS
QUAD_POS = {u: i for i, u in enumerate(QUAD_UNITS)}

JOBS = (["cT", "ada0", "vT"] + [f"xT{i}" for i in range(4)] + ["adaT0", "ada1", "adaT1", "if"]
        + ["qk0", "ifT", "qk1", "qk2", "qk3"]
        + ["ada3", "v0", "adaT3", "v1"] + [f"s{i}" for i in range(8)] + ["ml0", "ml1", "ada4", "ml2", "ml3", "adaT4"]
        + ["cols", "Mb0", "Mb1", "mv0", "aT0", "aT1", "mv1", "rb", "ada2", "o0", "o1", "aT2", "mo0", "aT3", "mo1"]
        + ["ga0", "ga1", "gt1b0", "gt1b1", "ms0", "ms1", "ga2", "num0", "ms2", "num1", "ms3", "ga3", "num2", "num3"]
        + ["yaT0", "yaT1"] + [f"gm{i}" for i in range(4)] + ["ymT0", "ymT1"]
        + [f"bra{i}" for i in range(4)] + [f"brm{i}" for i in range(4)]
        + ["ada5", "wo0", "wo1", "wo2", "x2T0", "x2T1", "wo3", "x2T2", "lgT", "x2T3", "lg", "gt2b0", "gt2b1", "rank"])
UNIT_JOB = unit_jobs()
DENSE_JOB = [UNIT_JOB[n] for n in DENSE]
JOB = {n: i for i, n in enumerate(JOBS)}

CONSTS, NCONST = {}, 0
for _name, _shape in (("ident", (P,)), ("ones", (P,)), ("tri", (P,)), ("alibi", (HEADS, 384)), ("mask", (384,)),
                      ("slot", (TT, QUAD, CAP)), ("iota8", (TT, 8))):
    CONSTS[_name] = (NCONST, _shape)
    NCONST += int(np.prod(_shape))


def constants():
    out = np.zeros((P, NCONST), np.float32)

    def put(name, value):
        c0, shape = CONSTS[name]
        out[:, c0:c0 + int(np.prod(shape))] = np.broadcast_to(value, (P,) + shape).reshape(P, -1)

    i = np.arange(P)
    put("ident", np.eye(P))
    put("ones", np.ones((P, P)))
    put("tri", (i[:, None] < i[None, :]) * 1.0)
    slopes = 2.0 ** (-8.0 * np.arange(1, HEADS + 1) / HEADS)
    dist = (P + i)[:, None] - np.arange(2 * P)[None, :]
    ali = np.where(dist >= 0, -slopes[:, None, None] * dist, NEG).transpose(1, 0, 2)
    put("alibi", np.concatenate([ali[:, :, P:], ali], axis=2))
    tri = np.where(i[None, :] >= i[:, None], 0.0, NEG)
    put("mask", np.concatenate([tri, np.zeros((P, P)), tri], axis=1))
    put("slot", np.arange(CAP)[None, None, None, :])
    put("iota8", np.arange(8)[None, None, :])
    return out


def build(nc, t, out):
    with ExitStack() as ctx:
        def sb(name, shape, dt=F32):
            return ctx.enter_context(nc.sbuf_tensor(name, [P] + list(shape), dt))

        def sem(name):
            return ctx.enter_context(nc.semaphore(name))

        def both(name, shape):
            with nc.sbuf_tensor(name + "_r", [P] + list(shape), F32R) as rounded:
                pass
            return sb(name, shape), rounded

        ring, ring_r = both("ring", [SLOTS, UNIT])
        const = sb("const", [NCONST])
        x = sb("x", [TT, D])
        xn = sb("xn", [TT, D])
        hT, hT_lo = both("hT", [KD, T])
        qkT, yT_lo = both("qkT", [8, T])
        v = sb("v", [TT, 512])
        raw, raw_r = both("raw", [8, T + 3])
        gm, merged_lo = both("gm", [KD, T])
        mqk = sb("mqk", [8, T])
        vaug = sb("vaug", [TT, HEADS, P + 1])
        osig = sb("osig", [TT, 512])
        att = sb("att", [3072])
        WT = sb("WT", [2, 384])
        o = sb("o", [TT, 512])
        tmp = sb("tmp", [2, 512])
        vrows = sb("vrows", [P])
        cols = sb("cols", [NROWS])
        w_if, w_if_lo = both("w_if", [KD, 8])
        w_if_hi = sb("w_if_hi", [KD, 8], F32R)
        b_r = sb("b_r", [G + NE])
        w_r = sb("w_r", [KD, G + NE])
        sm = sb("sm", [320])
        router = sb("router", [800])
        flag = sb("flag", [1], I32)
        idx = sb("idx", [2, TT, 8], U32)

        ga = gm
        gm2 = mqk
        sc = att[:, 0:1536].rearrange("p (b c n) -> p b c n", b=2, c=2)
        a_sb = xn[:].rearrange("p a n -> p (a n)")[:, 0:1536].rearrange("p (h n) -> p h n", h=HEADS)
        wts = [WT[:, 0], WT[:, 1], att[:, 1536:1920], att[:, 1920:2304]]
        aT = att[:, 2304:3072].rearrange("p (b n) -> p b n", b=2)
        gt1b = att[:, 0:1024]
        gt2b = att[:, 1024:2048]
        nfb = att[:, 2048:3072]
        lgT = tmp[:, 0, 0:T]
        yT, yT_hi = qkT, raw_r[:, :, 0:T]
        hT_hi = ring_r[:, SLOTS - 1, :].rearrange("p (k n) -> p k n", k=KD)
        merged_hi = hT_hi
        sig, act_a, hid = tmp[:, 0, 0:F], tmp[:, 0, F:2 * F], tmp[:, 1, 0:F]
        hidT = WT[:].rearrange("p b n -> p (b n)")[:, 0:2 * P].rearrange("p (f n) -> p f n", f=2)
        arow = sb("arow", [2, 256])
        rbias = sb("rbias", [G + NE])
        lamv = tmp[:, 0, 0:4 * DA_HD].rearrange("p (a n) -> p a n", a=4)
        spare = const[:, CONSTS["alibi"][0]:CONSTS["alibi"][0] + 1024]
        pone = spare[:, 0:256].rearrange("p (t e n) -> p t e n", t=TT, e=QUAD)
        pgate = spare[:, 256:512].rearrange("p (t e n) -> p t e n", t=TT, e=QUAD)
        ptg = spare[:, 512:1024].rearrange("p (b t n) -> p b t n", b=2, t=TT)
        grow = o[:].rearrange("p a (b n) -> p (a b) n", b=2)
        xg = raw[:, :, 0:256].rearrange("p k (b n) -> p b k n", b=2)
        outs = v
        outs2 = outs[:].rearrange("p a n -> p (a n)")
        junk = hT[:].rearrange("p a n -> p (a n)")

        def K(name):
            c0, shape = CONSTS[name]
            ap = const[:, c0:c0 + int(np.prod(shape))]
            if len(shape) == 2:
                return ap.rearrange("p (a b) -> p a b", a=shape[0])
            if len(shape) == 3:
                return ap.rearrange("p (a b c) -> p a b c", a=shape[0], b=shape[1])
            return ap

        ident, ones = K("ident"), K("ones")

        def col(name, i=0, n=1):
            r0 = ROWS[name][0]
            return cols[:, r0 + i:r0 + i + n]

        small_at, small = [0], {}

        def S(name, n=1):
            if name not in small:
                small[name] = (small_at[0], n)
                small_at[0] += n
            a, n = small[name]
            return sm[:, a:a + n]

        r_at, r_names = [0], {}

        def R(name, *shape):
            if name not in r_names:
                r_names[name] = (r_at[0], shape)
                r_at[0] += int(np.prod(shape))
            a, shape = r_names[name]
            ap = router[:, a:a + int(np.prod(shape))]
            if len(shape) == 2:
                return ap.rearrange("p (a b) -> p a b", a=shape[0])
            if len(shape) == 3:
                return ap.rearrange("p (a b c) -> p a b c", a=shape[0], b=shape[1])
            return ap

        bank = [ctx.enter_context(nc.psum_tensor(f"bank{i}", [P, 512], F32)) for i in range(8)]
        bank_full = [sem(f"bank_full{i}") for i in range(8)]
        bank_free = [sem(f"bank_free{i}") for i in range(8)]

        def pb(job):
            return bank[JOB[job] % 8]

        def full(job):
            return bank_full[JOB[job] % 8], JOB[job] // 8 + 1

        def free(job):
            return bank_free[JOB[job] % 8], JOB[job] // 8 + 1

        def filled(ins, job):
            ins.then_inc(bank_full[JOB[job] % 8], 1)

        def release(ins, job):
            ins.then_inc(bank_free[JOB[job] % 8], 1)

        y_banks = [pb(job) for job in ("wo3", "x2T2", "lgT", "x2T3")]
        token_bank, up_bank, out_banks = pb("lg"), pb("gt2b0"), (pb("gt2b1"), pb("rank"))

        x_in, const_in, const2_in, c_in, vec_in, bc_in, nf_in, gt1_in, gt2_in, wr_in, out_done = (
            sem(n) for n in ("x_in", "const_in", "const2_in", "c_in", "vec_in", "bc_in", "nf_in", "gt1_in", "gt2_in",
                             "wr_in", "out_done"))
        landed = [sem(f"landed{i}") for i in range(XSLOTS)]
        used = sem("used")
        dve_chain, act_chain = sem("dve_chain"), sem("act_chain")
        names = ["sq", "var", "std", "xn_r", "cols_r", "mod1", "gates", "gexp", "gln", "grows", "conv_out", "mqk_r",
                 "smax", "pexp", "a_r", "emn", "warg", "wexp", "pv", "h_sq", "var2", "std2", "hn_r", "var3", "std3",
                 "mod2", "wr_r", "merged", "lexp", "lam_e", "x2", "sq2", "var4", "std4", "x2n", "lg_r",
                 "rexp", "mask_r", "flag_r", "pads", "sq5", "var5", "std5", "y_out",
                 "g_full", "g_evac", "pg_ready", "pt_full", "pt_evac", "sig_r", "hid_done", "hT_evac",
                 "o_dve", "scat", "act_end", "dve_end", "moe_chain", "y_full", "r_chain", "w_hi", "w_lo", "h_hi",
                 "h_hi_dve", "h_lo", "if_hi", "y_lo", "m_hi", "m_lo", "r4"]
        s = {n: sem(n) for n in names}

        w_ada = t["w_ada"][0].rearrange("(k p) n -> p k n", p=P)
        w_in = t["w_in"][0].rearrange("(k p) n -> p k n", p=P)
        w_bra = t["w_br_a"][0].rearrange("(k p) n -> p k n", p=P)
        w_brm = t["w_br_m"][0].rearrange("(k p) n -> p k n", p=P)
        w_out = t["w_out"][0].rearrange("(k p) n -> p k n", p=P)
        w_e = {"w1": t["w_e1"].rearrange("l g e (k p) f -> (l g e) p k f", p=P),
               "w3": t["w_e3"].rearrange("l g e (k p) f -> (l g e) p k f", p=P),
               "w2": t["w_e2"].rearrange("l g e (k p) n -> (l g e) p k n", p=P)}

        def slot_of(n):
            return n % RING if n < NPRE + RING else n - NPRE

        def landed_value(n):
            return 16 * sum(slot_of(m) == slot_of(n) for m in range(n + 1))

        def slot(i, k):
            at = ring[:, i, :] if i < SLOTS else (hT, qkT, gm, mqk)[i - SLOTS][:].rearrange("p a n -> p (a n)")
            return at.rearrange("p (k n) -> p k n", k=k)

        def unit(n, k):
            return slot(slot_of(n), k)

        def hi(d):
            return ring_r[:, RING + d % HI, :]

        block = ctx.enter_context(nc.Block())

        @block.sync
        def _(sp):
            sp.dma_start(vrows[ROWS["c"][0]:ROWS["c"][1], :], t["c"].rearrange("l (r n) -> (l r) n", n=P)
                         ).then_inc(c_in, 16)
            sp.dma_start(const[:, 0:2 * P], t["const"][:, 0:2 * P]).then_inc(const_in, 16)
            for tt in range(TT):
                sp.dma_start(x[:, tt, :], t["x"][0, tt * P:(tt + 1) * P, :]).then_inc(x_in, 16)
            src = {"in": w_in, "br_a": w_bra, "br_m": w_brm, "out": w_out}
            for n, (kind, c0) in enumerate(UNITS):
                if n >= RING:
                    sp.wait_ge(*full(UNIT_JOB[n - RING]))
                if kind == "ada":
                    i, k0 = c0
                    sp.dma_start(unit(n, 2), w_ada[:, k0:k0 + 2, i * D:(i + 1) * D]).then_inc(landed[slot_of(n)], 16)
                    continue
                k = 4 if kind in ("br_a", "br_m") else 8
                w = UNIT // k
                sp.dma_start(unit(n, k), src[kind][:, :, c0:c0 + w]).then_inc(landed[slot_of(n)], 16)

            def load(q, j, u):
                w, e = QUAD_UNITS[u]
                i = slot_of(NPRE + (j * QU + u) % XSLOTS)
                expert = w_e[w][q * QUAD + e] if isinstance(q, int) else \
                    w_e[w][bass.ds(q * QUAD + e, 1)].rearrange("a p k n -> p (a k) n")
                sp.dma_start(slot(i, 2 if w == "w2" else 8), expert).then_inc(landed[i], 16)

            def load_round(r, q0, first=0):
                for m in range(first, LOOP * QU):
                    sp.wait_ge(used, r * (LOOP * QU) + (m - XSLOTS + 1))
                    load(q0 + m // QU, m // QU, m % QU)

            last = [full(UNIT_JOB[NPRE + u - RING]) for u in range(RING)] + [full("wo3")] * (SLOTS - RING)
            last += [full("lgT"), full("brm3"), full("wo3"), (s["merged"], 4)]
            for m in range(XSLOTS):
                sp.wait_ge(*last[m])
                load(m // QU, m // QU, m % QU)
            load_round(0, 0, XSLOTS)
            with sp.Fori(1, NQ // LOOP) as r:
                load_round(r, r * LOOP)
            sp.wait_ge(s["flag_r"], 1)
            over = sp.value_load(flag[0:1, 0:1], min_val=0, max_val=1)
            with sp.If(over > 0):
                with sp.Fori(1, PASSES) as p:
                    with sp.Fori(0, NQ // LOOP) as r:
                        load_round(p * (NQ // LOOP) + r, r * LOOP)
            for tt in range(TT):
                for c in range(2):
                    sl = slice(512 * c, 512 * c + 512)
                    sp.wait_ge(s["y_out"], 2 * tt + c + 1)
                    sp.dma_start(out[0, tt * P:(tt + 1) * P, sl], x[:, tt, sl]).then_inc(out_done, 16)
            sp.wait_ge(out_done, 16 * 2 * TT)

        @block.gpsimd
        def _(pool):
            pool.memset(raw[:, :, 0:3], 0.0).then_inc(s["pads"], 1)
            pool.memset(vaug[:, :, :, P:P + 1], 1.0).then_inc(s["pads"], 1)
            for d, n in enumerate(DENSE):
                pool.wait_ge(s["w_hi"], d + 1)
                pool.tensor_tensor(ring_r[:, slot_of(n), :], ring[:, slot_of(n), :], hi(d).bitcast(F32),
                                   ALU.subtract).then_inc(s["w_lo"], 1)

        @block.scalar
        def _(act):
            chain = [0]

            def link(ins):
                chain[0] += 1
                ins.then_inc(act_chain, 1)
                act.wait_ge(act_chain, chain[0])

            for name, src in (("norm1", t["norm1"]), ("norm2", t["norm2"]), ("b_ada", t["b_ada"]),
                              ("conv_w", t["conv_w"].rearrange("l j n -> l (j n)")), ("conv_b", t["conv_b"]),
                              ("diff_norm", t["diff_norm"]), ("mlstm_norm", t["mlstm_norm"])):
                r0, r1 = ROWS[name]
                act.dma_start(vrows[r0:r1, :], src.rearrange("l (r n) -> (l r) n", n=P)).then_inc(vec_in, 16)
            act.wait_ge(*full("cT"))
            release(act.activation(S("cs", 8), pb("cT")[:, 0:8], ACT.Silu), "cT")
            act.dma_start(w_if[:], w_in[:, :, C_IF:C_IF + 8]).then_inc(bc_in, 16)
            act.dma_start(S("b_if", 1)[0:8, :], t["b_if"][0].rearrange("(p o) -> p o", o=1)).then_inc(bc_in, 16)
            for i, n in enumerate(("lam_q1", "lam_k1", "lam_q2", "lam_k2")):
                act.dma_start(lamv[:, i, :], t[n][0].partition_broadcast(P)).then_inc(bc_in, 16)

            def split(d):
                n = DENSE[d]
                act.wait_ge(landed[slot_of(n)], landed_value(n))
                if d >= HI:
                    act.wait_ge(*full(DENSE_JOB[d - HI]))
                act.activation(hi(d), ring[:, slot_of(n), :], ACT.Copy).then_inc(s["w_hi"], 1)

            act.wait_ge(x_in, 16 * TT)
            for tt in range(TT):
                act.activation(junk[:, tt * D:(tt + 1) * D], x[:, tt, :], ACT.Square,
                               accum_out=S("ms1", TT)[:, tt:tt + 1]).then_inc(s["sq"], 1)
            act.wait_ge(s["var"], 1)
            act.activation(S("std1", TT), S("var1", TT), ACT.Sqrt).then_inc(s["std"], 1)
            act.wait_ge(bc_in, 96)
            act.activation(w_if_hi[:], w_if[:], ACT.Copy).then_inc(s["if_hi"], 1)
            act.wait_ge(s["mod1"], 2)
            for dst in (hT_hi, hT):
                for i in range(2):
                    act.wait_ge(*full(f"xT{i}"))
                    for j in range(2):
                        k = 2 * i + j
                        ins = act.activation(dst[:, k, :], pb(f"xT{i}")[:, j * T:(j + 1) * T], ACT.Identity,
                                             bias=S("B1", KD)[:, k:k + 1], scale=S("A1", KD)[:, k:k + 1])
                    if dst is hT:
                        release(ins, f"xT{i}")
                    else:
                        ins.then_inc(s["h_hi"], 1)
                if dst is hT_hi:
                    split(0)
            act.dma_start(const[:, 2 * P:NCONST], t["const"][:, 2 * P:NCONST]).then_inc(const2_in, 16)
            split(1)
            split(2)
            act.dma_start(b_r[:, 0:G], t["b_rg"][0].partition_broadcast(P)).then_inc(wr_in, 16)
            act.dma_start(b_r[:, G:G + NE], t["b_re"][0].partition_broadcast(P)).then_inc(wr_in, 16)
            act.dma_start(w_r[:, :, 0:G], t["w_rg"][0].rearrange("(k p) n -> p k n", p=P)).then_inc(wr_in, 16)
            act.dma_start(w_r[:, :, G:G + NE], t["w_re"][0].rearrange("(k p) n -> p k n", p=P)).then_inc(wr_in, 16)
            act.wait_ge(s["lam_e"], 1)
            act.activation(S("lexp", 2), S("ldot", 2), ACT.Exp).then_inc(s["lexp"], 1)
            for i in range(4):
                act.wait_ge(*full(f"qk{i}"))
                release(act.activation(qkT[:, 2 * i:2 * i + 2, :], pb(f"qk{i}")[:].rearrange("p (a n) -> p a n", a=2),
                                       ACT.Copy), f"qk{i}")
                split(3 + i)
                if i == 1:
                    act.wait_ge(s["gates"], 2)
                    act.activation(grow[0:4, 2, :], grow[0:4, 2, :], ACT.Exp).then_inc(s["gexp"], 1)
                    act.wait_ge(s["gexp"], 1)
                    act.activation(grow[0:4, 2, :], grow[0:4, 2, :], ACT.Ln, bias=1.0).then_inc(s["gln"], 1)
            split(7)
            split(8)
            for h in range(HEADS):
                for c in range(2):
                    act.wait_ge(s["smax"], 2 * h + c + 1)
                    act.activation(sc[:, h % 2, c, 0:P], sc[:, h % 2, c, 0:P], ACT.Exp,
                                   bias=S(f"nmx{h % 2}", 4)[:, 2 * c:2 * c + 1],
                                   accum_out=S(f"Z{h % 2}", 4)[:, 2 * c:2 * c + 1])
                    act.activation(sc[:, h % 2, c, P:384], sc[:, h % 2, c, P:384], ACT.Exp,
                                   bias=S(f"nmx{h % 2}", 4)[:, 2 * c + 1:2 * c + 2],
                                   accum_out=S(f"Z{h % 2}", 4)[:, 2 * c + 1:2 * c + 2]).then_inc(s["pexp"], 1)
                act.wait_ge(s["pads"], 1)
                act.wait_ge(*full(f"ml{h}"))
                release(act.activation(raw[:, 2 * h:2 * h + 2, 3:T + 3],
                                       pb(f"ml{h}")[:].rearrange("p (a n) -> p a n", a=2), ACT.Copy), f"ml{h}")
                split(9 + h)
            act.wait_ge(s["pads"], 2)
            for i in range(2):
                act.wait_ge(*full(f"mv{i}"))
                release(act.activation(vaug[:, :, 2 * i:2 * i + 2, 0:P],
                                       pb(f"mv{i}")[:].rearrange("p (t h n) -> p t h n", t=2, h=2), ACT.Copy), f"mv{i}")
                split(13 + i)

            def copy_a(h):
                act.wait_ge(*full(f"aT{h}"))
                if h >= 2:
                    act.wait_ge(s["pv"], h - 1)
                release(act.activation(aT[:, h % 2, :], pb(f"aT{h}")[:, 0:384], ACT.Copy), f"aT{h}")

            copy_a(0)
            copy_a(1)
            act.wait_ge(*free("cols"))
            act.activation(S("emn", 8), S("ccol", 16)[:, 8:16], ACT.Exp).then_inc(s["emn"], 1)
            for h in range(HEADS):
                if h % 2:
                    act.wait_ge(*free(f"Mb{h // 2}"))
                else:
                    act.wait_ge(s["warg"], h // 2 + 1)
                act.activation(wts[h][:, 0:T], wts[h][:, 0:T], ACT.Exp, bias=S("ccol", 16)[:, h:h + 1])
                act.activation(wts[h][:, T:384], wts[h][:, T:384], ACT.Exp,
                               bias=S("ccol", 16)[:, 4 + h:5 + h]).then_inc(s["wexp"], 1)
            copy_a(2)
            split(15)
            copy_a(3)
            for i in range(4):
                act.wait_ge(s["conv_out"], i + 1)
                pair = mqk[:, 2 * i:2 * i + 2, :].rearrange("p a n -> p (a n)")
                act.activation(pair, pair, ACT.Silu).then_inc(s["mqk_r"], 1)
            for i in range(2):
                act.wait_ge(*full(f"mo{i}"))
                release(act.activation(osig[:, :, 256 * i:256 * i + 256],
                                       pb(f"mo{i}")[:].rearrange("p (t n) -> p t n", t=2), ACT.Sigmoid), f"mo{i}")
            split(16)
            act.wait_ge(s["a_r"], 8)
            act.dma_start(gt1b, t["b_ada"][0, 2 * D:3 * D].partition_broadcast(P)).then_inc(gt1_in, 16)
            for tt in range(TT):
                act.wait_ge(*full(f"o{tt}"))
                for h in range(HEADS):
                    ins = act.activation(o[:, tt, h * P:(h + 1) * P], pb(f"o{tt}")[:, h * P:(h + 1) * P], ACT.Square,
                                         accum_out=S("ms2", 8)[:, tt * 4 + h:tt * 4 + h + 1])
            ins.then_inc(s["h_sq"], 1)
            act.wait_ge(s["var2"], 1)
            act.activation(S("std2", 8), S("var2", 8), ACT.Sqrt).then_inc(s["std2"], 1)
            for i in range(4):
                act.wait_ge(*full(f"ga{i}"))
                release(act.activation(ga[:, 2 * i:2 * i + 2, :], pb(f"ga{i}")[:].rearrange("p (a n) -> p a n", a=2),
                                       ACT.Sigmoid), f"ga{i}")
                split(17 + i)
            for h in range(HEADS):
                act.wait_ge(*free(f"num{h}"))
                for tt in range(TT):
                    ins = act.activation(tmp[:, 0, (2 * h + tt) % 4 * P:((2 * h + tt) % 4 + 1) * P],
                                         osig[:, tt, h * P:(h + 1) * P], ACT.Square,
                                         accum_out=S("ms3", 8)[:, tt * 4 + h:tt * 4 + h + 1])
                    if h == 3 and tt == 1:
                        ins.then_inc(s["h_sq"], 1)
                    else:
                        link(ins)
            act.wait_ge(s["var3"], 1)
            act.activation(S("std3", 8), S("var3", 8), ACT.Sqrt).then_inc(s["std3"], 1)
            for i in range(2):
                act.wait_ge(*full(f"yaT{i}"))
                for dst in (yT, yT_hi):
                    ins = act.activation(dst[:, 2 * i:2 * i + 2, :], pb(f"yaT{i}")[:].rearrange("p (a n) -> p a n", a=2),
                                         ACT.Identity, scale=S("dgain", 1), bias=0.0)
                release(ins, f"yaT{i}")
            act.wait_ge(*full("num2"))
            act.wait_ge(*full("num3"))
            act.dma_start(gt2b, t["b_ada"][0, 5 * D:6 * D].partition_broadcast(P)).then_inc(gt2_in, 16)
            act.dma_start(nfb, t["norm_f"].partition_broadcast(P)).then_inc(nf_in, 16)
            for i in range(4):
                act.wait_ge(*full(f"gm{i}"))
                release(act.activation(gm2[:, 2 * i:2 * i + 2, :], pb(f"gm{i}")[:].rearrange("p (a n) -> p a n", a=2),
                                       ACT.Sigmoid), f"gm{i}")
                split(21 + i)
            for i in range(2):
                act.wait_ge(*full(f"ymT{i}"))
                for dst in (yT, yT_hi):
                    ins = act.activation(dst[:, 4 + 2 * i:6 + 2 * i, :], pb(f"ymT{i}")[:].rearrange("p (a n) -> p a n", a=2),
                                         ACT.Identity, scale=col("mlstm_norm"), bias=0.0)
                release(ins, f"ymT{i}")
            for d in range(25, 28):
                split(d)
            for i in range(4):
                act.wait_ge(s["merged"], i + 1)
                act.activation(merged_hi[:, 2 * i:2 * i + 2, :], ga[:, 2 * i:2 * i + 2, :], ACT.Copy).then_inc(s["m_hi"], 1)
            split(28)
            split(29)
            act.activation(S("table", 1), S("std1", TT)[:, 0:1], ACT.Sqrt)

            def square(i):
                act.wait_ge(s["x2"], i + 1)
                for tt in range(TT):
                    ins = act.activation(o[:, tt, 256 * (i % 2):256 * (i % 2) + 256], x[:, tt, 256 * i:256 * i + 256],
                                         ACT.Square, accum_out=S("ms4", 8)[:, 2 * i + tt:2 * i + tt + 1])
                    if i < 3 or tt == 0:
                        link(ins)
                if i == 3:
                    ins.then_inc(s["sq2"], 1)

            def copy_x(i):
                act.wait_ge(*full(f"x2T{i}"))
                release(act.activation(hT[:, 2 * i:2 * i + 2, :], pb(f"x2T{i}")[:].rearrange("p (a n) -> p a n", a=2),
                                       ACT.Copy), f"x2T{i}")

            square(0)
            copy_x(0)
            square(1)
            copy_x(1)
            square(2)
            copy_x(2)
            square(3)
            copy_x(3)
            act.wait_ge(s["var4"], 1)
            act.activation(S("std4", TT), S("var4", TT), ACT.Sqrt).then_inc(s["std4"], 1)
            act.wait_ge(s["r4"], 1)
            for tt in range(TT):
                act.activation(xn[:, tt, :], x[:, tt, :], ACT.Identity, bias=0.0,
                               scale=S("r4", TT)[:, tt:tt + 1]).then_inc(s["x2n"], 1)
            act.wait_ge(s["lg_r"], 1)
            for tt in range(TT):
                act.activation(R("gexp", TT, G)[:, tt, :], R("lg", TT, 36)[:, tt, 0:G], ACT.Exp,
                               bias=R("ngmax", TT)[:, tt:tt + 1],
                               accum_out=R("gsum", TT)[:, tt:tt + 1]).then_inc(s["rexp"], 1)
            act.wait_ge(s["lg_r"], 2)
            act.activation(R("e2", TT), R("dv", TT), ACT.Exp).then_inc(s["rexp"], 1)


            def gather_half(b, half, count):
                act.wait_ge(s["g_full"], count)
                for j in range(4):
                    k = 4 * half + j
                    ins = act.activation(xg[:, b, k, :], token_bank[:, j * P:(j + 1) * P], ACT.Identity,
                                         bias=S("B2", KD)[:, k:k + 1], scale=S("A2", KD)[:, k:k + 1])
                ins.then_inc(s["g_evac"], 1)

            def quad(it, b):
                gather_half(1 - b, 0, it * 2 + 3)
                gather_half(1 - b, 1, it * 2 + 4)
                act.wait_ge(used, it * QU + UP_UNITS)
                act.activation(sig, up_bank[:, 0:F], ACT.Sigmoid).then_inc(s["sig_r"], 1)

            gather_half(0, 0, 1)
            gather_half(0, 1, 2)
            with act.Fori(0, NQ // 2) as i:
                for b in range(2):
                    quad(i * 2 + b, b)
            act.wait_ge(s["flag_r"], 1)
            over = act.value_load(flag[0:1, 0:1], min_val=0, max_val=1)
            with act.If(over > 0):
                with act.Fori(1, PASSES) as p:
                    with act.Fori(0, NQ // 2) as i:
                        for b in range(2):
                            quad(p * NQ + i * 2 + b, b)
            act.activation(S("table", 1), ones[:, 0:1], ACT.Sqrt).then_inc(s["act_end"], 1)

            for tt in range(TT):
                act.wait_ge(s["y_full"], tt + 1)
                for c in range(2):
                    act.activation(junk[:, (2 * tt + c) * 512:(2 * tt + c + 1) * 512], y_banks[2 * tt + c][:], ACT.Square,
                                   accum_out=S("ms5", 4)[:, 2 * tt + c:2 * tt + c + 1]).then_inc(s["sq5"], 1)
                act.wait_ge(s["var5"], tt + 1)
                act.activation(S("std5", TT)[:, tt:tt + 1], S("var5", TT)[:, tt:tt + 1], ACT.Sqrt).then_inc(s["std5"], 1)

        @block.vector
        def _(dve):
            chain = [0]

            def link(ins):
                chain[0] += 1
                ins.then_inc(dve_chain, 1)
                dve.wait_ge(dve_chain, chain[0])

            def own(ins, name, n):
                ins.then_inc(s[name], 1)
                dve.wait_ge(s[name], n)

            def rows(i):
                dve.wait_ge(*full(f"ada{i}"))
                if i >= 2:
                    last = {3: "adaT1", 4: "adaT0", 2: "adaT4", 5: "adaT3"}[i]
                    dve.wait_ge(*full(last))
                release(dve.tensor_copy(arow[:, i % 2, :], pb(f"ada{i}")[:, 0:256]), f"ada{i}")

            def columns(dst, i):
                dve.wait_ge(*full(f"adaT{i}"))
                turned = pb(f"adaT{i}")[:, 0:256].rearrange("p (j u r) -> p u j r", j=2, u=4)[:, :, :, 0]
                release(dve.tensor_tensor(dst.rearrange("p (u j) -> p u j", u=4), turned,
                                          col("b_ada", 8 * i, 8).rearrange("p (u j) -> p u j", u=4), ALU.add),
                        f"adaT{i}")
                dve.wait_ge(*free(f"adaT{i}"))

            def spread(dst, g):
                for i in range(2):
                    job, sl = f"gt{g}b{i}", slice(512 * i, 512 * i + 512)
                    dve.wait_ge(*full(job))
                    release(dve.tensor_tensor(dst[:, sl], pb(job)[:], dst[:, sl], ALU.add), job)

            dve.wait_ge(s["sq"], 2)
            dve.tensor_scalar(S("var1", TT), S("ms1", TT), 1.0 / D, EPS, ALU.mult, ALU.add).then_inc(s["var"], 1)
            dve.wait_ge(s["std"], 1)
            link(dve.reciprocal(S("r1", TT), S("std1", TT)))
            for tt in range(TT):
                dve.tensor_scalar(xn[:, tt, :], x[:, tt, :], S("r1", TT)[:, tt:tt + 1], None,
                                  ALU.mult).then_inc(s["xn_r"], 1)
            dve.wait_ge(*full("vT"))
            release(dve.tensor_copy(cols[:], pb("vT")[:, 0:NROWS]), "vT")
            dve.wait_ge(*free("vT"))
            dve.tensor_scalar(S("dgain", 1), col("diff_norm"), 1.0 - LAMBDA_INIT, None, ALU.mult).then_inc(s["cols_r"], 1)
            rows(0)
            m1 = S("m1", 16)
            columns(m1[:, 0:8], 0)
            dve.tensor_copy(S("B1", KD), m1[:, 0:8]).then_inc(s["mod1"], 1)
            dve.wait_ge(s["if_hi"], 1)
            dve.tensor_tensor(w_if_lo[:], w_if[:], w_if_hi[:].bitcast(F32), ALU.subtract).then_inc(s["if_hi"], 1)
            dve.wait_ge(bc_in, 96)
            for i in range(2):
                ins = dve.tensor_tensor_reduce(lamv[:, 2 * i, :], lamv[:, 2 * i, :], lamv[:, 2 * i + 1, :], 1.0, 0.0,
                                               ALU.mult, ALU.add, S("ldot", 2)[:, i:i + 1])
            ins.then_inc(s["lam_e"], 1)
            rows(1)
            columns(m1[:, 8:16], 1)
            dve.scalar_tensor_tensor(out=S("A1", KD), in0=m1[:, 8:16], scalar=1.0, in1=col("norm1", 0, 8),
                                     op0=ALU.add, op1=ALU.mult).then_inc(s["mod1"], 1)
            dve.wait_ge(s["mod1"], 2)
            for dst in (hT_hi, hT):
                for i in range(2, 4):
                    dve.wait_ge(*full(f"xT{i}"))
                    for j in range(2):
                        k = 2 * i + j
                        ins = dve.tensor_scalar(dst[:, k, :], pb(f"xT{i}")[:, j * T:(j + 1) * T], S("A1", KD)[:, k:k + 1],
                                                S("B1", KD)[:, k:k + 1], ALU.mult, ALU.add)
                    if dst is hT:
                        release(ins, f"xT{i}")
                    else:
                        ins.then_inc(s["h_hi_dve"], 1)
            dve.wait_ge(*free("xT3"))
            dve.tensor_tensor(hT_lo[:, 4:8, :], hT[:, 4:8, :], hT_hi[:, 4:8, :].bitcast(F32), ALU.subtract)
            dve.wait_ge(*free("xT0"))
            dve.wait_ge(*free("xT1"))
            dve.tensor_tensor(hT_lo[:, 0:4, :], hT[:, 0:4, :], hT_hi[:, 0:4, :].bitcast(F32),
                              ALU.subtract).then_inc(s["h_lo"], 1)
            dve.wait_ge(s["lexp"], 1)
            link(dve.tensor_tensor(S("nlam", 1), S("lexp", 2)[:, 1:2], S("lexp", 2)[:, 0:1], ALU.subtract))
            link(dve.tensor_scalar(S("nlam2", 1), S("nlam", 1), -LAMBDA_INIT, None, ALU.add))
            dve.wait_ge(*full("if"))
            release(dve.tensor_scalar(grow[0:8, 2, :], pb("if")[0:8, 0:T], S("b_if", 1)[0:8, :], None, ALU.add), "if")
            dve.wait_ge(*full("ifT"))
            release(dve.tensor_copy(grow[0:4, 0:2, :], pb("ifT")[0:4, :].rearrange("p (a n) -> p a n", a=2)), "ifT")
            dve.wait_ge(*free("ifT"))
            link(dve.tensor_scalar(grow[0:4, 3, :], grow[0:4, 1, :], -1.0, None, ALU.mult))
            own(dve.tensor_tensor(grow[0:4, 2, :], grow[0:4, 3, :], grow[0:4, 1, :], ALU.min), "gates", 1)
            own(dve.tensor_scalar(grow[0:4, 3, :], grow[0:4, 1, :], 0.0, None, ALU.min), "gates", 2)
            B2, A2 = S("B2", KD), S("A2", KD)
            rows(3)
            for i in range(2):
                dve.wait_ge(*full(f"v{i}"))
                if i == 1:
                    columns(B2, 3)
                    dve.tensor_copy(S("B2_r", KD), B2).then_inc(s["mod2"], 1)
                release(dve.tensor_copy(v[:, :, 256 * i:256 * i + 256],
                                        pb(f"v{i}")[:].rearrange("p (t n) -> p t n", t=2)), f"v{i}")
            dve.wait_ge(*free("v1"))
            dve.wait_ge(const2_in, 16)
            dve.wait_ge(s["gln"], 1)
            link(dve.tensor_tensor(grow[0:4, 3, :], grow[0:4, 3, :], grow[0:4, 2, :], ALU.subtract))
            one, zero = ones[0:4, 0:1].to_broadcast([4, T]), K("mask")[0:4, P:P + 1].to_broadcast([4, T])
            link(dve.tensor_tensor_scan(grow[0:4, 1, :], one, grow[0:4, 3, :], 0.0, ALU.mult, ALU.add))
            link(dve.tensor_tensor(grow[0:4, 2, :], grow[0:4, 0, :], grow[0:4, 1, :], ALU.subtract))
            link(dve.tensor_tensor_scan(grow[0:4, 3, :], zero, grow[0:4, 2, :], 0.0, ALU.add, ALU.max))
            dve.scalar_tensor_tensor(out=grow[0:4, 0, :], in0=grow[0:4, 1, :], scalar=-1.0, in1=grow[0:4, 3, :],
                                     op0=ALU.mult, op1=ALU.subtract).then_inc(s["grows"], 1)

            def scores(h):
                if h >= 2:
                    dve.wait_ge(s["a_r"], 2 * h - 2)
                for c in range(2):
                    job = f"s{2 * h + c}"
                    dve.wait_ge(*full(job))
                    release(dve.scalar_tensor_tensor(out=sc[:, h % 2, c, :], in0=pb(job)[:, 0:384], scalar=DA_HD ** -0.5,
                                                     in1=K("alibi")[:, h, :], op0=ALU.mult, op1=ALU.add), job)
                    dve.wait_ge(*free(job))
                    dve.tensor_reduce(S(f"nmx{h % 2}", 4)[:, 2 * c:2 * c + 1], sc[:, h % 2, c, 0:P], AX.X, ALU.max, negate=True)
                    dve.tensor_reduce(S(f"nmx{h % 2}", 4)[:, 2 * c + 1:2 * c + 2], sc[:, h % 2, c, P:384], AX.X, ALU.max,
                                      negate=True).then_inc(s["smax"], 1)

            def combine(h):
                dve.wait_ge(s["pexp"], 2 * h + 2)
                link(dve.reciprocal(S(f"rZ{h % 2}", 4), S(f"Z{h % 2}", 4)))
                link(dve.tensor_scalar(S("rZl", 2), S(f"rZ{h % 2}", 4)[:, 2:4], S("nlam2", 1), None, ALU.mult))
                for i, (a, b) in enumerate(((0, P), (P, 384))):
                    link(dve.tensor_scalar(a_sb[:, h, a:b], sc[:, h % 2, 1, a:b], S("rZl", 2)[:, i:i + 1], None,
                                           ALU.mult))
                    dve.scalar_tensor_tensor(out=a_sb[:, h, a:b], in0=sc[:, h % 2, 0, a:b],
                                             scalar=S(f"rZ{h % 2}", 4)[:, i:i + 1], in1=a_sb[:, h, a:b],
                                             op0=ALU.mult, op1=ALU.add).then_inc(s["a_r"], 1)

            def conv(i):
                dve.wait_ge(*free(f"ml{i}"))
                for k in (2 * i, 2 * i + 1):
                    link(dve.tensor_scalar(mqk[:, k, :], raw[:, k, 3:T + 3], col("conv_w", 24 + k), col("conv_b", k),
                                           ALU.mult, ALU.add))
                    for j in range(3):
                        ins = dve.scalar_tensor_tensor(out=mqk[:, k, :], in0=raw[:, k, j:j + T],
                                                       scalar=col("conv_w", 8 * j + k), in1=mqk[:, k, :],
                                                       op0=ALU.mult, op1=ALU.add)
                        if j < 2:
                            link(ins)
                    if k % 2 == 0:
                        link(ins)
                ins.then_inc(s["conv_out"], 1)

            scores(0)
            scores(1)
            combine(0)
            scores(2)
            combine(1)
            scores(3)
            rows(4)
            conv(0)
            combine(2)
            columns(A2, 4)
            own(dve.scalar_tensor_tensor(out=A2, in0=A2, scalar=1.0, in1=col("norm2", 0, 8),
                                         op0=ALU.add, op1=ALU.mult), "mod2", 2)
            conv(1)
            combine(3)
            dve.wait_ge(*full("cols"))
            release(dve.tensor_copy(S("ccol", 16), pb("cols")[:, 0:16]), "cols")

            def decay_arg(h):
                job = f"Mb{h // 2}"
                dve.wait_ge(*full(job))
                m = pb(job)[:, (h % 2) * T:(h % 2) * T + T]
                dve.tensor_tensor(wts[h][:, 0:T], K("mask")[:, 0:T], m, ALU.subtract)
                ins = dve.tensor_tensor(wts[h][:, T:384], K("mask")[:, T:384], m[:, P:T], ALU.subtract)
                if h % 2:
                    release(ins, job)
                else:
                    ins.then_inc(s["warg"], 1)

            for h in range(HEADS):
                decay_arg(h)
            rows(2)
            conv(2)
            conv(3)
            dve.wait_ge(wr_in, 64)
            dve.wait_ge(*full("rb"))
            release(dve.tensor_tensor(rbias[:], pb("rb")[:, 0:G + NE], b_r[:], ALU.add), "rb")
            dve.wait_ge(*free("rb"))
            for k in range(KD):
                dve.tensor_scalar(w_r[:, k, :], w_r[:, k, :], A2[:, k:k + 1], None, ALU.mult).then_inc(s["wr_r"], 1)
            dve.wait_ge(s["h_sq"], 1)
            dve.tensor_scalar(S("var2", 8), S("ms2", 8), 1.0 / P, EPS, ALU.mult, ALU.add).then_inc(s["var2"], 1)
            dve.wait_ge(s["std2"], 1)
            link(dve.reciprocal(S("r2", 8), S("std2", 8)))
            for tt in range(TT):
                release(dve.tensor_tensor(o[:, tt, :].rearrange("p (h n) -> p h n", h=4),
                                          pb(f"o{tt}")[:].rearrange("p (h n) -> p h n", h=4),
                                          S("r2", 8)[:, 4 * tt:4 * tt + 4].unsqueeze(2).to_broadcast([P, 4, P]),
                                          ALU.mult), f"o{tt}")

            def decay(h):
                dve.wait_ge(s["wexp"], h + 1)
                job = f"ms{h}"
                dve.wait_ge(*full(job))
                release(dve.scalar_tensor_tensor(out=wts[h], in0=pb(job)[:, 0:384], scalar=P ** -0.5,
                                                 in1=wts[h], op0=ALU.mult, op1=ALU.mult), job)

            def hidden(h):
                job = f"num{h}"
                dve.wait_ge(*full(job))
                dve.wait_ge(s["emn"], 1)
                nd = pb(job)[:, 0:2 * (P + 1)].rearrange("p (t n) -> p t n", t=2)
                den, em = nd[:, :, P:P + 1], S("emn", 8).rearrange("p (t n) -> p t n", t=2)[:, :, h:h + 1]
                d1, d2 = (S(n, 2).rearrange("p (t n) -> p t n", t=2) for n in ("d1", "d2"))
                link(dve.scalar_tensor_tensor(out=d1, in0=den, scalar=-1.0, in1=em, op0=ALU.mult, op1=ALU.max))
                link(dve.tensor_tensor(d2, den, d1, ALU.max))
                link(dve.reciprocal(S("rd", 2), S("d2", 2)))
                for tt in range(TT):
                    ins = dve.scalar_tensor_tensor(out=osig[:, tt, h * P:(h + 1) * P], in0=nd[:, tt, 0:P],
                                                   scalar=S("rd", 2)[:, tt:tt + 1], in1=osig[:, tt, h * P:(h + 1) * P],
                                                   op0=ALU.mult, op1=ALU.mult)
                release(ins, job)

            dve.wait_ge(gt1_in, 16)
            spread(gt1b, 1)
            decay(0)
            decay(1)
            hidden(0)
            decay(2)
            hidden(1)
            decay(3)
            hidden(2)
            hidden(3)
            dve.wait_ge(s["h_sq"], 2)
            dve.tensor_scalar(S("var3", 8), S("ms3", 8), 1.0 / P, EPS, ALU.mult, ALU.add).then_inc(s["var3"], 1)
            dve.wait_ge(s["std3"], 1)
            link(dve.reciprocal(S("r3", 8), S("std3", 8)))
            for tt in range(TT):
                view = osig[:, tt, :].rearrange("p (h n) -> p h n", h=4)
                dve.tensor_tensor(view, view, S("r3", 8)[:, 4 * tt:4 * tt + 4].unsqueeze(2).to_broadcast([P, 4, P]),
                                  ALU.mult).then_inc(s["hn_r"], 1)

            def y_low(name, i):
                dve.wait_ge(*free(f"y{name}T{i}"))
                a = 2 * i + (4 if name == "m" else 0)
                dve.tensor_tensor(yT_lo[:, a:a + 2, :], yT[:, a:a + 2, :], yT_hi[:, a:a + 2, :].bitcast(F32),
                                  ALU.subtract).then_inc(s["y_lo"], 1)

            for name in ("a", "m"):
                for i in range(2):
                    y_low(name, i)
            for i in range(4):
                job, view = f"bra{i}", ga[:, 2 * i:2 * i + 2, :]
                dve.wait_ge(*free(f"ga{i}"))
                dve.wait_ge(*full(job))
                release(dve.tensor_tensor(view, pb(job)[:].rearrange("p (a n) -> p a n", a=2), view, ALU.mult), job)

            def merged_low(i):
                two = slice(2 * i, 2 * i + 2)
                dve.wait_ge(s["m_hi"], i + 1)
                dve.tensor_tensor(merged_lo[:, two, :], ga[:, two, :], merged_hi[:, two, :].bitcast(F32),
                                  ALU.subtract).then_inc(s["m_lo"], 1)

            for i in range(4):
                job, view, va = f"brm{i}", gm2[:, 2 * i:2 * i + 2, :], ga[:, 2 * i:2 * i + 2, :]
                dve.wait_ge(*free(f"gm{i}"))
                dve.wait_ge(*full(job))
                release(dve.tensor_tensor(view, pb(job)[:].rearrange("p (a n) -> p a n", a=2), view, ALU.mult), job)
                dve.wait_ge(*free(job))
                own(dve.tensor_tensor(va, va, view, ALU.add), "merged", i + 1)
                if i:
                    merged_low(i - 1)
            merged_low(3)

            def residual(i):
                dve.wait_ge(*full(f"wo{i}"))
                if i >= 1:
                    dve.wait_ge(s["x2"], i)
                g = gt1b[:, 256 * i:256 * i + 256].unsqueeze(1).to_broadcast([P, TT, 256])
                tv = tmp[:, 0, :].rearrange("p (t n) -> p t n", t=2)
                release(dve.tensor_tensor(tv, pb(f"wo{i}")[:].rearrange("p (t n) -> p t n", t=2), g, ALU.mult), f"wo{i}")
                dve.wait_ge(*free(f"wo{i}"))
                xv = x[:, :, 256 * i:256 * i + 256]
                own(dve.tensor_tensor(xv, xv, tv, ALU.add), "x2", i + 1)

            rows(5)
            for i in range(4):
                residual(i)
            dve.memset(ptg[:, 1], 0.0).then_inc(s["pt_evac"], 1)
            dve.memset(outs2, 0.0).then_inc(s["o_dve"], 1)
            dve.memset(hid, 0.0).then_inc(s["hid_done"], 1)
            dve.wait_ge(s["sq2"], 1)
            link(dve.tensor_reduce(S("ms4s", TT), S("ms4", 8).rearrange("p (i t) -> p t i", t=TT), AX.X, ALU.add))
            dve.tensor_scalar(S("var4", TT), S("ms4s", TT), 1.0 / D, EPS, ALU.mult, ALU.add).then_inc(s["var4"], 1)
            dve.wait_ge(s["std4"], 1)
            own(dve.reciprocal(S("r4", TT), S("std4", TT)), "r4", 1)

            lg, g8 = R("lg", TT, 36), R("g8", TT, 8)
            link(dve.memset(g8, -3.0e38))
            dve.wait_ge(*full("lgT"))
            release(dve.tensor_copy(lgT[0:G + NE, :], pb("lgT")[0:G + NE, 0:T]), "lgT")
            dve.wait_ge(*full("lg"))
            release(dve.tensor_tensor(lg, pb("lg")[:, 0:72].rearrange("p (t n) -> p t n", t=2),
                                      S("r4", TT).unsqueeze(2).to_broadcast([P, TT, 36]), ALU.mult), "lg")
            dve.wait_ge(*free("lg"))
            link(dve.tensor_tensor(lg, lg, rbias[:].unsqueeze(1).to_broadcast([P, TT, 36]), ALU.add))
            link(dve.tensor_copy(g8[:, :, 0:G], lg[:, :, 0:G]))
            g_top, e_top, esel = R("g_top", TT, 8), R("e_top", TT, 8), R("esel", TT, 8)
            for tt in range(TT):
                ins = dve.max(g_top[:, tt, :], g8[:, tt, :])
            link(ins)
            dve.tensor_scalar(R("ngmax", TT).unsqueeze(2), g_top[:, :, 0:1], -1.0, None, ALU.mult).then_inc(s["lg_r"], 1)
            for tt in range(TT):
                ins = dve.max_index(idx[:, 0, tt, :], g_top[:, tt, :], g8[:, tt, :])
            link(ins)
            gi, ei = R("gi", TT, 8), R("ei", TT, 8)
            link(dve.tensor_copy(gi, idx[:, 0]))
            ohg = R("ohg", TT, G)
            iota8 = K("iota8")
            link(dve.tensor_tensor(ohg, iota8[:, :, 0:G], gi[:, :, 0:1].to_broadcast([P, TT, G]), ALU.is_equal))
            prod = R("prod", TT, G, E)
            e_lg = lg[:, :, G:G + NE].rearrange("p t (g e) -> p t g e", g=G)
            link(dve.tensor_tensor(prod, e_lg, ohg.unsqueeze(3).to_broadcast([P, TT, G, E]), ALU.mult))
            link(dve.tensor_reduce(esel, prod.rearrange("p t g e -> p t e g"), AX.X, ALU.add))
            for tt in range(TT):
                ins = dve.max(e_top[:, tt, :], esel[:, tt, :])
            link(ins)
            own(dve.tensor_tensor(R("dv", TT).unsqueeze(2), e_top[:, :, 1:2], e_top[:, :, 0:1], ALU.subtract), "lg_r", 2)
            for tt in range(TT):
                ins = dve.max_index(idx[:, 1, tt, :], e_top[:, tt, :], esel[:, tt, :])
            link(ins)
            link(dve.tensor_copy(ei, idx[:, 1]))
            oh1, oh2 = R("oh1", TT, E), R("oh2", TT, E)
            dve.tensor_tensor(oh1, iota8, ei[:, :, 0:1].to_broadcast([P, TT, E]), ALU.is_equal)
            link(dve.tensor_tensor(oh2, iota8, ei[:, :, 1:2].to_broadcast([P, TT, E]), ALU.is_equal))
            m8 = R("m8", TT, E)
            link(dve.tensor_tensor(m8, oh1, oh2, ALU.add))
            mask = R("mask", TT, NE)
            own(dve.tensor_tensor(mask.rearrange("p t (g e) -> p t g e", g=G),
                                  ohg.unsqueeze(3).to_broadcast([P, TT, G, E]),
                                  m8.unsqueeze(2).to_broadcast([P, TT, G, E]), ALU.mult), "mask_r", 1)
            NX = NE + QUAD
            gate, rank = R("gate", TT, NX), R("rank", TT, NX)
            dve.wait_ge(*full("rank"))
            link(dve.scalar_tensor_tensor(out=rank[:, :, 0:NE], in0=pb("rank")[:, 0:2 * NE].rearrange("p (t n) -> p t n", t=2),
                                          scalar=1.0, in1=mask, op0=ALU.add, op1=ALU.mult))
            link(dve.tensor_scalar(rank[:, :, 0:NE], rank[:, :, 0:NE], -1.0, None, ALU.add))
            dve.tensor_tensor(pone[:], K("slot"), rank[:, :, 0:QUAD].unsqueeze(3).to_broadcast([P, TT, QUAD, CAP]),
                              ALU.is_equal).then_inc(s["moe_chain"], 1)
            link(dve.tensor_scalar(rank[:, :, NE:NX], rank[:, :, 0:QUAD], -float(CAP), None, ALU.add))
            dve.wait_ge(gt2_in, 16)
            spread(gt2b, 2)
            dve.wait_ge(s["rexp"], 3)
            den = R("den", TT)
            link(dve.tensor_scalar(den, R("e2", TT), 1.0, None, ALU.add))
            link(dve.tensor_tensor(den, den, R("gsum", TT), ALU.mult))
            w1, w2 = R("w1", TT), R("w2", TT)
            link(dve.reciprocal(w1, den))
            link(dve.tensor_tensor(w2, w1, R("e2", TT), ALU.mult))
            we = R("we", TT, E)
            dve.tensor_tensor(oh1, oh1, w1.unsqueeze(2).to_broadcast([P, TT, E]), ALU.mult)
            link(dve.tensor_tensor(oh2, oh2, w2.unsqueeze(2).to_broadcast([P, TT, E]), ALU.mult))
            link(dve.tensor_tensor(we, oh1, oh2, ALU.add))
            link(dve.tensor_tensor(R("g32", TT, NE).rearrange("p t (g e) -> p t g e", g=G),
                                   ohg.unsqueeze(3).to_broadcast([P, TT, G, E]),
                                   we.unsqueeze(2).to_broadcast([P, TT, G, E]), ALU.mult))
            link(dve.tensor_copy(gate[:, :, 0:NE], R("g32", TT, NE)))
            link(dve.tensor_copy(gate[:, :, NE:NX], gate[:, :, 0:QUAD]))
            dve.wait_ge(s["moe_chain"], 1)
            dve.tensor_tensor(pgate[:], pone[:], gate[:, :, 0:QUAD].unsqueeze(3).to_broadcast([P, TT, QUAD, CAP]),
                              ALU.mult).then_inc(s["pg_ready"], 1)
            release(dve.reduce_max(S("cmax", 1)[0:1, :], pb("rank")[0:1, 2 * NE:3 * NE], AX.X), "rank")
            dve.wait_ge(*free("rank"))
            dve.tensor_scalar(flag[0:1, :], S("cmax", 1)[0:1, :], CAP + 0.5, None, ALU.is_gt).then_inc(s["flag_r"], 1)

            MC = 2

            def one_hot(at, base, c0):
                dve.tensor_tensor(pone[:], K("slot"), rank[:, :, at].unsqueeze(3).to_broadcast([P, TT, QUAD, CAP]),
                                  ALU.is_equal).then_inc(s["moe_chain"], 1)
                dve.wait_ge(s["moe_chain"], base + c0)
                dve.tensor_tensor(pgate[:], pone[:], gate[:, :, at].unsqueeze(3).to_broadcast([P, TT, QUAD, CAP]),
                                  ALU.mult).then_inc(s["pg_ready"], 1)

            def quad(q, it, b):
                dve.wait_ge(s["pt_full"], it + 1)
                one_hot(bass.ds(q * QUAD + QUAD, QUAD), it * MC, 2)
                dve.wait_ge(s["sig_r"], it + 1)
                dve.tensor_tensor(act_a, up_bank[:, 0:F], sig, ALU.mult).then_inc(s["moe_chain"], 1)
                dve.wait_ge(s["moe_chain"], it * MC + 3)
                dve.tensor_tensor(hid, up_bank[:, F:2 * F], act_a, ALU.mult).then_inc(s["hid_done"], 1)
                dve.wait_ge(s["pt_full"], it + 2)
                dve.tensor_copy(hidT.rearrange("p f n -> p (f n)"), token_bank[:, T:2 * T]).then_inc(s["hT_evac"], 1)
                dve.wait_ge(s["scat"], it + 1)
                dve.tensor_copy(ptg[:, 1 - b].rearrange("p t n -> p (t n)"), token_bank[:, 0:T]).then_inc(s["pt_evac"], 1)
                dve.wait_ge(used, it * QU + QU)
                for c in range(2):
                    sl = slice(512 * c, 512 * c + 512)
                    ins = dve.tensor_tensor(outs2[:, sl], out_banks[c][:], gt2b[:, sl], ALU.mult)
                ins.then_inc(s["o_dve"], 1)

            dve.wait_ge(s["pt_full"], 1)
            dve.tensor_copy(ptg[:, 0].rearrange("p t n -> p (t n)"), token_bank[:, 0:T]).then_inc(s["pt_evac"], 1)
            with dve.Fori(0, NQ // 2) as i:
                for b in range(2):
                    quad(i * 2 + b, i * 2 + b, b)
            dve.wait_ge(s["flag_r"], 1)
            over = dve.value_load(flag[0:1, 0:1], min_val=0, max_val=1)
            with dve.If(over > 0):
                with dve.Fori(1, PASSES) as p:
                    dve.tensor_scalar(rank, rank, -float(CAP), None, ALU.add).then_inc(s["r_chain"], 1)
                    dve.wait_ge(s["r_chain"], p)
                    dve.tensor_copy(S("step", 1), ones[:, 0:1])
                    with dve.Fori(0, NQ // 2) as i:
                        for b in range(2):
                            quad(i * 2 + b, p * NQ + i * 2 + b, b)
            dve.tensor_copy(S("end", 1), ones[:, 0:1]).then_inc(s["dve_end"], 1)

            dve.wait_ge(nf_in, 16)
            for tt in range(TT):
                m5, v5, r5 = S("m5", TT)[:, tt:tt + 1], S("var5", TT)[:, tt:tt + 1], S("r5", TT)[:, tt:tt + 1]
                dve.wait_ge(s["sq5"], 2 * tt + 1)
                link(dve.tensor_scalar(m5, S("ms5", 4)[:, 2 * tt:2 * tt + 1], 1.0 / D, EPS, ALU.mult, ALU.add))
                dve.wait_ge(s["sq5"], 2 * tt + 2)
                dve.scalar_tensor_tensor(out=v5, in0=S("ms5", 4)[:, 2 * tt + 1:2 * tt + 2], scalar=1.0 / D, in1=m5,
                                         op0=ALU.mult, op1=ALU.add).then_inc(s["var5"], 1)
                dve.wait_ge(s["std5"], tt + 1)
                link(dve.reciprocal(r5, S("std5", TT)[:, tt:tt + 1]))
                for c in range(2):
                    sl = slice(512 * c, 512 * c + 512)
                    dve.scalar_tensor_tensor(out=x[:, tt, sl], in0=y_banks[2 * tt + c][:], scalar=r5, in1=nfb[:, sl],
                                             op0=ALU.mult, op1=ALU.mult).then_inc(s["y_out"], 1)

        @block.tensor
        def _(pe):
            at = [0]

            def take(job):
                n = JOB[job]
                if n >= 8:
                    pe.wait_ge(bank_free[n % 8], n // 8)
                return bank[n % 8]

            def next_unit(k):
                n = at[0]
                at[0] += 1
                pe.wait_ge(landed[slot_of(n)], landed_value(n))
                return unit(n, k)

            def ada(i):
                ps = take(f"ada{i}")
                for k0 in range(0, KD, 2):
                    w = next_unit(2)
                    for k in range(k0, k0 + 2):
                        for u in range(4):
                            ins = pe.matmul(ps[32 * u:32 * u + 32, 0:256], S("cs", 8)[:, k:k + 1].to_broadcast([P, 32]),
                                            w[:, k - k0, 256 * u:256 * u + 256], start=(k == 0), stop=(k == KD - 1),
                                            tile_position=(0, 32 * u))
                filled(ins, f"ada{i}")

            def ada_turn(i):
                ps = take(f"adaT{i}")
                pe.wait_ge(*free(f"ada{i}"))
                for j in range(2):
                    ins = pe.transpose(ps[:, j * P:(j + 1) * P], arow[:, i % 2, j * P:(j + 1) * P], ident)
                filled(ins, f"adaT{i}")

            def ada_spread(i, g, half):
                ps = take(f"gt{g}b{half}")
                pe.wait_ge(*free(f"ada{i}"))
                for j in range(2):
                    u = 2 * half + j
                    ins = pe.matmul(ps[:, j * 256:(j + 1) * 256], ident[:, 32 * u:32 * u + 1].to_broadcast([P, P]),
                                    arow[:, i % 2, :], start=True, stop=True)
                filled(ins, f"gt{g}b{half}")

            dense = [0]

            def next_dense(k):
                d = dense[0]
                dense[0] += 1
                n = DENSE[d]
                assert n == at[0]
                at[0] += 1
                pe.wait_ge(s["w_hi"], d + 1)
                return hi(d).rearrange("p (k n) -> p k n", k=k), \
                    ring_r[:, slot_of(n), :].rearrange("p (k n) -> p k n", k=k), ((s["w_lo"], d + 1),)

            def product(out, a, b, nk):
                passes = ((a[0], b[0]), (a[1], b[0]), (a[0], b[1]))
                for i, (left, right) in enumerate(passes):
                    if i == 1:
                        for needed in a[2]:
                            pe.wait_ge(*needed)
                    if i == 2:
                        for needed in b[2]:
                            pe.wait_ge(*needed)
                    for k in range(nk):
                        ins = pe.matmul(out, left(k), right(k), start=(i == 0 and k == 0), stop=(i == 2 and k == nk - 1))
                return ins

            def proj_T(job, src, w, j0=0, nk=KD):
                ps = take(job)
                for j in range(2):
                    c = slice((j0 + j) * P, (j0 + j + 1) * P)
                    ins = product(ps[:, j * T:(j + 1) * T], (lambda k: w[0][:, k, c], lambda k: w[1][:, k, c], w[2]), src, nk)
                filled(ins, job)

            def proj(job, src, w):
                ps = take(job)
                for tt in range(TT):
                    c = slice(tt * P, (tt + 1) * P)
                    ins = product(ps[:, tt * 256:(tt + 1) * 256],
                                  (lambda k: src[0](k)[:, c], lambda k: src[1](k)[:, c], src[2]),
                                  (lambda k: w[0][:, k, :], lambda k: w[1][:, k, :], w[2]), KD)
                filled(ins, job)

            hsrc = (lambda k: hT_hi[:, k, :], lambda k: hT_lo[:, k, :],
                    ((s["h_lo"], 1),))

            pe.wait_ge(const_in, 16)
            pe.wait_ge(c_in, 16)
            filled(pe.transpose(take("cT")[:, 0:8], vrows[0:8, :], ident[0:8, 0:8]), "cT")
            pe.wait_ge(*free("cT"))
            ada(0)
            pe.wait_ge(vec_in, 112)
            filled(pe.transpose(take("vT")[:, 0:NROWS], vrows[0:NROWS, :], ident[0:NROWS, 0:NROWS]), "vT")
            pe.wait_ge(s["xn_r"], 2)
            for i in range(4):
                ps = take(f"xT{i}")
                for j in range(2):
                    for tt in range(TT):
                        k = 2 * i + j
                        ins = pe.transpose(ps[:, j * T + tt * P:j * T + (tt + 1) * P], xn[:, tt, k * P:(k + 1) * P], ident)
                filled(ins, f"xT{i}")
            ada_turn(0)
            ada(1)
            ada_turn(1)
            ps = take("if")
            pe.wait_ge(s["if_hi"], 2)
            pe.wait_ge(s["h_hi"], 2)
            pe.wait_ge(s["h_hi_dve"], 2)
            ins = product(ps[0:8, 0:T], (lambda k: w_if_hi[:, k, :], lambda k: w_if_lo[:, k, :], ((s["if_hi"], 2),)),
                          hsrc, KD)
            filled(ins, "if")
            for i in range(4):
                if i == 1:
                    ps = take("ifT")
                    pe.wait_ge(*free("if"))
                    for g in range(2):
                        ins = pe.matmul(ps[0:4, g * T:(g + 1) * T], ident[0:8, 4 * g:4 * g + 4], grow[0:8, 2, :],
                                        start=True, stop=True)
                    filled(ins, "ifT")
                proj_T(f"qk{i}", hsrc, next_dense(8))
            ada(3)
            proj("v0", hsrc, next_dense(8))
            ada_turn(3)
            proj("v1", hsrc, next_dense(8))
            for i in range(4):
                pe.wait_ge(*free(f"qk{i}"))
            for h in range(HEADS):
                for c in range(2):
                    ps = take(f"s{2 * h + c}")
                    r = slice(64 * c, 64 * c + 64)
                    pe.matmul(ps[:, 0:P], qkT[r, h, 0:P], qkT[r, 4 + h, 0:P], start=True, stop=True)
                    filled(pe.matmul(ps[:, P:384], qkT[r, h, P:T], qkT[r, 4 + h, :], start=True, stop=True),
                           f"s{2 * h + c}")
            for i in range(4):
                if i == 2:
                    ada(4)
                proj_T(f"ml{i}", hsrc, next_dense(8))
            ada_turn(4)
            ps = take("cols")
            pe.wait_ge(s["grows"], 1)
            pe.wait_ge(const2_in, 16)
            for j, row in enumerate((2, 0)):
                for tt in range(TT):
                    ins = pe.transpose(ps[:, 8 * j + 4 * tt:8 * j + 4 * tt + 4], grow[0:4, row, tt * P:(tt + 1) * P],
                                       ident[0:4, 0:4])
            filled(ins, "cols")
            for i in range(2):
                ps = take(f"Mb{i}")
                for j in range(2):
                    pick = ident[0:4, 2 * i + j:2 * i + j + 1].to_broadcast([4, P])
                    ins = pe.matmul(ps[:, j * T:(j + 1) * T], pick, grow[0:4, 3, :], start=True, stop=True)
                filled(ins, f"Mb{i}")
            proj("mv0", hsrc, next_dense(8))
            pe.wait_ge(*free("v0"))
            pe.wait_ge(*free("v1"))

            def transpose_a(h):
                ps = take(f"aT{h}")
                pe.wait_ge(s["a_r"], 2 * h + 2)
                for j in range(3):
                    ins = pe.transpose(ps[:, j * P:(j + 1) * P], a_sb[:, h, j * P:(j + 1) * P], ident)
                filled(ins, f"aT{h}")

            def times_v(h):
                pe.wait_ge(*free(f"aT{h}"))
                hs = slice(h * P, (h + 1) * P)
                ins = pe.matmul(po[0][:, hs], aT[:, h % 2, 0:P], v[:, 0, hs], start=True, stop=True)
                if h == 3:
                    filled(ins, "o0")
                pe.matmul(po[1][:, hs], aT[:, h % 2, P:2 * P], v[:, 0, hs], start=True, stop=False)
                ins = pe.matmul(po[1][:, hs], aT[:, h % 2, 2 * P:384], v[:, 1, hs], start=False, stop=True)
                if h < 3:
                    ins.then_inc(s["pv"], 1)
                else:
                    filled(ins, "o1")

            transpose_a(0)
            transpose_a(1)
            proj("mv1", hsrc, next_dense(8))
            ps = take("rb")
            pe.wait_ge(wr_in, 64)
            pe.wait_ge(s["mod2"], 1)
            for k in range(KD):
                ins = pe.matmul(ps[:, 0:G + NE], S("B2", KD)[:, k:k + 1].to_broadcast([P, P]), w_r[:, k, :],
                                start=(k == 0), stop=(k == KD - 1))
            filled(ins, "rb")
            ada(2)
            po = [take("o0"), take("o1")]
            times_v(0)
            times_v(1)
            transpose_a(2)
            proj("mo0", hsrc, next_dense(8))
            transpose_a(3)
            times_v(2)
            proj("mo1", hsrc, next_dense(8))
            times_v(3)

            def mscores(h):
                ps = take(f"ms{h}")
                pe.wait_ge(s["mqk_r"], 4)
                pe.matmul(ps[:, 0:T], mqk[:, 4 + h, 0:P], mqk[:, h, :], start=True, stop=True)
                filled(pe.matmul(ps[:, T:384], mqk[:, 4 + h, P:T], mqk[:, h, P:T], start=True, stop=True), f"ms{h}")

            def numerator(h):
                ps = take(f"num{h}")
                pe.wait_ge(*free(f"ms{h}"))
                pe.wait_ge(*free("mv0"))
                pe.wait_ge(*free("mv1"))
                n = P + 1
                pe.matmul(ps[:, 0:n], wts[h][:, 0:P], vaug[:, 0, h, :], start=True, stop=True)
                pe.matmul(ps[:, n:2 * n], wts[h][:, P:T], vaug[:, 0, h, :], start=True, stop=False)
                filled(pe.matmul(ps[:, n:2 * n], wts[h][:, T:384], vaug[:, 1, h, :], start=False, stop=True),
                       f"num{h}")

            def gate_a(i):
                proj_T(f"ga{i}", hsrc, next_dense(8))

            gate_a(0)
            gate_a(1)
            ada_spread(2, 1, 0)
            ada_spread(2, 1, 1)
            mscores(0)
            mscores(1)
            gate_a(2)
            numerator(0)
            mscores(2)
            numerator(1)
            mscores(3)
            gate_a(3)
            numerator(2)
            numerator(3)
            for i in range(2):
                ps = take(f"yaT{i}")
                pe.wait_ge(*free("o0"))
                pe.wait_ge(*free("o1"))
                for j in range(2):
                    for tt in range(TT):
                        h = 2 * i + j
                        ins = pe.transpose(ps[:, j * T + tt * P:j * T + (tt + 1) * P], o[:, tt, h * P:(h + 1) * P], ident)
                filled(ins, f"yaT{i}")
            for i in range(4):
                proj_T(f"gm{i}", hsrc, next_dense(8))
            for i in range(2):
                ps = take(f"ymT{i}")
                pe.wait_ge(s["hn_r"], 2)
                for j in range(2):
                    for tt in range(TT):
                        h = 2 * i + j
                        ins = pe.transpose(ps[:, j * T + tt * P:j * T + (tt + 1) * P], osig[:, tt, h * P:(h + 1) * P],
                                           ident)
                filled(ins, f"ymT{i}")
            for name, y0 in (("a", 0), ("m", 4)):
                low = (s["y_lo"], 2 if name == "a" else 4)
                pe.wait_ge(*low)
                src = (lambda k: yT_hi[:, y0 + k, :], lambda k: yT_lo[:, y0 + k, :], (low,))
                for u in range(2):
                    w = next_dense(4)
                    for i in range(2):
                        proj_T(f"br{name}{2 * u + i}", src, w, 2 * i, 4)
            ada(5)
            pe.wait_ge(s["m_hi"], 4)
            merged_src = (lambda k: merged_hi[:, k, :], lambda k: merged_lo[:, k, :], ((s["m_lo"], 4),))

            def out_proj(i):
                proj(f"wo{i}", merged_src, next_dense(8))

            def turn_x(i):
                ps = take(f"x2T{i}")
                pe.wait_ge(s["x2"], i + 1)
                for j in range(2):
                    for tt in range(TT):
                        k = 2 * i + j
                        ins = pe.transpose(ps[:, j * T + tt * P:j * T + (tt + 1) * P], x[:, tt, k * P:(k + 1) * P], ident)
                filled(ins, f"x2T{i}")

            out_proj(0)
            out_proj(1)
            out_proj(2)
            turn_x(0)
            turn_x(1)
            out_proj(3)
            turn_x(2)
            pe.wait_ge(s["wr_r"], KD)
            pl = take("lgT")

            def logits(ks):
                for k in ks:
                    ins = pe.matmul(pl[0:G + NE, 0:T], w_r[:, k, :], hT[:, k, :], start=(k == 0), stop=(k == KD - 1))
                return ins

            for i in range(3):
                pe.wait_ge(*free(f"x2T{i}"))
                logits((2 * i, 2 * i + 1))
            turn_x(3)
            pe.wait_ge(*free("x2T3"))
            filled(logits((6, 7)), "lgT")
            ps = take("lg")
            pe.wait_ge(*free("lgT"))
            for tt in range(TT):
                ins = pe.transpose(ps[:, tt * 36:(tt + 1) * 36], lgT[0:G + NE, tt * P:(tt + 1) * P],
                                   ident[0:G + NE, 0:G + NE])
            filled(ins, "lg")
            ada_spread(5, 2, 0)
            ada_spread(5, 2, 1)
            ps = take("rank")
            pe.wait_ge(s["mask_r"], 1)
            m = R("mask", TT, NE)
            tri = K("tri")
            pe.matmul(ps[:, 0:NE], tri, m[:, 0, :], start=True, stop=True)
            pe.matmul(ps[:, NE:2 * NE], ones, m[:, 0, :], start=True, stop=False)
            pe.matmul(ps[:, NE:2 * NE], tri, m[:, 1, :], start=False, stop=True)
            pe.matmul(ps[0:1, 2 * NE:3 * NE], ones[:, 0:1], m[:, 0, :], start=True, stop=False)
            filled(pe.matmul(ps[0:1, 2 * NE:3 * NE], ones[:, 0:1], m[:, 1, :], start=False, stop=True), "rank")

            def scatter(b, stop):
                for tt in range(TT):
                    for c in range(2):
                        ins = pe.matmul(y_banks[2 * tt + c][:], ptg[:, b, tt, :], outs2[:, 512 * c:512 * c + 512],
                                        start=False, stop=stop, skip_group_check=True)
                    if stop:
                        ins.then_inc(s["y_full"], 1)
                return ins

            def gather(half):
                for j in range(4):
                    k = 4 * half + j
                    for tt in range(TT):
                        ins = pe.matmul(token_bank[:, j * P:(j + 1) * P], xn[:, tt, k * P:(k + 1) * P],
                                        pone[:, tt].rearrange("p a n -> p (a n)"), start=(tt == 0), stop=(tt == TT - 1))
                ins.then_inc(s["g_full"], 1)

            def turn(with_hidden):
                for tt in range(TT):
                    ins = pe.transpose(token_bank[:, tt * P:(tt + 1) * P], pgate[:, tt].rearrange("p a n -> p (a n)"), ident)
                if with_hidden:
                    for f in range(2):
                        ins = pe.transpose(token_bank[:, T + f * P:T + (f + 1) * P], hid[:, f * P:(f + 1) * P], ident)
                ins.then_inc(s["pt_full"], 1)

            def arrived(w, e, r, j):
                m = j * QU + QUAD_POS[(w, e)]
                n = NPRE + m % XSLOTS
                pe.wait_ge(landed[slot_of(n)], r * (16 * TURNS) + (landed_value(n) + 16 * (m // XSLOTS)))
                return unit(n, 2 if w == "w2" else 8)

            def up(w, r, j, b):
                half = slice(0, F) if w == "w1" else slice(F, 2 * F)
                wt = [arrived(w, e, r, j) for e in range(QUAD)]
                for k in range(KD):
                    for e in range(QUAD):
                        ins = pe.matmul(up_bank[e * CAP:(e + 1) * CAP, half], xg[:, b, k, e * CAP:(e + 1) * CAP],
                                        wt[e][:, k, :], start=(k == 0), stop=(k == KD - 1), tile_position=(0, e * CAP))
                        if k == KD - 1:
                            ins.then_inc(used, 1)

            def down(r, j):
                for pair in ((0, 1), (2, 3)):
                    wt = {e: arrived("w2", e, r, j) for e in pair}
                    for c in range(2):
                        for f in range(2):
                            for e in pair:
                                ins = pe.matmul(out_banks[c][e * CAP:(e + 1) * CAP, :], hidT[:, f, e * CAP:(e + 1) * CAP],
                                                wt[e][:, f, 512 * c:512 * c + 512], start=(f == 0), stop=(f == 1),
                                                tile_position=(0, e * CAP))
                                if c == 1 and f == 1:
                                    ins.then_inc(used, 1)

            def quad(r, j):
                it, b = r * LOOP + j, j % 2
                pe.wait_ge(s["g_evac"], it * 2 + 2)
                pe.wait_ge(s["hid_done"], it + 1)
                up("w1", r, j, b)
                pe.wait_ge(s["pg_ready"], it + 2)
                pe.wait_ge(s["pt_evac"], it + 2)
                gather(0)
                pe.wait_ge(s["o_dve"], it + 1)
                scatter(1 - b, False).then_inc(s["scat"], 1)
                pe.wait_ge(s["g_evac"], it * 2 + 3)
                gather(1)
                up("w3", r, j, b)
                pe.wait_ge(s["g_evac"], it * 2 + 4)
                pe.wait_ge(s["hid_done"], it + 2)
                turn(True)
                pe.wait_ge(s["hT_evac"], it + 1)
                down(r, j)

            pe.wait_ge(s["moe_chain"], 1)
            pe.wait_ge(s["x2n"], 2)
            gather(0)
            for job in ("wo3", "x2T2", "lgT", "x2T3"):
                pe.wait_ge(*free(job))

            def start_y(tt):
                for c in range(2):
                    pe.matmul(y_banks[2 * tt + c][:], ident, x[:, tt, 512 * c:512 * c + 512], start=True, stop=False,
                              skip_group_check=True)

            start_y(0)
            pe.wait_ge(s["g_evac"], 1)
            gather(1)
            start_y(1)
            pe.wait_ge(s["g_evac"], 2)
            pe.wait_ge(s["pg_ready"], 1)
            turn(False)
            for job in ("rank", "gt2b0", "gt2b1"):
                pe.wait_ge(*free(job))
            with pe.Fori(0, NQ // LOOP) as r:
                for j in range(LOOP):
                    quad(r, j)
            pe.wait_ge(s["flag_r"], 1)
            over = pe.value_load(flag[0:1, 0:1], min_val=0, max_val=1)
            with pe.If(over > 0):
                with pe.Fori(1, PASSES) as p:
                    with pe.Fori(0, NQ // LOOP) as r:
                        for j in range(LOOP):
                            quad(p * (NQ // LOOP) + r, j)
            pe.wait_ge(s["act_end"], 1)
            pe.wait_ge(s["dve_end"], 1)
            scatter(1, True)


_INS = ['x', 'c', 'w_ada', 'b_ada', 'norm1', 'w_in', 'b_if', 'conv_w', 'conv_b', 'lam_q1', 'lam_k1', 'lam_q2',
        'lam_k2', 'diff_norm', 'mlstm_norm', 'w_br_a', 'w_br_m', 'w_out', 'norm2', 'w_rg', 'b_rg', 'w_re', 'b_re',
        'w_e1', 'w_e3', 'w_e2', 'norm_f']


def kernel(**inputs):
    import concourse.bacc as bacc
    from concourse.bass_utils import run_bass_kernel_spmd

    nc = bacc.Bacc("TRN2", target_bir_lowering=False, num_devices=1)
    arrays, aps = {}, {}
    for name in _INS:
        a = np.ascontiguousarray(inputs[name])
        arrays[f"in_{name}"] = a
        aps[name] = nc.dram_tensor(f"in_{name}", a.shape, mybir.dt.from_np(a.dtype), kind="ExternalInput").ap()
    arrays["in_const"] = constants()
    aps["const"] = nc.dram_tensor("in_const", (P, NCONST), F32, kind="ExternalInput").ap()
    out = nc.dram_tensor("out_0", (1, T, D), F32, kind="ExternalOutput").ap()
    build(nc, aps, out)
    result = run_bass_kernel_spmd(nc, [arrays], core_ids=[0])
    return result.results[0]["out_0"]
```
